# Optimizing a Trainium2 kernel written in Bass

```python
import jax, jax.numpy as jnp
from jax import lax
import numpy as np

D_MODEL = 2048
BATCH = 1
SEQ = 512
DEPTH = 1

MLSTM_HEADS = 4
MLSTM_HEAD_DIM = 256
D_MLSTM = MLSTM_HEADS * MLSTM_HEAD_DIM
CHUNK = 128
FOURIER_GROUPS = 4
FOURIER_GROUP_DIM = 256
D_FOURIER = FOURIER_GROUPS * FOURIER_GROUP_DIM
N_BRANCHES = 2
N_EXPERTS = 16
CAPACITY_FACTOR = 2
D_EXPERT = 1024
EPS = 1e-6
N_GATE_COLS = 4 * MLSTM_HEADS
N_IN = 4 * D_MLSTM + D_FOURIER + N_GATE_COLS + N_BRANCHES * D_MODEL

kernel_name = "hybrid_mlstm_fnet_ec_moe_encoder"

def rms_norm(x, g):
    xf = x.astype(jnp.float32)
    y = xf * lax.rsqrt(jnp.mean(xf * xf, axis=-1, keepdims=True) + EPS)
    return (y * g.astype(jnp.float32)).astype(x.dtype)

def _mlstm_scan(q, k, v, log_i, log_f):
    bsz, seq, nh, dh = q.shape
    nc = seq // CHUNK

    def chunks(a):
        a = a.reshape((bsz, nc, CHUNK) + a.shape[2:])
        return jnp.moveaxis(a, (1, 3), (0, 2))

    tril = jnp.tril(jnp.ones((CHUNK, CHUNK), dtype=bool))

    def step(carry, inp):
        c_st, n_st, m_st = carry
        qc, kc, vc, lic, lfc = inp
        b = jnp.cumsum(lfc, axis=-1)
        dmat = b[..., :, None] - b[..., None, :] + lic[..., None, :]
        dmat = jnp.where(tril, dmat, -jnp.inf)
        inter = b + m_st[..., None]
        m_j = jnp.maximum(inter, jnp.max(dmat, axis=-1))
        w = jnp.exp(dmat - m_j[..., None])
        s = jnp.einsum('bhjd,bhsd->bhjs', qc, kc) * w
        sc_inter = jnp.exp(inter - m_j)
        num = jnp.einsum('bhjs,bhse->bhje', s, vc) + sc_inter[..., None] * jnp.einsum('bhed,bhjd->bhje', c_st, qc)
        den = jnp.sum(s, axis=-1) + sc_inter * jnp.einsum('bhd,bhjd->bhj', n_st, qc)
        h = num / jnp.maximum(jnp.abs(den), jnp.exp(-m_j))[..., None]
        b_last = b[..., -1]
        g = b_last[..., None] - b + lic
        m_new = jnp.maximum(b_last + m_st, jnp.max(g, axis=-1))
        wk = jnp.exp(g - m_new[..., None])
        decay = jnp.exp(b_last + m_st - m_new)
        c_new = decay[..., None, None] * c_st + jnp.einsum('bhs,bhse,bhsd->bhed', wk, vc, kc)
        n_new = decay[..., None] * n_st + jnp.einsum('bhs,bhsd->bhd', wk, kc)
        return (c_new, n_new, m_new), h

    init = (jnp.zeros((bsz, nh, dh, dh), jnp.float32),
            jnp.zeros((bsz, nh, dh), jnp.float32),
            jnp.zeros((bsz, nh), jnp.float32))
    _, hs = lax.scan(step, init, (chunks(q), chunks(k), chunks(v), chunks(log_i), chunks(log_f)))
    hs = jnp.moveaxis(hs, (0, 2), (1, 3))
    return hs.reshape(bsz, seq, nh, dh)

def _mixer_block(h, w_in, b_if, mh_g, w_a, w_b, w_out):
    bsz, seq, _ = h.shape
    proj = jnp.einsum('bsd,dn->bsn', h, w_in)
    offs = np.cumsum([D_MLSTM, D_MLSTM, D_MLSTM, D_MLSTM, D_FOURIER, N_GATE_COLS])
    q, k, v, o_pre, u, if_pre, gate_pre = jnp.split(proj, offs, axis=-1)

    shp = (bsz, seq, MLSTM_HEADS, MLSTM_HEAD_DIM)
    qf = q.astype(jnp.float32).reshape(shp) * (MLSTM_HEAD_DIM ** -0.5)
    kf = k.astype(jnp.float32).reshape(shp)
    vf = v.astype(jnp.float32).reshape(shp)
    gates = if_pre.astype(jnp.float32).reshape(bsz, seq, 4, MLSTM_HEADS) + b_if.astype(jnp.float32)
    li_f, lf_f = gates[:, :, 0], jax.nn.log_sigmoid(gates[:, :, 1])
    li_b, lf_b = gates[:, :, 2], jax.nn.log_sigmoid(gates[:, :, 3])
    h_fwd = _mlstm_scan(qf, kf, vf, li_f, lf_f)
    flip = lambda a: jnp.flip(a, axis=1)
    h_bwd = flip(_mlstm_scan(flip(qf), flip(kf), flip(vf), flip(li_b), flip(lf_b)))
    hm = h_fwd + h_bwd
    hm = hm * lax.rsqrt(jnp.mean(hm * hm, axis=-1, keepdims=True) + EPS)
    hm = hm.reshape(bsz, seq, D_MLSTM) * mh_g.astype(jnp.float32)
    hm = (jax.nn.sigmoid(o_pre.astype(jnp.float32)) * hm).astype(h.dtype)
    y_a = jnp.einsum('bsc,cd->bsd', hm, w_a)

    ug = u.astype(jnp.float32).reshape(bsz, seq, FOURIER_GROUPS, FOURIER_GROUP_DIM)
    uf = jnp.fft.fft2(ug, axes=(1, 3), norm='ortho').real.astype(h.dtype)
    y_b = jnp.einsum('bsc,cd->bsd', uf.reshape(bsz, seq, D_FOURIER), w_b)

    g_a, g_b = jnp.split(jax.nn.sigmoid(gate_pre.astype(jnp.float32)), N_BRANCHES, axis=-1)
    merged = (g_a * y_a.astype(jnp.float32) + g_b * y_b.astype(jnp.float32)).astype(h.dtype)
    return jnp.einsum('bsd,de->bse', merged, w_out)

def _expert_choice_ffn(h, w_router, w1, w3, w2):
    bsz, seq, d = h.shape
    cap = CAPACITY_FACTOR * seq // N_EXPERTS
    logits = jnp.einsum('bsd,de->bse', h, w_router).astype(jnp.float32)
    aff = jax.nn.softmax(logits, axis=-1)
    gate, idx = lax.top_k(jnp.swapaxes(aff, 1, 2), cap)
    xg = jax.vmap(lambda hb, ib: hb[ib])(h, idx)
    a = jnp.einsum('becd,edf->becf', xg, w1)
    b = jnp.einsum('becd,edf->becf', xg, w3)
    y = jnp.einsum('becf,efd->becd', jax.nn.silu(a) * b, w2)
    y = y * gate[..., None].astype(y.dtype)
    out = jax.vmap(lambda ib, yb: jnp.zeros((seq, d), yb.dtype).at[ib.reshape(-1)].add(yb.reshape(-1, d)))(idx, y)
    return out

def setup_inputs(seed: int = 0) -> dict:
    key = jax.random.key(seed)
    ks = jax.random.split(key, 16)
    f32 = jnp.float32
    nrm = lambda k, shape, fan_in: jax.random.normal(k, shape, f32) * (fan_in ** -0.5)
    x = jax.random.normal(ks[0], (BATCH, SEQ, D_MODEL), f32)
    norm1_g = 1.0 + 0.02 * jax.random.normal(ks[1], (DEPTH, D_MODEL), f32)
    w_in = nrm(ks[2], (DEPTH, D_MODEL, N_IN), D_MODEL)
    b_i = 0.1 * jax.random.normal(ks[3], (DEPTH, 2, MLSTM_HEADS), f32)
    b_f = 3.0 + 3.0 * jax.random.uniform(ks[4], (DEPTH, 2, MLSTM_HEADS), f32)
    b_if = jnp.stack([b_i[:, 0], b_f[:, 0], b_i[:, 1], b_f[:, 1]], axis=1)
    mh_g = 1.0 + 0.02 * jax.random.normal(ks[5], (DEPTH, D_MLSTM), f32)
    w_a = nrm(ks[6], (DEPTH, D_MLSTM, D_MODEL), D_MLSTM)
    w_b = nrm(ks[7], (DEPTH, D_FOURIER, D_MODEL), D_FOURIER)
    w_out = nrm(ks[8], (DEPTH, D_MODEL, D_MODEL), D_MODEL)
    norm2_g = 1.0 + 0.02 * jax.random.normal(ks[9], (DEPTH, D_MODEL), f32)
    w_router = nrm(ks[10], (DEPTH, D_MODEL, N_EXPERTS), D_MODEL)
    w1 = nrm(ks[11], (DEPTH, N_EXPERTS, D_MODEL, D_EXPERT), D_MODEL)
    w3 = nrm(ks[12], (DEPTH, N_EXPERTS, D_MODEL, D_EXPERT), D_MODEL)
    w2 = nrm(ks[13], (DEPTH, N_EXPERTS, D_EXPERT, D_MODEL), D_EXPERT)
    final_g = 1.0 + 0.02 * jax.random.normal(ks[14], (D_MODEL,), f32)
    return {"x": x, "norm1_g": norm1_g, "w_in": w_in, "b_if": b_if, "mh_g": mh_g,
            "w_a": w_a, "w_b": w_b, "w_out": w_out, "norm2_g": norm2_g,
            "w_router": w_router, "w1": w1, "w3": w3, "w2": w2, "final_g": final_g}

def reference(x, norm1_g, w_in, b_if, mh_g, w_a, w_b, w_out, norm2_g, w_router, w1, w3, w2, final_g):
    for l in range(DEPTH):
        h = rms_norm(x, norm1_g[l])
        x = x + _mixer_block(h, w_in[l], b_if[l], mh_g[l], w_a[l], w_b[l], w_out[l])
        h2 = rms_norm(x, norm2_g[l])
        x = x + _expert_choice_ffn(h2, w_router[l], w1[l], w3[l], w2[l])
    return rms_norm(x, final_g)


_drawn_inputs = setup_inputs


def setup_inputs(seed=0):
    import zlib

    import numpy as np

    out = dict(_drawn_inputs(seed))
    spreads = {}
    factors = {'mh_g': 7.095, 'norm2_g': 4.323, 'final_g': 2.786}
    for name, (base, spread) in spreads.items():
        noise = np.random.default_rng([zlib.crc32(name.encode()), seed]).standard_normal(out[name].shape)
        drawn = base * np.exp(spread * noise) if base else spread * noise
        out[name] = __import__('jax').numpy.asarray(drawn.astype(out[name].dtype))
    for name, factor in factors.items():
        out[name] = (out[name] * factor).astype(out[name].dtype)
    return out
```

```python
from contextlib import ExitStack

import numpy as np
import concourse.bass as bass
from concourse import mybir

ACT = mybir.ActivationFunctionType
ALU = mybir.AluOpType
F32 = mybir.dt.float32
F32R = mybir.dt.float32r
AXX = mybir.AxisListType.X
ds = bass.ds

P = 128
SEQ, D = 512, 2048
NT, KD = SEQ // P, D // P
H, DH = 4, 256
DM = H * DH
KM = DM // P
N_GATE = 4 * H
E, CAP, FE = 16, 64, 1024
KF = FE // P
EPS = 1e-6
NB = 512
COL_Q, COL_K, COL_V, COL_O, COL_U = (DM * i for i in range(5))
COL_IF = 5 * DM
COL_GA = COL_IF + N_GATE
COL_GB = COL_GA + D
MASKED = -1e30

C_ID, C_IOTA, C_PAIR, C_SELI, C_SELF, C_MASK, C_SELROW = 0, 128, 256, 320, 384, 448, 1472
C_END = C_SELROW + 8 * P


def shape_constants():
    c = np.zeros((P, C_END), np.float32)
    p = np.arange(P)
    c[p, C_ID + p] = 1.0
    c[:, C_IOTA:C_IOTA + P] = np.arange(P) % CAP
    c[p, C_PAIR + p % CAP] = 1.0
    for h in range(H):
        for direction in range(2):
            c[2 * direction * H + h, C_SELI + 32 * direction + h] = 1.0
            c[(2 * direction + 1) * H + h, C_SELF + 32 * direction + h] = 1.0
            at = C_SELROW + (2 * h + direction) * P
            c[32 * direction + h, at:at + P] = 1.0
    later = np.where(p[None, :] >= p[:, None], 0.0, MASKED)
    c[:, C_MASK:C_MASK + NB] = np.tile(later, (1, NT))
    c[:, C_MASK + NB:C_MASK + 2 * NB] = np.tile(later.T, (1, NT))
    a = 2 * np.pi * (np.outer(np.arange(DH), np.arange(DH)) % DH) / DH
    channel = np.concatenate([np.cos(a), -np.sin(a)], 1) / np.sqrt(DH)
    a = 2 * np.pi * (np.outer(np.arange(SEQ), np.arange(SEQ)) % SEQ) / SEQ
    token = np.concatenate([np.cos(a), np.sin(a)], 1) / np.sqrt(SEQ)
    return c, channel.astype(np.float32), token.astype(np.float32)


def build(nc, x, norm1_g, w_in, b_if, mh_g, w_a, w_b, w_out, norm2_g, w_router, w1, w3, w2, final_g,
          consts, dft_channel, dft_token, out):
    ctx = ExitStack()
    ctx.enter_context(nc.allow_non_contiguous_dma(reason="small per-channel vectors"))
    KB = 1024
    BASE = 16512

    def sb(name, kb, shape, dt=F32):
        return nc.alloc_sbuf_tensor_at(name, shape, dt, offset=BASE + int(kb * KB))

    def sem(name):
        return ctx.enter_context(nc.semaphore(name))

    cst = sb("cst", 0, [P, C_END])
    wif = sb("wif", 9.75, [P, KD, N_GATE])
    small = sb("small", 10.75, [P, 320])
    raw = sb("raw", 12, [P, 4, 2, NB])
    hi = sb("hi", 28, [P, 2, 2, NB], F32R)
    lo = sb("lo", 36, [P, 2, 2, NB], F32R)
    xh = sb("xh", 44, [P, KD, NB], F32R)
    xl = sb("xl", 76, [P, KD, NB], F32R)
    uh = sb("uh", 108, [P, 4, NB], F32R)
    ul = sb("ul", 116, [P, 4, NB], F32R)
    dft_raw = sb("dft_raw", 124, [P, 2, NB])
    dft_hi = sb("dft_hi", 128, [P, 2, NB], F32R)
    dft_lo = sb("dft_lo", 132, [P, 2, NB], F32R)
    junk = sb("junk", 108, [P, D])
    xin = sb("xin", 140, [P, NT, D])
    vh = sb("vh", 140, [P, NT, 2, NB], F32R)
    vl = sb("vl", 156, [P, NT, 2, NB], F32R)
    uf = sb("uf", 172, [P, KM, NB])
    q_t = sb("q_t", 108, [P, 4, NB])
    k_t = sb("k_t", 116, [P, 4, NB])
    o_t = sb("o_t", 124, [P, 4, NB])
    v_aug = sb("v_aug", 132, [P, NT, 2, DH + 1])
    prob = sb("prob", 140.5, [P, 2, 10, P])
    hcomb = sb("hcomb", 150.5, [P, NT, DH])
    wgt = sb("wgt", 154.5, [P, 2, 2, NB])
    neg_m = sb("neg_m", 162.5, [64, NB])
    diag = sb("diag", 164.5, [P, 2, NB])
    a_col = sb("a_col", 168.5, [P, NT, 64])
    em_col = sb("em_col", 169.5, [P, NT, 64])
    sel_pair = sb("sel_pair", 204, [64, 4, P])
    r_g16 = sb("r_g16", 140.5, [N_GATE, NB])
    r_ones = sb("r_ones", 142.5, [64, NB])
    r_1 = sb("r_1", 144.5, [64, NB])
    r_2 = sb("r_2", 146.5, [64, NB])
    r_b = sb("r_b", 148.5, [64, NB])
    r_m = sb("r_m", 150.5, [64, NB])
    r_a = sb("r_a", 152.5, [64, NB])
    hm = sb("hm", 188, [P, KM, NB])
    merged = sb("merged", 108, [P, KD, NB])
    bh = sb("bh", 140, [P, KM, NB], F32R)
    bl = sb("bl", 156, [P, KM, NB], F32R)
    sig = sb("sig", 172, [P, 4, NB])
    x2 = sb("x2", 140, [P, NT, D])
    h2t = sb("h2t", 44, [P, KD, NB])
    gain = sb("gain", 76, [P, D])
    h2 = sb("h2", 108, [P, NT, D])
    wr = sb("wr", 84, [P, KD, E])
    logit = sb("logit", 85, [P, NT, E])
    aff_t = sb("aff_t", 86, [E, NB])
    work = sb("work", 88, [E, NB])
    picked = sb("picked", 90, [E, NB])
    place = sb("place", 92, [E, NB])
    e_ones = sb("e_ones", 94, [E, NB])
    top8 = sb("top8", 96, [E, 8])
    aff = sb("aff", 204, [P, NT, E + 1])
    slot = sb("slot", 204.5, [P, NT, E + 1])
    gate = sb("gate", 205, [P, 2])
    stat = sb("stat", 205.25, [P, 32])
    eraw = sb("eraw", 172, [P, 4, D])
    ehi = sb("ehi", 44, [P, 2, D], F32R)
    elo = sb("elo", 60, [P, 2, D], F32R)
    xg = sb("xg", 76, [P, KD, P], F32R)
    ab = sb("ab", 84, [P, 2, FE])
    act_s = sb("act_s", 92, [P, 2, NB])
    hx = sb("hx", 96, [P, KF, P], F32R)
    onehot = sb("onehot", 100, [P, NT, P])
    h_f = sb("h_f", 102, [P, NB])
    onehot_t = sb("onehot_t", 1.75, [P, 2, NB], F32R)
    yh = sb("yh", 12, [P, 2, D], F32R)
    yl = sb("yl", 28, [P, 2, D], F32R)
    fgain = sb("fgain", 44, [P, D])
    junk_g = sb("junk_g", 60, [P, D])

    ps = ctx.enter_context(nc.psum_tensor("ps", [P, 8, NB], F32))

    ident = cst[:, C_ID:C_ID + P]
    iota = cst[:, C_IOTA:C_IOTA + P]
    pair_sum = cst[:, C_PAIR:C_PAIR + CAP]
    g1_col = small[:, 0:16]
    mh_col = small[:, 16:24]
    bif_col = small[0:N_GATE, 24:25]
    ss1 = small[:, 28:32]
    rs1 = small[:, 32:36]
    neg_half = small[:, 36:40]
    den = small[:, 40:48]
    ssh = small[:, 48:52]
    rsh = small[:, 52:56]
    junk_h = sb("junk_h", 171, [P, DH])
    eps4 = small[:, 56:60]

    def row_chunk(w, k, col, g):
        width = (w.shape[1] - col) // NB * NB
        block = w[k * P:(k + 2) * P, col:col + width].rearrange("(k p) (g n) -> p g k n", p=P, n=NB)
        return block[:, ds(g, 1)].rearrange("p g k n -> p (g k) n")

    A_N, C_N, D_N, E_N = 12, 32, 12, 16
    A_IT, C_IT, D_IT, E_IT = 2, 2, 4, 2
    A0 = 0
    C0 = A0 + A_N * A_IT
    D0 = C0 + C_N * C_IT
    D2 = D0 + D_N * D_IT
    E0 = D2 + D_N * D_IT
    DENSE = E0 + E_N * E_IT

    consts_in = sem("consts_in")
    dft_in = sem("dft_in")
    x_in = [sem(f"x_in{t}") for t in range(NT)]
    raw_in = [sem(f"raw_in{s}") for s in range(4)]
    hi_ready, lo_ready, chunk_used = sem("hi_ready"), sem("lo_ready"), sem("chunk_used")
    neg_half_set = sem("neg_half_set")
    ss1_ready, rs1_mid, rs1_ready = sem("ss1_ready"), sem("rs1_mid"), sem("rs1_ready")
    x_scaled, xt_mm, xh_ready, xl_ready = sem("x_scaled"), sem("xt_mm"), sem("xh_ready"), sem("xl_ready")
    dft_hi_ready, dft_lo_ready = sem("dft_hi_ready"), sem("dft_lo_ready")
    uh_ready, ul_ready = sem("uh_ready"), sem("ul_ready")
    v_mm, vh_ready, vl_ready = sem("v_mm"), sem("vh_ready"), sem("vl_ready")
    uf_act, uf_dve = sem("uf_act"), sem("uf_dve")
    gates_mm, g16_ready, gsel_mm = sem("gates_mm"), sem("g16_ready"), sem("gsel_mm")
    rows_dve, rows_act, rows_t = sem("rows_dve"), sem("rows_act"), sem("rows_t")
    cols_ready = sem("cols_ready")
    kq_act, kq_dve, v_act, v_dve, o_exp, o_dve = (sem("kq_act"), sem("kq_dve"), sem("v_act"), sem("v_dve"),
                                                  sem("o_exp"), sem("o_dve"))
    sel_ready, ones_ready = sem("sel_ready"), sem("ones_ready")
    bc_mm, diag_ready, wgt_ready, sc_mm, p_ready = (sem("bc_mm"), sem("diag_ready"), sem("wgt_ready"),
                                                    sem("sc_mm"), sem("p_ready"))
    pv_mm, pv_out, c_chain = sem("pv_mm"), sem("pv_out"), sem("c_chain")
    ssh_ready, rsh_mid, rsh_ready, hn_ready, hn_t, hm_ready = (sem("ssh_ready"), sem("rsh_mid"), sem("rsh_ready"),
                                                               sem("hn_ready"), sem("hn_t"), sem("hm_ready"))
    bh_ready, bl_ready = sem("bh_ready"), sem("bl_ready")
    sig_exp, d_chain, merged_ready = sem("sig_exp"), sem("d_chain"), sem("merged_ready")
    mh_ready, ml_ready = sem("mh_ready"), sem("ml_ready")
    x2_in, x2_ready = sem("x2_in"), sem("x2_ready")
    gain_in, wr_in = sem("gain_in"), sem("wr_in")
    ss2_ready, rs2_mid, rs2_ready, h2_ready = sem("ss2_ready"), sem("rs2_mid"), sem("rs2_ready"), sem("h2_ready")
    h2t_mm, h2t_act, h2t_dve = sem("h2t_mm"), sem("h2t_act"), sem("h2t_dve")
    logit_mm, negmax_ready, expl_ready, aff_ready = (sem("logit_mm"), sem("negmax_ready"), sem("expl_ready"),
                                                     sem("aff_ready"))
    aff_t_mm, f_chain, slot_mm, slot_ready = sem("aff_t_mm"), sem("f_chain"), sem("slot_mm"), sem("slot_ready")
    eraw_in = [sem(f"eraw_in{s}") for s in range(4)]
    ehi_ready, elo_ready, echunk_used = sem("ehi_ready"), sem("elo_ready"), sem("echunk_used")
    y_zero = sem("y_zero")
    onehot_ready, gather_mm, xgh_ready, xgl_ready = (sem("onehot_ready"), sem("gather_mm"), sem("xgh_ready"),
                                                     sem("xgl_ready"))
    gate_g_mm, gate_ready, onehot_t_mm, onehot_t_ready = (sem("gate_g_mm"), sem("gate_ready"),
                                                          sem("onehot_t_mm"), sem("onehot_t_ready"))
    a_out, at_mm, a_exp, g_chain = sem("a_out"), sem("at_mm"), sem("a_exp"), sem("g_chain")
    b_act, b_dve, bt_mm, h_ready, hh_ready, hl_ready = (sem("b_act"), sem("b_dve"), sem("bt_mm"),
                                                              sem("h_ready"), sem("hh_ready"), sem("hl_ready"))
    yh_ready, yl_ready, sc_out_mm, acc_ready = (sem("yh_ready"), sem("yl_ready"),
                                                      sem("sc_out_mm"), sem("acc_ready"))
    fg_in, ss3_ready, rs3_mid, rs3_ready, fin_ready, out_written = (sem("fg_in"), sem("ss3_ready"), sem("rs3_mid"),
                                                                    sem("rs3_ready"), sem("fin_ready"),
                                                                    sem("out_written"))
    block = ctx.enter_context(nc.Block())

    CCH = 2 * 8

    @block.sync
    def _(sp):
        def load(n0, per, i, j, src, slots=1):
            n = n0 + j
            if n >= 4 and slots:
                sp.wait_ge(lo_ready, i * per + (n - 4 + slots))
            sp.dma_start(raw[:, n % 4], src).then_inc(raw_in[n % 4], 16)

        sp.dma_start(cst[:], consts).then_inc(consts_in, 16)
        for j in range(4):
            load(A0, 0, 0, j, row_chunk(w_in, 2 * j, COL_U, 0))
        for i in range(A_IT):
            for j in range(4 if i == 0 else 0, 8):
                load(A0 + i * A_N, 0, 0, j, row_chunk(w_in, 2 * j, COL_U, i))
            for t in range(NT):
                load(A0 + i * A_N, 0, 0, 8 + t,
                     dft_token[t * P:(t + 1) * P, :].rearrange("p (k n) -> p k n", k=2))
        with sp.Fori(1, C_IT + 1) as turn:
            i = turn - 1
            for g, col in enumerate((COL_K, COL_Q, COL_V, COL_O)):
                for j in range(8):
                    load(C0, C_N, i, 8 * g + j, row_chunk(w_in, 2 * j, col, i),
                         slots=2 if (g, j) == (0, 7) else 0 if (g, j) == (1, 0) else 1)
        for base, col, w in ((D0, COL_GB, w_b), (D2, COL_GA, w_a)):
            with sp.Fori(1, D_IT + 1) as turn:
                i = turn - 1
                for j in range(8):
                    load(base, D_N, i, j, row_chunk(w_in, 2 * j, col, i), slots=2 if j == 7 else 1)
                for j in range(4):
                    load(base, D_N, i, 8 + j, row_chunk(w, 2 * j, 0, i), slots=0 if j == 0 else 1)
        with sp.Fori(1, E_IT + 1) as turn:
            i = turn - 1
            for g in range(2):
                for j in range(8):
                    load(E0, E_N, i, 8 * g + j, row_chunk(w_out, 2 * j, 0, i * 2 + g))
        G_N = 48

        def load_expert(i, j, head=False):
            e, c = j // 24, j % 24
            if not head:
                sp.wait_ge(elo_ready, i * G_N + (j - 3))
            if c < 16:
                w = w1 if c < 8 else w3
                k = 2 * (c % 8)
                src = w[ds(i * 2 + e, 1), k * P:(k + 2) * P, :].rearrange("e (k p) n -> p (e k) n", p=P)
                dst = eraw[:, j % 4].rearrange("p (k n) -> p k n", k=2)
            else:
                k = c - 16
                src = w2[ds(i * 2 + e, 1), k * P:(k + 1) * P, :].rearrange("e p n -> p (e n)")
                dst = eraw[:, j % 4]
            sp.dma_start(dst, src).then_inc(eraw_in[j % 4], 16)

        sp.wait_ge(merged_ready, 2 * D_IT)
        for j in range(4):
            load_expert(0, j, head=True)
        for j in range(4, G_N):
            load_expert(0, j)
        with sp.Fori(2, E // 2 + 1) as turn:
            i = turn - 1
            for j in range(G_N):
                load_expert(i, j)
        for t in range(NT):
            sp.wait_ge(fin_ready, t + 1)
            sp.dma_start(out[t * P:(t + 1) * P, :], x2[:, t]).then_inc(out_written, 16)
        sp.wait_ge(out_written, 16 * NT)

    @block.scalar
    def _(act):
        copy = ACT.Copy

        def split_hi(n0, per, i, j):
            n = n0 + j
            act.wait_ge(raw_in[n % 4], (i * per // 4 if isinstance(i, int) else i * (per // 4)) * 16
                        + 16 * (n // 4 + 1))
            if n >= 2:
                act.wait_ge(chunk_used, i * per + (n - 1))
            act.activation(hi[:, n % 2], raw[:, n % 4], copy).then_inc(hi_ready, 1)

        for t in range(NT):
            act.dma_start(xin[:, t], x[t * P:(t + 1) * P, :]).then_inc(x_in[t], 16)
        act.dma_start(g1_col, norm1_g.rearrange("o (k p) -> p (o k)", p=P)).then_inc(consts_in, 16)
        act.dma_start(mh_col, mh_g.rearrange("o (k p) -> p (o k)", p=P)).then_inc(consts_in, 16)
        act.dma_start(bif_col, b_if.rearrange("o a (h c) -> (o a h) c", c=1)).then_inc(consts_in, 16)
        act.dma_start(wif[:], w_in[:, COL_IF:COL_IF + N_GATE].rearrange("(k p) n -> p k n", p=P)).then_inc(consts_in, 16)
        act.dma_start(dft_raw[:], dft_channel.rearrange("(k p) n -> p k n", p=P)).then_inc(dft_in, 16)
        for t in range(NT):
            act.wait_ge(x_in[t], 16)
            if t:
                act.wait_ge(ss1_ready, t)
            act.activation(junk[:], xin[:, t], ACT.Square, accum_out=ss1[:, t:t + 1]).then_inc(ss1_ready, 1)
        split_hi(A0, 0, 0, 0)
        act.wait_ge(consts_in, 16 * 5)
        for k in range(KD):
            act.wait_ge(xt_mm, k + 1)
            act.activation(xh[:, k], ps[:, k % 8], copy, scale=g1_col[:, k:k + 1]).then_inc(xh_ready, 1)
        act.wait_ge(dft_in, 16)
        act.wait_ge(ss1_ready, NT)
        act.activation(dft_hi[:], dft_raw[:], copy).then_inc(dft_hi_ready, 1)
        for i in range(A_IT):
            for j in range(A_N):
                split_hi(A0 + i * A_N, 0, 0, j + 1)
                if j == 7:
                    act.wait_ge(chunk_used, A0 + i * A_N + 8)
                    for m in range(4):
                        act.activation(uh[:, m], ps[:, m], copy).then_inc(uh_ready, 1)
                    for b in range(8):
                        act.wait_ge(v_mm, 8 * i + b + 1)
                        act.activation(vh[:, b % 4, b // 4], ps[:, (4 + b) % 8], copy).then_inc(vh_ready, 1)
                if j == 11:
                    act.wait_ge(chunk_used, A0 + (i + 1) * A_N)
                    for m in range(2):
                        act.activation(uf[:, 4 * i + m], ps[:, 4 + m], copy).then_inc(uf_act, 1)
        act.wait_ge(gates_mm, 1)
        act.activation(r_g16[:], ps[0:N_GATE, 0], ACT.Identity, bias=bif_col).then_inc(g16_ready, 1)
        act.wait_ge(gsel_mm, 1)
        act.activation(r_1[:], ps[0:64, 2], ACT.Abs).then_inc(rows_act, 1)
        act.wait_ge(rows_act, 1)
        act.activation(r_2[:], r_1[:], ACT.Exp, scale=-1.0).then_inc(rows_act, 1)
        act.wait_ge(rows_act, 2)
        act.activation(r_1[:], r_2[:], ACT.Ln, bias=1.0).then_inc(rows_act, 1)
        act.wait_ge(rows_t, 1)
        act.activation(a_col[:], ps[:, 3, 0:256].rearrange("p (t c) -> p t c", t=NT), copy).then_inc(cols_ready, 1)
        act.activation(em_col[:], ps[:, 3, 256:512].rearrange("p (t c) -> p t c", t=NT), ACT.Exp,
                       scale=-1.0).then_inc(cols_ready, 1)
        with act.Fori(0, C_IT) as i:
            for j in range(C_N):
                split_hi(C0, C_N, i, j + 1)
                if j == 7:
                    act.wait_ge(chunk_used, i * C_N + (C0 + 8))
                    for m in range(2):
                        act.activation(k_t[:, m], ps[:, m], copy).then_inc(kq_act, 1)
                if j == 15:
                    act.wait_ge(chunk_used, i * C_N + (C0 + 16))
                    for m in range(2):
                        act.activation(q_t[:, m], ps[:, 4 + m], copy).then_inc(kq_act, 1)
                if j == 23:
                    act.wait_ge(chunk_used, i * C_N + (C0 + 24))
                    for t in range(2):
                        act.activation(v_aug[:, t, :, 0:DH], ps[:, t].rearrange("p (h d) -> p h d", h=2),
                                       copy).then_inc(v_act, 1)
                if j == 31:
                    act.wait_ge(chunk_used, i * C_N + (C0 + 32))
                    for m in range(4):
                        act.activation(o_t[:, m], ps[:, 4 + m], ACT.Exp, scale=-1.0).then_inc(o_exp, 1)
                    for hh in range(2):
                        act.wait_ge(diag_ready, i * 4 + 2 * hh + 2)
                        for s in range(NT):
                            if s >= 2:
                                act.wait_ge(p_ready, i * 16 + 8 * hh + 2 * s - 2)
                            elif hh:
                                act.wait_ge(p_ready, i * 16 + 8)
                            for d in range(2):
                                bias = a_col[:, s, ds(i * 2 + (hh + 32 * d), 1)]
                                act.activation(wgt[:, d, s % 2, s * P:(s + 1) * P], diag[:, d, s * P:(s + 1) * P],
                                               ACT.Exp, bias=bias).then_inc(wgt_ready, 1)
                                rest = slice((s + 1) * P, NB) if d == 0 else slice(0, s * P)
                                if rest.stop > rest.start:
                                    act.activation(wgt[:, d, s % 2, rest], ps[:, d, rest],
                                                   ACT.Exp, bias=bias).then_inc(wgt_ready, 1)
                        for t in range(NT):
                            act.wait_ge(pv_out, i * 8 + 4 * hh + t + 1)
                            if t or hh:
                                act.wait_ge(ssh_ready, i * 8 + 4 * hh + t)
                            act.activation(junk_h[:], hcomb[:, t], ACT.Square, scale=DH ** -0.5,
                                           accum_out=ssh[:, t:t + 1]).then_inc(ssh_ready, 1)
        for half, base in ((0, D0), (1, D2)):
            src = hm if half else uf
            if half:
                act.wait_ge(chunk_used, D2)
            else:
                act.wait_ge(hm_ready, 4 * C_IT)
                act.wait_ge(hn_t, 2 * C_IT)
            for k in range(KM):
                act.activation(bh[:, k], src[:, k], copy).then_inc(bh_ready, 1)
            if not half:
                act.wait_ge(bl_ready, KM)
            with act.Fori(0, D_IT) as i:
                for j in range(D_N):
                    split_hi(base, D_N, i, j + 1)
                    if j == 7:
                        act.wait_ge(chunk_used, i * D_N + (base + 8))
                        act.wait_ge(merged_ready, i + D_IT * half)
                        for m in range(4):
                            act.activation(sig[:, m], ps[:, m], ACT.Exp, scale=-1.0).then_inc(sig_exp, 1)
        act.wait_ge(merged_ready, 2 * D_IT)
        for k in range(KD):
            act.activation(xh[:, k], merged[:, k], copy).then_inc(mh_ready, 1)
        act.wait_ge(chunk_used, E0)
        for t in range(NT):
            act.dma_start(x2[:, t], x[t * P:(t + 1) * P, :]).then_inc(x2_in, 16)
        act.dma_start(wif[:], w_router.rearrange("(k p) n -> p k n", p=P)).then_inc(wr_in, 16)
        with act.Fori(0, E_IT - 1) as i:
            for j in range(E_N):
                split_hi(E0, E_N, i, j + 1)
        for j in range(E_N - 1):
            split_hi(E0 + E_N * (E_IT - 1), 0, 0, j + 1)
        act.wait_ge(chunk_used, DENSE)
        act.dma_start(gain[:], norm2_g[0:1, :].partition_broadcast(P)).then_inc(gain_in, 16)
        for t in range(NT):
            act.wait_ge(x2_ready, 8 * E_IT)
            if t:
                act.wait_ge(ss2_ready, t)
            act.activation(h2t[:, 0:4].rearrange("p k n -> p (k n)"), x2[:, t], ACT.Square,
                           accum_out=stat[:, t:t + 1]).then_inc(ss2_ready, 1)
        for t in range(NT):
            for b in (0, 2):
                act.wait_ge(h2t_mm, 4 * t + b + 1)
                if t == 0 and b == 0:
                    act.wait_ge(ss2_ready, NT)
                act.activation(h2t[:, 4 * b:4 * b + 4, t * P:(t + 1) * P],
                               ps[:, (4 * t + b) % 4].rearrange("p (k n) -> p k n", k=4), copy).then_inc(h2t_act, 1)
        for t in range(NT):
            act.wait_ge(negmax_ready, 1)
            act.activation(logit[:, t], ps[:, 4, t * E:(t + 1) * E], ACT.Exp, bias=stat[:, 8 + t:9 + t],
                           accum_out=stat[:, 12 + t:13 + t]).then_inc(expl_ready, 1)

        G_N = 48

        def split_ehi(i, j, first=False):
            act.wait_ge(eraw_in[j % 4], i * (G_N // 4 * 16) + 16 * (j // 4 + 1))
            if not first:
                act.wait_ge(echunk_used, i * G_N + (j - 1))
            act.activation(ehi[:, j % 2], eraw[:, j % 4], copy).then_inc(ehi_ready, 1)

        def gathered_hi(g, c):
            act.wait_ge(gather_mm, 2 * g + (c + 1))
            act.activation(xg[:, 8 * c:8 * c + 8, 0:CAP], ps[:, c].rearrange("p (k n) -> p k n", k=8),
                           copy).then_inc(xgh_ready, 1)

        act.wait_ge(slot_ready, 1)
        gathered_hi(0, 0)
        gathered_hi(0, 1)
        split_ehi(0, 0, True)
        split_ehi(0, 1, True)

        def expert_iteration(i, last):
            for j in range(G_N):
                ee, c = j // 24, j % 24
                if j and not (last and j == G_N - 1):
                    split_ehi(i, j + 1)
                n = i * 2 + ee
                if c == 7:
                    act.wait_ge(echunk_used, n * 24 + 8)
                    for b in range(2):
                        act.activation(ab[:, 0, b * NB:(b + 1) * NB], ps[:, b], copy).then_inc(a_out, 1)
                if c == 9:
                    act.wait_ge(at_mm, n + 1)
                    act.activation(act_s[:, 0], ps[:, 0], ACT.Exp, scale=-1.0).then_inc(a_exp, 1)
                if c == 13:
                    act.wait_ge(onehot_t_mm, n + 1)
                    act.activation(onehot_t[:, ee], ps[:, 1], copy).then_inc(onehot_t_ready, 1)
                if c == 15:
                    act.wait_ge(echunk_used, n * 24 + 16)
                    act.activation(ab[:, 1, 0:NB], ps[:, 2], copy).then_inc(b_act, 1)
                    act.wait_ge(h_ready, n + 1)
                    act.activation(hx[:, :, 0:CAP], h_f[:].rearrange("p (k n) -> p k n", k=KF),
                                   copy).then_inc(hh_ready, 1)
                if c == 18:
                    gathered_hi(n + 1, 0)
                if c == 20:
                    gathered_hi(n + 1, 1)
                if c == 23:
                    act.wait_ge(echunk_used, n * 24 + 24)
                    for b in range(4):
                        act.activation(yh[:, ee, b * NB:(b + 1) * NB], ps[:, 4 + b], copy,
                                       scale=gate[:, ee:ee + 1]).then_inc(yh_ready, 1)

        with act.Fori(0, E // 2 - 1) as i:
            act.wait_ge(y_zero, 2)
            expert_iteration(i, False)
            split_ehi(i + 1, 1)
        expert_iteration(E // 2 - 1, True)
        act.wait_ge(echunk_used, E * 24)
        act.dma_start(fgain[:], final_g.rearrange("(o n) -> o n", o=1).partition_broadcast(P)).then_inc(fg_in, 16)
        for t in range(NT):
            act.wait_ge(acc_ready, 16 * (E // 2 + 1))
            if t:
                act.wait_ge(ss3_ready, t)
            act.activation(junk_g[:], x2[:, t], ACT.Square, accum_out=stat[:, t:t + 1]).then_inc(ss3_ready, 1)

    @block.gpsimd
    def _(pool):
        pool.memset(neg_half, -0.5).then_inc(neg_half_set, 1)
        pool.memset(eps4, EPS).then_inc(neg_half_set, 1)
        for t in range(NT):
            pool.wait_ge(ss1_ready, t + 1)
            if t == 0:
                pool.wait_ge(neg_half_set, 2)
            pool.tensor_scalar(rs1[:, t:t + 1], ss1[:, t:t + 1], 1.0 / D, EPS, ALU.mult, ALU.add).then_inc(rs1_mid, 1)
            pool.wait_ge(rs1_mid, t + 1)
            pool.tensor_tensor(rs1[:, t:t + 1], rs1[:, t:t + 1], neg_half[:, 0:1], ALU.pow).then_inc(rs1_ready, 1)
        pool.wait_ge(dft_lo_ready, 1)
        pool.wait_ge(ul_ready, 4 * A_IT)
        pool.wait_ge(chunk_used, C0)
        pool.memset(v_aug[:, :, :, DH:DH + 1], 1.0).then_inc(ones_ready, 1)
        with pool.Fori(0, C_IT) as i:
            for hh in range(2):
                pool.wait_ge(ssh_ready, i * 8 + 4 * hh + 4)
                pool.tensor_tensor(rsh, ssh, eps4, ALU.add).then_inc(rsh_mid, 1)
                pool.wait_ge(rsh_mid, i * 2 + (hh + 1))
                pool.tensor_tensor(rsh, rsh, neg_half, ALU.pow).then_inc(rsh_ready, 1)
        for t in range(NT):
            pool.wait_ge(ss2_ready, t + 1)
            pool.tensor_scalar(stat[:, 4 + t:5 + t], stat[:, t:t + 1], 1.0 / D, EPS, ALU.mult,
                               ALU.add).then_inc(rs2_mid, 1)
            pool.wait_ge(rs2_mid, t + 1)
            pool.tensor_tensor(stat[:, 4 + t:5 + t], stat[:, 4 + t:5 + t], neg_half[:, 0:1],
                               ALU.pow).then_inc(rs2_ready, 1)

        for t in range(NT):
            pool.wait_ge(ss3_ready, t + 1)
            pool.tensor_scalar(stat[:, 4 + t:5 + t], stat[:, t:t + 1], 1.0 / D, EPS, ALU.mult,
                               ALU.add).then_inc(rs3_mid, 1)
            pool.wait_ge(rs3_mid, t + 1)
            pool.tensor_tensor(stat[:, 4 + t:5 + t], stat[:, 4 + t:5 + t], neg_half[:, 0:1],
                               ALU.pow).then_inc(rs3_ready, 1)

    @block.vector
    def _(dve):
        def split_lo(n0, per, i, j):
            n = n0 + j
            dve.wait_ge(hi_ready, i * per + (n + 1))
            dve.tensor_tensor(lo[:, n % 2], raw[:, n % 4], hi[:, n % 2].bitcast(F32),
                              ALU.subtract).then_inc(lo_ready, 1)

        for t in range(NT):
            dve.wait_ge(rs1_ready, t + 1)
            dve.tensor_scalar(xin[:, t], xin[:, t], rs1[:, t:t + 1], None, ALU.mult).then_inc(x_scaled, 1)
        split_lo(A0, 0, 0, 0)
        for k in range(KD):
            dve.wait_ge(xh_ready, k + 1)
            dve.scalar_tensor_tensor(xl[:, k], ps[:, k % 8], g1_col[:, k:k + 1], xh[:, k].bitcast(F32),
                                     ALU.mult, ALU.subtract).then_inc(xl_ready, 1)
        dve.wait_ge(dft_hi_ready, 1)
        dve.tensor_tensor(dft_lo[:], dft_raw[:], dft_hi[:].bitcast(F32), ALU.subtract).then_inc(dft_lo_ready, 1)
        for i in range(A_IT):
            for j in range(A_N):
                split_lo(A0 + i * A_N, 0, 0, j + 1)
                if j == 7:
                    for m in range(4):
                        dve.wait_ge(uh_ready, 4 * i + m + 1)
                        dve.tensor_tensor(ul[:, m], ps[:, m], uh[:, m].bitcast(F32),
                                          ALU.subtract).then_inc(ul_ready, 1)
                    for b in range(8):
                        dve.wait_ge(vh_ready, 8 * i + b + 1)
                        dve.tensor_tensor(vl[:, b % 4, b // 4], ps[:, (4 + b) % 8],
                                          vh[:, b % 4, b // 4].bitcast(F32), ALU.subtract).then_inc(vl_ready, 1)
                if j == 11:
                    dve.wait_ge(chunk_used, A0 + (i + 1) * A_N)
                    for m in range(2, 4):
                        dve.tensor_copy(uf[:, 4 * i + m], ps[:, 4 + m]).then_inc(uf_dve, 1)
        dve.memset(r_ones[:], 1.0).then_inc(rows_dve, 1)
        dve.memset(r_b[:], 0.0).then_inc(rows_dve, 1)
        dve.wait_ge(gsel_mm, 1)
        dve.wait_ge(rows_act, 3)
        dve.scalar_tensor_tensor(r_2[:], ps[0:64, 2], 0.0, r_1[:], ALU.min, ALU.subtract).then_inc(rows_dve, 1)
        dve.wait_ge(rows_dve, 3)
        dve.tensor_tensor_scan(r_b[0:4], r_ones[0:4], r_2[0:4], 0.0, ALU.mult, ALU.add).then_inc(rows_dve, 1)
        dve.tensor_tensor_scan(r_b[32:36, ::-1], r_ones[32:36, ::-1], r_2[32:36, ::-1], 0.0,
                               ALU.mult, ALU.add).then_inc(rows_dve, 1)
        dve.wait_ge(rows_dve, 5)
        dve.tensor_tensor(r_a[:], ps[0:64, 1], r_b[:], ALU.subtract).then_inc(rows_dve, 1)
        dve.memset(r_m[:], 0.0).then_inc(rows_dve, 1)
        dve.wait_ge(rows_dve, 7)
        dve.tensor_tensor_scan(r_m[0:4], r_ones[0:4], r_a[0:4], 0.0, ALU.mult, ALU.max).then_inc(rows_dve, 1)
        dve.tensor_tensor_scan(r_m[32:36, ::-1], r_ones[32:36, ::-1], r_a[32:36, ::-1], 0.0,
                               ALU.mult, ALU.max).then_inc(rows_dve, 1)
        dve.wait_ge(rows_dve, 9)
        dve.tensor_scalar(neg_m[:], r_m[:], -1.0, None, ALU.mult).then_inc(rows_dve, 1)
        dve.tensor_tensor(r_b[:], r_b[:], r_m[:], ALU.add).then_inc(rows_dve, 1)
        with dve.Fori(0, C_IT) as i:
            for j in range(C_N):
                split_lo(C0, C_N, i, j + 1)
                if j == 7:
                    dve.wait_ge(chunk_used, i * C_N + (C0 + 8))
                    for m in range(2, 4):
                        dve.tensor_copy(k_t[:, m], ps[:, m]).then_inc(kq_dve, 1)
                    dve.tensor_copy(sel_pair[:].rearrange("p a b -> p (a b)"),
                                    cst[0:64, ds(i * 4 * P + C_SELROW, 4 * P)]).then_inc(sel_ready, 1)
                if j == 15:
                    dve.wait_ge(chunk_used, i * C_N + (C0 + 16))
                    for m in range(2, 4):
                        dve.tensor_copy(q_t[:, m], ps[:, 4 + m]).then_inc(kq_dve, 1)
                if j == 23:
                    dve.wait_ge(chunk_used, i * C_N + (C0 + 24))
                    for t in range(2, 4):
                        dve.tensor_copy(v_aug[:, t, :, 0:DH],
                                        ps[:, t].rearrange("p (h d) -> p h d", h=2)).then_inc(v_dve, 1)
                if j == 31:
                    for m in range(4):
                        dve.wait_ge(o_exp, i * 4 + (m + 1))
                        dve.tensor_scalar(o_t[:, m], o_t[:, m], 1.0, None, ALU.add).then_inc(o_dve, 1)
                        dve.wait_ge(o_dve, i * 8 + (2 * m + 1))
                        dve.reciprocal(o_t[:, m], o_t[:, m]).then_inc(o_dve, 1)
                    for hh in range(2):
                        for d in range(2):
                            dve.wait_ge(bc_mm, i * 4 + (2 * hh + d + 1))
                            dve.tensor_tensor(diag[:, d], ps[:, d],
                                              cst[:, C_MASK + d * NB:C_MASK + (d + 1) * NB],
                                              ALU.add).then_inc(diag_ready, 1)
                        w_seen = 0
                        for s in range(NT):
                            w_seen += 4 - (s == NT - 1) - (s == 0)
                            dve.wait_ge(sc_mm, i * 8 + (4 * hh + s + 1))
                            dve.wait_ge(wgt_ready, i * 28 + (14 * hh + w_seen))
                            f0 = s * NT - s * (s - 1) // 2
                            dve.scalar_tensor_tensor(
                                prob[:, 0, f0:f0 + NT - s].rearrange("p a b -> p (a b)"),
                                ps[:, 2 + s % 2, s * P:NB], DH ** -0.5, wgt[:, 0, s % 2, s * P:NB],
                                ALU.mult, ALU.mult).then_inc(p_ready, 1)
                            b0 = s * (s + 1) // 2
                            dve.scalar_tensor_tensor(
                                prob[:, 1, b0:b0 + s + 1].rearrange("p a b -> p (a b)"),
                                ps[:, 2 + s % 2, 0:(s + 1) * P], DH ** -0.5, wgt[:, 1, s % 2, 0:(s + 1) * P],
                                ALU.mult, ALU.mult).then_inc(p_ready, 1)
                        for t in range(NT):
                            b = 2 * (t % 2)
                            dd = den[:, 4 * (t % 2):4 * (t % 2) + 2]
                            rr = den[:, 4 * (t % 2) + 2:4 * (t % 2) + 4]
                            dve.wait_ge(pv_mm, i * 8 + (4 * hh + t + 1))
                            em = em_col[:, t].rearrange("p (d c) -> p d c", d=2)[:, :, ds(i * 2 + hh, 1)]
                            row_sum = ps[:, b:b + 2, DH:DH + 1]
                            dd3 = dd.rearrange("p (d c) -> p d c", c=1)
                            base = 32 * hh + 8 * t
                            dve.scalar_tensor_tensor(dd3, row_sum, -1.0, em, ALU.mult, ALU.max).then_inc(c_chain, 1)
                            dve.wait_ge(c_chain, i * 64 + (base + 1))
                            dve.tensor_tensor(dd3, row_sum, dd3, ALU.max).then_inc(c_chain, 1)
                            dve.wait_ge(c_chain, i * 64 + (base + 2))
                            dve.reciprocal(rr, dd).then_inc(c_chain, 1)
                            dve.wait_ge(c_chain, i * 64 + (base + 3))
                            dve.tensor_scalar(hcomb[:, t], ps[:, b, 0:DH], rr[:, 0:1], None,
                                              ALU.mult).then_inc(c_chain, 5)
                            dve.wait_ge(c_chain, i * 64 + (base + 8))
                            dve.scalar_tensor_tensor(hcomb[:, t], ps[:, b + 1, 0:DH], rr[:, 1:2], hcomb[:, t],
                                                     ALU.mult, ALU.add).then_inc(pv_out, 1)
                        dve.wait_ge(rsh_ready, i * 2 + (hh + 1))
                        for t in range(NT):
                            dve.tensor_scalar(hcomb[:, t], hcomb[:, t], rsh[:, t:t + 1], None,
                                              ALU.mult).then_inc(hn_ready, 1)
                        dve.wait_ge(hn_t, i * 2 + (hh + 1))
                        for c in range(2):
                            dve.scalar_tensor_tensor(hm[:, ds(i * 4 + (2 * hh + c), 1)].rearrange("p a b -> p (a b)"),
                                                     ps[:, c], mh_col[:, ds(i * 4 + (2 * hh + c), 1)],
                                                     o_t[:, 2 * hh + c], ALU.mult, ALU.mult).then_inc(hm_ready, 1)
        for half, base in ((0, D0), (1, D2)):
            src = hm if half else uf
            for k in range(KM):
                dve.wait_ge(bh_ready, KM * half + k + 1)
                dve.tensor_tensor(bl[:, k], src[:, k], bh[:, k].bitcast(F32), ALU.subtract).then_inc(bl_ready, 1)
            per = 8 if half == 0 else 12
            chain0 = 0 if half == 0 else 8 * D_IT
            with dve.Fori(0, D_IT) as i:
                for j in range(D_N):
                    split_lo(base, D_N, i, j + 1)
                    if j == 7:
                        for m in range(4):
                            dve.wait_ge(sig_exp, i * 4 + (4 * D_IT * half + m + 1))
                            dve.tensor_scalar(sig[:, m], sig[:, m], 1.0, None, ALU.add).then_inc(d_chain, 1)
                            dve.wait_ge(d_chain, i * per + (chain0 + 2 * m + 1))
                            dve.reciprocal(sig[:, m], sig[:, m]).then_inc(d_chain, 1)
                    if j == 11:
                        dve.wait_ge(chunk_used, i * D_N + (base + D_N))
                        dve.wait_ge(d_chain, i * per + (chain0 + 8))
                        for m in range(4):
                            dst = merged[:, ds(i * 4 + m, 1)].rearrange("p a b -> p (a b)")
                            if half == 0:
                                ins = dve.tensor_tensor(dst, ps[:, 4 + m], sig[:, m], ALU.mult)
                            else:
                                dve.tensor_tensor(sig[:, m], ps[:, 4 + m], sig[:, m], ALU.mult).then_inc(d_chain, 1)
                                dve.wait_ge(d_chain, i * per + (chain0 + 8 + m + 1))
                                ins = dve.tensor_tensor(dst, dst, sig[:, m], ALU.add)
                        ins.then_inc(merged_ready, 1)
        for k in range(KD):
            dve.wait_ge(mh_ready, k + 1)
            dve.tensor_tensor(xl[:, k], merged[:, k], xh[:, k].bitcast(F32), ALU.subtract).then_inc(ml_ready, 1)

        def add_out(i, g, it):
            dve.wait_ge(chunk_used, i * E_N + (E0 + 8 * (g + 1)))
            if g == 0 and it == 0:
                dve.wait_ge(x2_in, 16 * NT)
            for t in range(NT):
                dst = x2[:, t, ds(i * 2 * NB + g * NB, NB)]
                dve.tensor_tensor(dst, dst, ps[:, 4 * g + t], ALU.add).then_inc(x2_ready, 1)

        with dve.Fori(0, E_IT - 1) as i:
            for j in range(E_N):
                split_lo(E0, E_N, i, j + 1)
                if j % 8 == 7:
                    add_out(i, j // 8, 0)
        for j in range(E_N):
            if j < E_N - 1:
                split_lo(E0 + E_N * (E_IT - 1), 0, 0, j + 1)
            if j % 8 == 7:
                add_out(E_IT - 1, j // 8, 1)
        dve.wait_ge(gain_in, 16)
        for t in range(NT):
            dve.wait_ge(rs2_ready, t + 1)
            dve.scalar_tensor_tensor(h2[:, t], x2[:, t], stat[:, 4 + t:5 + t], gain[:], ALU.mult,
                                     ALU.mult).then_inc(h2_ready, 1)
            if t:
                for b in (1, 3):
                    dve.wait_ge(h2t_mm, 4 * (t - 1) + b + 1)
                    dve.tensor_copy(h2t[:, 4 * b:4 * b + 4, (t - 1) * P:t * P],
                                    ps[:, (4 * (t - 1) + b) % 4].rearrange("p (k n) -> p k n", k=4)).then_inc(h2t_dve, 1)
        for b in (1, 3):
            dve.wait_ge(h2t_mm, 4 * (NT - 1) + b + 1)
            dve.tensor_copy(h2t[:, 4 * b:4 * b + 4, (NT - 1) * P:NT * P],
                            ps[:, b].rearrange("p (k n) -> p k n", k=4)).then_inc(h2t_dve, 1)
        dve.wait_ge(logit_mm, NT)
        dve.tensor_reduce(stat[:, 8:12], ps[:, 4, 0:NT * E].rearrange("p (t e) -> p t e", t=NT), AXX, ALU.max,
                          negate=True).then_inc(negmax_ready, 1)
        dve.memset(aff[:], 0.0).then_inc(f_chain, 1)
        dve.memset(slot[:], -1.0).then_inc(f_chain, 1)
        dve.memset(e_ones[:], 1.0).then_inc(f_chain, 1)
        dve.wait_ge(expl_ready, NT)
        dve.reciprocal(stat[:, 16:20], stat[:, 12:16]).then_inc(f_chain, 1)
        dve.wait_ge(f_chain, 4)
        for t in range(NT):
            dve.tensor_scalar(aff[:, t, 0:E], logit[:, t], stat[:, 16 + t:17 + t], None,
                              ALU.mult).then_inc(aff_ready, 1)
        dve.wait_ge(aff_t_mm, 1)
        dve.tensor_copy(work[:], ps[0:E, 5]).then_inc(f_chain, 1)
        n = 5
        for r in range(CAP // 8):
            dve.wait_ge(f_chain, n)
            dve.max(top8[:], work[:]).then_inc(f_chain, 1)
            dve.wait_ge(f_chain, n + 1)
            dve.match_replace(work[:], top8[:], work[:], -1.0).then_inc(f_chain, 1)
            n += 2
        dve.wait_ge(f_chain, n)
        dve.tensor_scalar(picked[:], work[:], 0.0, None, ALU.is_lt).then_inc(f_chain, 1)
        dve.wait_ge(f_chain, n + 1)
        dve.tensor_tensor_scan(place[:], e_ones[:], picked[:], 0.0, ALU.mult, ALU.add).then_inc(f_chain, 1)
        dve.wait_ge(f_chain, n + 2)
        dve.tensor_tensor(place[:], place[:], picked[:], ALU.mult).then_inc(f_chain, 1)
        dve.wait_ge(f_chain, n + 3)
        dve.tensor_scalar(place[:], place[:], 1.0, None, ALU.subtract).then_inc(f_chain, 1)
        dve.wait_ge(slot_mm, 1)
        dve.tensor_copy(slot[:, :, 0:E], ps[:, 6, 0:NT * E].rearrange("p (t e) -> p t e", t=NT)).then_inc(slot_ready, 1)

        G_N = 48

        def split_elo(i, j):
            dve.wait_ge(ehi_ready, i * G_N + (j + 1))
            dve.tensor_tensor(elo[:, j % 2], eraw[:, j % 4], ehi[:, j % 2].bitcast(F32),
                              ALU.subtract).then_inc(elo_ready, 1)

        def gathered_lo(g, c):
            dve.wait_ge(xgh_ready, 2 * g + (c + 1))
            dve.tensor_tensor(xg[:, 8 * c:8 * c + 8, CAP:2 * CAP], ps[:, c].rearrange("p (k n) -> p k n", k=8),
                              xg[:, 8 * c:8 * c + 8, 0:CAP].bitcast(F32), ALU.subtract).then_inc(xgl_ready, 1)

        def build_onehot(g):
            dve.tensor_tensor(onehot[:], cst[:, C_IOTA:C_IOTA + P].unsqueeze(1).to_broadcast([P, NT, P]),
                              slot[:, :, ds(g, 1)].to_broadcast([P, NT, P]), ALU.is_equal).then_inc(onehot_ready, 1)

        def gate_out(g, slot_at):
            dve.wait_ge(gate_g_mm, g + 1)
            dve.tensor_copy(gate[:, slot_at:slot_at + 1], ps[:, 2, 0:1]).then_inc(gate_ready, 1)

        def accumulate(k):
            n0, blk = k
            dve.wait_ge(sc_out_mm, n0 + (blk + 1))
            t, b = blk // 4, blk % 4
            dst = x2[:, t, b * NB:(b + 1) * NB]
            dve.tensor_tensor(dst, dst, ps[:, 4 + b], ALU.add).then_inc(acc_ready, 1)

        dve.wait_ge(chunk_used, DENSE)
        dve.memset(yh[:].bitcast(F32), 0.0).then_inc(y_zero, 1)
        dve.memset(yl[:].bitcast(F32), 0.0).then_inc(y_zero, 1)
        dve.memset(onehot_t[:].bitcast(F32), 0.0).then_inc(y_zero, 1)
        dve.wait_ge(slot_ready, 1)
        build_onehot(0)
        gathered_lo(0, 0)
        gathered_lo(0, 1)
        gate_out(0, 0)
        split_elo(0, 0)
        split_elo(0, 1)

        def expert_iteration(i, last):
            for j in range(G_N):
                ee, c = j // 24, j % 24
                if j and not (last and j == G_N - 1):
                    split_elo(i, j + 1)
                n = i * 2 + ee
                if ee == 0 and c < 8:
                    accumulate((i * 16, 2 * c))
                    accumulate((i * 16, 2 * c + 1))
                if c == 10:
                    dve.wait_ge(a_exp, n + 1)
                    dve.tensor_scalar(act_s[:, 0], act_s[:, 0], 1.0, None, ALU.add).then_inc(g_chain, 1)
                    dve.wait_ge(g_chain, n * 3 + 1)
                    dve.reciprocal(act_s[:, 1], act_s[:, 0]).then_inc(g_chain, 1)
                    dve.wait_ge(g_chain, n * 3 + 2)
                    dve.tensor_tensor(act_s[:, 0], ps[:, 0], act_s[:, 1], ALU.mult).then_inc(g_chain, 1)
                if c == 13:
                    dve.wait_ge(onehot_t_mm, n + 1)
                    build_onehot(n + 1)
                if c == 15:
                    dve.wait_ge(echunk_used, n * 24 + 16)
                    dve.tensor_copy(ab[:, 1, NB:2 * NB], ps[:, 3]).then_inc(b_dve, 1)
                    dve.wait_ge(bt_mm, n + 1)
                    dve.wait_ge(g_chain, n * 3 + 3)
                    dve.tensor_tensor(h_f[:], ps[:, 2], act_s[:, 0], ALU.mult).then_inc(h_ready, 1)
                    dve.wait_ge(hh_ready, n + 1)
                    dve.tensor_tensor(hx[:, :, CAP:2 * CAP], h_f[:].rearrange("p (k n) -> p k n", k=KF),
                                      hx[:, :, 0:CAP].bitcast(F32), ALU.subtract).then_inc(hl_ready, 1)
                if c == 18:
                    gathered_lo(n + 1, 0)
                if c == 20:
                    gathered_lo(n + 1, 1)
                if c == 21:
                    gate_out(n + 1, 1 - ee)
                if c == 23:
                    for b in range(4):
                        dve.wait_ge(yh_ready, n * 4 + (b + 1))
                        dve.scalar_tensor_tensor(yl[:, ee, b * NB:(b + 1) * NB], ps[:, 4 + b], gate[:, ee:ee + 1],
                                                 yh[:, ee, b * NB:(b + 1) * NB].bitcast(F32), ALU.mult,
                                                 ALU.subtract).then_inc(yl_ready, 1)

        with dve.Fori(0, E // 2 - 1) as i:
            expert_iteration(i, False)
            split_elo(i + 1, 1)
        expert_iteration(E // 2 - 1, True)
        for blk in range(16):
            accumulate((16 * (E // 2), blk))
        dve.wait_ge(fg_in, 16)
        for t in range(NT):
            dve.wait_ge(rs3_ready, t + 1)
            dve.scalar_tensor_tensor(x2[:, t], x2[:, t], stat[:, 4 + t:5 + t], fgain[:], ALU.mult,
                                     ALU.mult).then_inc(fin_ready, 1)

    @block.tensor
    def _(pe):
        def three(dst, wh, wl, mh, ml, first, last):
            pe.matmul(dst, wh, mh, start=first, stop=False)
            pe.matmul(dst, wh, ml, start=False, stop=False)
            return pe.matmul(dst, wl, mh, start=False, stop=last)

        def weights_stationary(n0, per, i, j, mh, ml, bank0, k0, k_total, done=None):
            n = n0 + j
            pe.wait_ge(lo_ready, i * per + (n + 1))
            for kk in range(2):
                k = k0 + kk
                for m in range(4):
                    cols = slice(m * P, (m + 1) * P)
                    ins = three(ps[:, bank0 + m], hi[:, n % 2, kk, cols], lo[:, n % 2, kk, cols],
                                mh[:, k], ml[:, k], k == 0, k == k_total - 1)
            ins.then_inc(chunk_used, 1)

        def tokens_stationary(n0, per, i, j, bank0, k0, k_total):
            n = n0 + j
            pe.wait_ge(lo_ready, i * per + (n + 1))
            for kk in range(2):
                k = k0 + kk
                for t in range(NT):
                    tok = slice(t * P, (t + 1) * P)
                    ins = three(ps[:, bank0 + t], xh[:, k, tok], xl[:, k, tok], hi[:, n % 2, kk], lo[:, n % 2, kk],
                                k == 0, k == k_total - 1)
            ins.then_inc(chunk_used, 1)

        pe.wait_ge(consts_in, 16 * 5)
        pe.wait_ge(x_scaled, NT)
        for k in range(KD):
            if k >= 8:
                pe.wait_ge(xl_ready, k - 7)
            for t in range(NT):
                ins = pe.transpose(ps[:, k % 8, t * P:(t + 1) * P], xin[:, t, k * P:(k + 1) * P], ident)
            ins.then_inc(xt_mm, 1)
        pe.wait_ge(xl_ready, KD)
        for i in range(A_IT):
            base = A0 + i * A_N
            for j in range(8):
                weights_stationary(base, 0, 0, j, xh, xl, 0, 2 * j, KD)
            if i == 0:
                pe.wait_ge(dft_lo_ready, 1)
            else:
                pe.wait_ge(uf_act, 2 * i)
                pe.wait_ge(uf_dve, 2 * i)
            pe.wait_ge(ul_ready, 4 * i + 4)
            for b in range(8):
                g, t = b // 4, b % 4
                tok = slice(t * P, (t + 1) * P)
                for k in range(2):
                    ins = three(ps[:, (4 + b) % 8], uh[:, 2 * g + k, tok], ul[:, 2 * g + k, tok],
                                dft_hi[:, k], dft_lo[:, k], k == 0, k == 1)
                ins.then_inc(v_mm, 1)
            pe.wait_ge(vl_ready, 8 * i + 8)
            for t in range(NT):
                n = base + 8 + t
                pe.wait_ge(lo_ready, n + 1)
                for m in range(4):
                    for cs in range(2):
                        c0 = cs * DH + (m % 2) * P
                        ins = three(ps[:, 4 + m], vh[:, t, m // 2, c0:c0 + P], vl[:, t, m // 2, c0:c0 + P],
                                    hi[:, n % 2, cs], lo[:, n % 2, cs], t == 0 and cs == 0, t == NT - 1 and cs == 1)
                ins.then_inc(chunk_used, 1)
        for k in range(KD):
            pe.matmul(ps[0:N_GATE, 0], wif[:, k], xh[:, k].bitcast(F32), start=k == 0, stop=False)
            ins = pe.matmul(ps[0:N_GATE, 0], wif[:, k], xl[:, k].bitcast(F32), start=False, stop=k == KD - 1)
        ins.then_inc(gates_mm, 1)
        pe.wait_ge(g16_ready, 1)
        pe.matmul(ps[0:64, 1], cst[0:N_GATE, C_SELI:C_SELI + 64], r_g16[:], start=True, stop=True)
        pe.matmul(ps[0:64, 2], cst[0:N_GATE, C_SELF:C_SELF + 64], r_g16[:], start=True, stop=True).then_inc(gsel_mm, 1)
        pe.wait_ge(rows_dve, 11)
        for t in range(NT):
            pe.transpose(ps[:, 3, t * 64:(t + 1) * 64], r_a[:, t * P:(t + 1) * P], ident[0:64, 0:64])
        for t in range(NT):
            ins = pe.transpose(ps[:, 3, 256 + t * 64:256 + (t + 1) * 64], r_b[:, t * P:(t + 1) * P],
                               ident[0:64, 0:64])
        ins.then_inc(rows_t, 1)
        pe.wait_ge(cols_ready, 2)
        with pe.Fori(0, C_IT) as i:
            for j in range(8):
                weights_stationary(C0, C_N, i, j, xh, xl, 0, 2 * j, KD)
            for j in range(8):
                weights_stationary(C0, C_N, i, 8 + j, xh, xl, 4, 2 * j, KD)
            pe.wait_ge(kq_act, i * 4 + 2)
            pe.wait_ge(kq_dve, i * 4 + 2)
            for j in range(8):
                tokens_stationary(C0, C_N, i, 16 + j, 0, 2 * j, KD)
            pe.wait_ge(kq_act, i * 4 + 4)
            pe.wait_ge(kq_dve, i * 4 + 4)
            for j in range(8):
                weights_stationary(C0, C_N, i, 24 + j, xh, xl, 4, 2 * j, KD)
            pe.wait_ge(v_act, i * 2 + 2)
            pe.wait_ge(v_dve, i * 2 + 2)
            pe.wait_ge(sel_ready, i + 1)
            pe.wait_ge(ones_ready, 1)
            for hh in range(2):
                if hh:
                    pe.wait_ge(hm_ready, i * 4 + 2)
                for d in range(2):
                    pe.matmul(ps[:, d], sel_pair[:, 2 * hh + d], neg_m[:], start=True,
                              stop=True).then_inc(bc_mm, 1)
                for s in range(NT):
                    if s >= 2:
                        pe.wait_ge(p_ready, i * 16 + (8 * hh + 2 * s - 2))
                    elif hh:
                        pe.wait_ge(pv_out, i * 8 + 4)
                    for c in range(2):
                        ins = pe.matmul(ps[:, 2 + s % 2], k_t[:, 2 * hh + c, s * P:(s + 1) * P],
                                        q_t[:, 2 * hh + c], start=c == 0, stop=c == 1)
                    ins.then_inc(sc_mm, 1)
                pe.wait_ge(p_ready, i * 16 + (8 * hh + 8))
                for t in range(NT):
                    if t >= 2:
                        pe.wait_ge(pv_out, i * 8 + (4 * hh + t - 1))
                    b = 2 * (t % 2)
                    for s in range(t + 1):
                        f0 = s * NT - s * (s - 1) // 2 + t - s
                        pe.matmul(ps[:, b, 0:DH + 1], prob[:, 0, f0], v_aug[:, s, hh], start=s == 0, stop=s == t)
                    for s in range(t, NT):
                        ins = pe.matmul(ps[:, b + 1, 0:DH + 1], prob[:, 1, s * (s + 1) // 2 + t], v_aug[:, s, hh],
                                        start=s == t, stop=s == NT - 1)
                    ins.then_inc(pv_mm, 1)
                pe.wait_ge(hn_ready, i * 8 + (4 * hh + 4))
                for t in range(NT):
                    for c in range(2):
                        ins = pe.transpose(ps[:, c, t * P:(t + 1) * P], hcomb[:, t, c * P:(c + 1) * P], ident)
                ins.then_inc(hn_t, 1)
            pe.wait_ge(hm_ready, i * 4 + 4)
            pe.wait_ge(o_exp, i * 4 + 4)
        for half, base in ((0, D0), (1, D2)):
            with pe.Fori(0, D_IT) as i:
                for j in range(8):
                    weights_stationary(base, D_N, i, j, xh, xl, 0, 2 * j, KD)
                pe.wait_ge(bl_ready, KM * (half + 1))
                pe.wait_ge(merged_ready, i + D_IT * half)
                for j in range(4):
                    weights_stationary(base, D_N, i, 8 + j, bh, bl, 4, 2 * j, KM)
                pe.wait_ge(sig_exp, i * 4 + (4 * D_IT * half + 4))
        pe.wait_ge(merged_ready, 2 * D_IT)
        pe.wait_ge(ml_ready, KD)
        with pe.Fori(0, E_IT) as i:
            for g in range(2):
                pe.wait_ge(x2_ready, i * 8 + (0 if g == 0 else 0))
                for j in range(8):
                    tokens_stationary(E0, E_N, i, 8 * g + j, 4 * g, 2 * j, KD)
            pe.wait_ge(x2_ready, i * 8 + 8)
        for t in range(NT):
            pe.wait_ge(h2_ready, t + 1)
            for b in range(4):
                n = 4 * t + b
                if t:
                    pe.wait_ge(h2t_act, 2 * (t - 1) + b // 2 + 1)
                    pe.wait_ge(h2t_dve, 2 * (t - 1) + (b + 1) // 2)
                for k in range(4):
                    dk = 4 * b + k
                    ins = pe.transpose(ps[:, n % 4, k * P:(k + 1) * P], h2[:, t, dk * P:(dk + 1) * P], ident)
                ins.then_inc(h2t_mm, 1)
            if t == 0:
                pe.wait_ge(wr_in, 16)
        for t in range(NT):
            pe.wait_ge(h2t_act, 2 * t + 2)
            pe.wait_ge(h2t_dve, 2 * t + 2)
            for k in range(KD):
                ins = pe.matmul(ps[:, 4, t * E:(t + 1) * E], h2t[:, k, t * P:(t + 1) * P], wif[:, k],
                                start=k == 0, stop=k == KD - 1)
            ins.then_inc(logit_mm, 1)
        pe.wait_ge(aff_ready, NT)
        for t in range(NT):
            ins = pe.transpose(ps[0:E, 5, t * P:(t + 1) * P], aff[:, t, 0:E], ident)
        ins.then_inc(aff_t_mm, 1)
        pe.wait_ge(f_chain, 5 + 2 * (CAP // 8) + 4)
        for t in range(NT):
            ins = pe.transpose(ps[:, 6, t * E:(t + 1) * E], place[:, t * P:(t + 1) * P], ident[0:E, 0:E])
        ins.then_inc(slot_mm, 1)

        def gather(ks, done):
            for k in ks:
                for t in range(NT):
                    ins = pe.matmul(ps[:, k // 8, (k % 8) * CAP:(k % 8 + 1) * CAP], h2[:, t, k * P:(k + 1) * P],
                                    onehot[:, t, 0:CAP], start=t == 0, stop=t == NT - 1)
            if done:
                ins.then_inc(gather_mm, 1)

        def gather_gate(g):
            for t in range(NT):
                ins = pe.matmul(ps[:, 2, 0:1], onehot[:, t], aff[:, t, ds(g, 1)], start=t == 0, stop=t == NT - 1)
            ins.then_inc(gate_g_mm, 1)

        def scatter(blk):
            t, b = blk // 4, blk % 4
            tok, cols = slice(t * P, (t + 1) * P), slice(b * NB, (b + 1) * NB)
            pe.matmul(ps[:, 4 + b], onehot_t[:, 0, tok], yh[:, 0, cols], start=True, stop=False)
            pe.matmul(ps[:, 4 + b], onehot_t[:, 0, tok], yl[:, 0, cols], start=False, stop=False)
            pe.matmul(ps[:, 4 + b], onehot_t[:, 1, tok], yh[:, 1, cols], start=False, stop=False)
            pe.matmul(ps[:, 4 + b], onehot_t[:, 1, tok], yl[:, 1, cols], start=False,
                      stop=True).then_inc(sc_out_mm, 1)

        G_N = 48
        pe.wait_ge(onehot_ready, 1)
        gather(range(0, 8), True)
        gather(range(8, 16), True)
        gather_gate(0)
        pe.wait_ge(y_zero, 3)
        with pe.Fori(0, E // 2) as i:
            for ee in range(2):
                n = i * 2 + ee
                pe.wait_ge(xgl_ready, n * 2 + 2)
                for c in range(24):
                    j = 24 * ee + c
                    if c == 16:
                        pe.wait_ge(hl_ready, n + 1)
                        if ee == 0:
                            pe.wait_ge(acc_ready, i * 16 + 16)
                        pe.wait_ge(onehot_ready, n + 2)
                    pe.wait_ge(elo_ready, i * G_N + (j + 1))
                    if c < 16:
                        for kk in range(2):
                            k = 2 * (c % 8) + kk
                            for half in range(2):
                                dst = ps[:, 2 * (c // 8) + half]
                                cols = slice(kk * FE + half * NB, kk * FE + (half + 1) * NB)
                                pe.matmul(dst, xg[:, k], ehi[:, j % 2, cols], start=k == 0, stop=False)
                                ins = pe.matmul(dst, xg[:, k], elo[:, j % 2, cols], start=False, stop=k == KD - 1)
                    else:
                        k = c - 16
                        for b in range(4):
                            cols = slice(b * NB, (b + 1) * NB)
                            pe.matmul(ps[:, 4 + b], hx[:, k], ehi[:, j % 2, cols], start=k == 0, stop=False)
                            ins = pe.matmul(ps[:, 4 + b], hx[:, k], elo[:, j % 2, cols], start=False,
                                            stop=k == KF - 1)
                    ins.then_inc(echunk_used, 1)
                    if ee == 0 and c < 8:
                        if c == 0:
                            pe.wait_ge(yl_ready, i * 8)
                            pe.wait_ge(onehot_t_ready, i * 2)
                        for blk in (2 * c, 2 * c + 1):
                            if blk >= 4:
                                pe.wait_ge(acc_ready, i * 16 + (blk - 3))
                            scatter(blk)
                    if c == 8:
                        pe.wait_ge(a_out, n * 2 + 2)
                        for f in range(KF):
                            ins = pe.matmul(ps[:, 0, f * CAP:(f + 1) * CAP], ab[:, 0, f * P:(f + 1) * P], pair_sum,
                                            start=True, stop=True)
                        ins.then_inc(at_mm, 1)
                    if c == 12:
                        for t in range(NT):
                            ins = pe.transpose(ps[:, 1, t * P:(t + 1) * P], onehot[:, t], ident)
                        ins.then_inc(onehot_t_mm, 1)
                    if c == 15:
                        pe.wait_ge(b_act, n + 1)
                        pe.wait_ge(b_dve, n + 1)
                        for f in range(KF):
                            ins = pe.matmul(ps[:, 2, f * CAP:(f + 1) * CAP], ab[:, 1, f * P:(f + 1) * P], pair_sum,
                                            start=True, stop=True)
                        ins.then_inc(bt_mm, 1)
                    if 16 <= c < 20:
                        gather(range(4 * (c - 16), 4 * (c - 16) + 4), c in (17, 19))
                    if c == 20:
                        gather_gate(n + 1)
        pe.wait_ge(yl_ready, 4 * E)
        pe.wait_ge(onehot_t_ready, E)
        for blk in range(16):
            if blk >= 4:
                pe.wait_ge(acc_ready, 16 * (E // 2) + blk - 3)
            scatter(blk)


_INS = ["x", "norm1_g", "w_in", "b_if", "mh_g", "w_a", "w_b", "w_out", "norm2_g", "w_router", "w1", "w3", "w2",
        "final_g"]


def kernel(**inputs):
    import concourse.bacc as bacc
    from concourse.bass_utils import run_bass_kernel_spmd

    nc = bacc.Bacc("TRN2", target_bir_lowering=False, num_devices=1)
    arrays = {f"in_{n}": np.ascontiguousarray(inputs[n]) for n in _INS}
    arrays["in_consts"], arrays["in_dft_channel"], arrays["in_dft_token"] = shape_constants()
    views = {n: nc.dram_tensor(n, a.shape, mybir.dt.from_np(a.dtype), kind="ExternalInput").ap()
             for n, a in arrays.items()}
    out = nc.dram_tensor("out", (1, SEQ, D), F32, kind="ExternalOutput").ap()
    make(nc, views, out)
    return run_bass_kernel_spmd(nc, [arrays], core_ids=[0]).results[0]["out"]


def make(nc, v, out):
    build(nc, v["in_x"].rearrange("b s d -> (b s) d"), v["in_norm1_g"],
          v["in_w_in"].rearrange("l d n -> (l d) n"), v["in_b_if"], v["in_mh_g"],
          v["in_w_a"].rearrange("l d n -> (l d) n"), v["in_w_b"].rearrange("l d n -> (l d) n"),
          v["in_w_out"].rearrange("l d n -> (l d) n"), v["in_norm2_g"],
          v["in_w_router"].rearrange("l d n -> (l d) n"),
          v["in_w1"].rearrange("l e d n -> (l e) d n"), v["in_w3"].rearrange("l e d n -> (l e) d n"),
          v["in_w2"].rearrange("l e d n -> (l e) d n"), v["in_final_g"], v["in_consts"], v["in_dft_channel"],
          v["in_dft_token"], out.rearrange("b s d -> (b s) d"))
```

```python
from contextlib import ExitStack

import numpy as np
import concourse.bass as bass
from concourse import mybir

ACT = mybir.ActivationFunctionType
ALU = mybir.AluOpType
F32 = mybir.dt.float32
F32R = mybir.dt.float32r
BF16 = mybir.dt.bfloat16
AXX = mybir.AxisListType.X
ds = bass.ds

P = 128
SEQ, D = 512, 2048
NT, KD = SEQ // P, D // P
H, DH = 4, 256
DM = H * DH
KM = DM // P
N_GATE = 4 * H
E, CAP, FE = 16, 64, 1024
KF = FE // P
EPS = 1e-6
NB = 512
COL_Q, COL_K, COL_V, COL_O, COL_U = (DM * i for i in range(5))
COL_IF = 5 * DM
COL_GA = COL_IF + N_GATE
COL_GB = COL_GA + D
MASKED = -1e30
DENSE_RING, DENSE_AHEAD = 4, 3

C_ID, C_IOTA, C_PAIR, C_SELI, C_SELF, C_MASK, C_SELROW = 0, 128, 256, 320, 384, 448, 1472
C_END = C_SELROW + 8 * P


def shape_constants():
    c = np.zeros((P, C_END), np.float32)
    p = np.arange(P)
    c[p, C_ID + p] = 1.0
    c[:, C_IOTA:C_IOTA + P] = np.arange(P) % CAP
    c[p, C_PAIR + p % CAP] = 1.0
    for h in range(H):
        for direction in range(2):
            c[2 * direction * H + h, C_SELI + 32 * direction + h] = 1.0
            c[(2 * direction + 1) * H + h, C_SELF + 32 * direction + h] = 1.0
            at = C_SELROW + (2 * h + direction) * P
            c[32 * direction + h, at:at + P] = 1.0
    later = np.where(p[None, :] >= p[:, None], 0.0, MASKED)
    c[:, C_MASK:C_MASK + NB] = np.tile(later, (1, NT))
    c[:, C_MASK + NB:C_MASK + 2 * NB] = np.tile(later.T, (1, NT))
    a = 2 * np.pi * (np.outer(np.arange(DH), np.arange(DH)) % DH) / DH
    channel = np.concatenate([np.cos(a), -np.sin(a)], 1) / np.sqrt(DH)
    a = 2 * np.pi * (np.outer(np.arange(SEQ), np.arange(SEQ)) % SEQ) / SEQ
    token = np.concatenate([np.cos(a), np.sin(a)], 1) / np.sqrt(SEQ)
    return c, channel.astype(np.float32), token.astype(np.float32)


def build(nc, x, norm1_g, w_in, b_if, mh_g, w_a, w_b, w_out, norm2_g, w_router, w1, w3, w2, final_g,
          consts, dft_channel, dft_token, out):
    ctx = ExitStack()
    ctx.enter_context(nc.allow_non_contiguous_dma(reason="small per-channel vectors"))
    KB = 1024
    BASE = 16512

    def sb(name, kb, shape, dt=F32):
        return nc.alloc_sbuf_tensor_at(name, shape, dt, offset=BASE + int(kb * KB))

    def sem(name):
        return ctx.enter_context(nc.semaphore(name))

    cst = sb("cst", 0, [P, C_END])
    wif = sb("wif", 9.75, [P, KD, N_GATE])
    small = sb("small", 10.75, [P, 320])
    raw = sb("raw", 12, [P, DENSE_RING, 2, NB])
    lo = sb("lo", 12, [P, DENSE_RING, 2, NB], F32R)
    hi = sb("hi", 28, [P, DENSE_RING, 2, NB], F32R)
    xh = sb("xh", 44, [P, KD, NB], F32R)
    xl = sb("xl", 76, [P, KD, NB], F32R)
    uh = sb("uh", 108, [P, 4, NB], F32R)
    ul = sb("ul", 116, [P, 4, NB], F32R)
    dft_raw = sb("dft_raw", 124, [P, 2, NB])
    dft_hi = sb("dft_hi", 128, [P, 2, NB], F32R)
    dft_lo = sb("dft_lo", 132, [P, 2, NB], F32R)
    junk = sb("junk", 108, [P, D])
    xin = sb("xin", 140, [P, NT, D])
    vh = sb("vh", 140, [P, NT, 2, NB], F32R)
    vl = sb("vl", 156, [P, NT, 2, NB], F32R)
    uf = sb("uf", 172, [P, KM, NB])
    q_t = sb("q_t", 108, [P, 4, NB])
    k_t = sb("k_t", 116, [P, 4, NB])
    o_t = sb("o_t", 124, [P, 4, NB])
    v_aug = sb("v_aug", 132, [P, NT, 2, DH + 1])
    prob = sb("prob", 140.5, [P, 2, 10, P])
    hcomb = sb("hcomb", 150.5, [P, NT, DH])
    wgt = sb("wgt", 154.5, [P, 2, 2, NB])
    neg_m = sb("neg_m", 162.5, [64, NB])
    diag = sb("diag", 164.5, [P, 2, NB])
    a_col = sb("a_col", 168.5, [P, NT, 64])
    em_col = sb("em_col", 169.5, [P, NT, 64])
    sel_pair = sb("sel_pair", 204, [64, 4, P])
    r_g16 = sb("r_g16", 140.5, [N_GATE, NB])
    r_ones = sb("r_ones", 142.5, [64, NB])
    r_1 = sb("r_1", 144.5, [64, NB])
    r_2 = sb("r_2", 146.5, [64, NB])
    r_b = sb("r_b", 148.5, [64, NB])
    r_m = sb("r_m", 150.5, [64, NB])
    r_a = sb("r_a", 152.5, [64, NB])
    hm = sb("hm", 188, [P, KM, NB])
    merged = sb("merged", 108, [P, KD, NB])
    bh = sb("bh", 140, [P, KM, NB], F32R)
    bl = sb("bl", 156, [P, KM, NB], F32R)
    sig = sb("sig", 172, [P, 4, NB])
    x2 = sb("x2", 140, [P, NT, D])
    x2t = sb("x2t", 108, [P, KD, NB])
    gain = sb("gain", 76, [P, D])
    h2 = sb("h2", 12, [P, NT, D])
    logit = sb("logit", 5.75, [P, NT, E])
    work = sb("work", 88, [E, NB])
    picked = sb("picked", 90, [E, NB])
    place = sb("place", 86, [E, NB])
    e_ones = sb("e_ones", 3.75, [E, NB])
    top8 = sb("top8", 84, [E, 8])
    h2_parts = sb("h2_parts", 108, [P, NT, 2, D], BF16)
    h2_rest = sb("h2_rest", 92, [P, NT, D], BF16)
    aff = sb("aff", 204, [P, NT, E + 1])
    slot = sb("slot", 204.5, [P, NT, E + 1])
    gate = sb("gate", 205, [P, 1])
    stat = sb("stat", 205.25, [P, 48])
    ring_at = (172, 180, 188, 196, 28, 36)
    eraw = [sb(f"eraw{s}", kb, [P, D]) for s, kb in enumerate(ring_at)]
    elo = [sb(f"elo{s}", kb, [P, D], F32R) for s, kb in enumerate(ring_at)]
    ehi = sb("ehi", 44, [P, 3, D], F32R)
    act_s = sb("act_s", 68, [P, NB])
    onehot = sb("onehot", 70, [P, NT, P])
    onehot_b = sb("onehot_b", 72, [P, NT, CAP], BF16)
    h_f = sb("h_f", 73, [P, NB])
    xg = sb("xg", 76, [P, KD, P], F32R)
    ab = sb("ab", 84, [P, FE])
    hx = sb("hx", 88, [P, KF, P], F32R)
    onehot_t = sb("onehot_t", 1.75, [P, NB], F32R)
    scattered = sb("scattered", 5.75, [P, 2, NB])
    yh = sb("yh", 12, [P, D], F32R)
    yl = sb("yl", 20, [P, D], F32R)
    fgain = sb("fgain", 44, [P, D])
    junk_g = sb("junk_g", 60, [P, D])

    ps = ctx.enter_context(nc.psum_tensor("ps", [P, 8, NB], F32))

    ident = cst[:, C_ID:C_ID + P]
    iota = cst[:, C_IOTA:C_IOTA + P]
    pair_sum = cst[:, C_PAIR:C_PAIR + CAP]
    g1_col = small[:, 0:16]
    g2_col = small[:, 64:80]
    ss2_parts = small[:, 80:96]
    mh_col = small[:, 16:24]
    bif_col = small[0:N_GATE, 24:25]
    ss1 = small[:, 28:32]
    rs1 = small[:, 32:36]
    neg_half = small[:, 36:40]
    den = small[:, 40:48]
    ssh = small[:, 48:52]
    rsh = small[:, 52:56]
    junk_h = sb("junk_h", 171, [P, DH])
    eps4 = small[:, 56:60]
    junk_f = sb("junk_f", 3.75, [P, NB])

    def row_chunk(w, k, col, g):
        width = (w.shape[1] - col) // NB * NB
        block = w[k * P:(k + 2) * P, col:col + width].rearrange("(k p) (g n) -> p g k n", p=P, n=NB)
        return block[:, ds(g, 1)].rearrange("p g k n -> p (g k) n")

    A_N, C_N, D_N, E_N = 12, 32, 12, 16
    A_IT, C_IT, D_IT, E_IT = 2, 2, 4, 2
    A0 = 0
    C0 = A0 + A_N * A_IT
    D0 = C0 + C_N * C_IT
    D2 = D0 + D_N * D_IT
    E0 = D2 + D_N * D_IT
    DENSE = E0 + E_N * E_IT

    consts_in = sem("consts_in")
    dft_in = sem("dft_in")
    x_in = [sem(f"x_in{t}") for t in range(NT)]
    raw_in = [sem(f"raw_in{s}") for s in range(4)]
    hi_ready, lo_ready, chunk_used = sem("hi_ready"), sem("lo_ready"), sem("chunk_used")
    neg_half_set = sem("neg_half_set")
    ss1_ready, rs1_mid, rs1_ready = sem("ss1_ready"), sem("rs1_mid"), sem("rs1_ready")
    x_scaled, xt_mm, xh_ready, xl_ready = sem("x_scaled"), sem("xt_mm"), sem("xh_ready"), sem("xl_ready")
    dft_hi_ready, dft_lo_ready = sem("dft_hi_ready"), sem("dft_lo_ready")
    uh_ready, ul_ready = sem("uh_ready"), sem("ul_ready")
    v_mm, vh_ready, vl_ready = sem("v_mm"), sem("vh_ready"), sem("vl_ready")
    uf_act, uf_dve = sem("uf_act"), sem("uf_dve")
    gates_mm, g16_ready, gsel_mm = sem("gates_mm"), sem("g16_ready"), sem("gsel_mm")
    rows_dve, rows_act, rows_t = sem("rows_dve"), sem("rows_act"), sem("rows_t")
    cols_ready = sem("cols_ready")
    kq_act, kq_dve, v_act, v_dve, o_exp, o_dve = (sem("kq_act"), sem("kq_dve"), sem("v_act"), sem("v_dve"),
                                                  sem("o_exp"), sem("o_dve"))
    sel_ready, ones_ready = sem("sel_ready"), sem("ones_ready")
    bc_mm, diag_ready, wgt_ready, sc_mm, p_ready = (sem("bc_mm"), sem("diag_ready"), sem("wgt_ready"),
                                                    sem("sc_mm"), sem("p_ready"))
    pv_mm, pv_out, c_chain = sem("pv_mm"), sem("pv_out"), sem("c_chain")
    ssh_ready, rsh_mid, rsh_ready, hn_ready, hn_t, hm_ready = (sem("ssh_ready"), sem("rsh_mid"), sem("rsh_ready"),
                                                               sem("hn_ready"), sem("hn_t"), sem("hm_ready"))
    bh_ready, bl_ready = sem("bh_ready"), sem("bl_ready")
    sig_tanh, d_chain, merged_ready = sem("sig_tanh"), sem("d_chain"), sem("merged_ready")
    mh_ready, ml_ready = sem("mh_ready"), sem("ml_ready")
    x2_in, x2_ready = sem("x2_in"), sem("x2_ready")
    gain_in, wr_in, wg_ready = sem("gain_in"), sem("wr_in"), sem("wg_ready")
    x2t_mm, x2t_act, x2t_dve = sem("x2t_mm"), sem("x2t_act"), sem("x2t_dve")
    logit_mm, logit_added = sem("logit_mm"), sem("logit_added")
    sq2_ready, ss2_ready, rs2_mid, rs2_ready, h2_ready = (sem("sq2_ready"), sem("ss2_ready"), sem("rs2_mid"),
                                                          sem("rs2_ready"), sem("h2_ready"))
    part1_ready, rem1_ready, part2_ready, rest_ready = (sem("part1_ready"), sem("rem1_ready"), sem("part2_ready"),
                                                        sem("rest_ready"))
    logit_scaled, negmax_ready, expl_ready, aff_ready = (sem("logit_scaled"), sem("negmax_ready"),
                                                         sem("expl_ready"), sem("aff_ready"))
    aff_t_mm, f_chain, slot_mm, slot_ready = sem("aff_t_mm"), sem("f_chain"), sem("slot_mm"), sem("slot_ready")
    eraw_in = [sem(f"eraw_in{s}") for s in range(len(eraw))]
    ehi_ready, elo_ready, echunk_used = sem("ehi_ready"), sem("elo_ready"), sem("echunk_used")
    onehot_b_ready, scat_out = sem("onehot_b_ready"), sem("scat_out")
    onehot_ready, gather_mm, xgh_ready, xgl_ready = (sem("onehot_ready"), sem("gather_mm"), sem("xgh_ready"),
                                                     sem("xgl_ready"))
    gate_g_mm, gate_ready, onehot_t_mm, onehot_t_ready = (sem("gate_g_mm"), sem("gate_ready"),
                                                          sem("onehot_t_mm"), sem("onehot_t_ready"))
    a_out, at_mm, a_tanh, silu_ready = sem("a_out"), sem("at_mm"), sem("a_tanh"), sem("silu_ready")
    b_out, bt_mm, h_ready, hh_ready, hl_ready = (sem("b_out"), sem("bt_mm"),
                                                              sem("h_ready"), sem("hh_ready"), sem("hl_ready"))
    yh_ready, yl_ready, sc_out_mm, acc_ready = (sem("yh_ready"), sem("yl_ready"),
                                                      sem("sc_out_mm"), sem("acc_ready"))
    fg_in, ss3_ready, rs3_mid, rs3_ready, fin_ready, out_written = (sem("fg_in"), sem("ss3_ready"), sem("rs3_mid"),
                                                                    sem("rs3_ready"), sem("fin_ready"),
                                                                    sem("out_written"))
    block = ctx.enter_context(nc.Block())

    E_CH = 24
    RING, E_HI = len(eraw), 3

    @block.sync
    def _(sp):
        def load(n0, per, i, j, src, slots=1):
            n = n0 + j
            if n >= 4 and slots:
                sp.wait_ge(chunk_used, i * per + (n - 4 + slots))
            sp.dma_start(raw[:, n % 4], src).then_inc(raw_in[n % 4], 16)

        sp.dma_start(cst[:], consts).then_inc(consts_in, 16)
        for j in range(4):
            load(A0, 0, 0, j, row_chunk(w_in, 2 * j, COL_U, 0))
        for i in range(A_IT):
            for j in range(4 if i == 0 else 0, 8):
                load(A0 + i * A_N, 0, 0, j, row_chunk(w_in, 2 * j, COL_U, i))
            for t in range(NT):
                load(A0 + i * A_N, 0, 0, 8 + t,
                     dft_token[t * P:(t + 1) * P, :].rearrange("p (k n) -> p k n", k=2))
        with sp.Fori(1, C_IT + 1) as turn:
            i = turn - 1
            for g, col in enumerate((COL_K, COL_Q, COL_V, COL_O)):
                for j in range(8):
                    load(C0, C_N, i, 8 * g + j, row_chunk(w_in, 2 * j, col, i),
                         slots=2 if (g, j) == (0, 7) else 0 if (g, j) == (1, 0) else 1)
        for base, col, w in ((D0, COL_GB, w_b), (D2, COL_GA, w_a)):
            with sp.Fori(1, D_IT + 1) as turn:
                i = turn - 1
                for j in range(8):
                    load(base, D_N, i, j, row_chunk(w_in, 2 * j, col, i), slots=2 if j == 7 else 1)
                for j in range(4):
                    load(base, D_N, i, 8 + j, row_chunk(w, 2 * j, 0, i), slots=0 if j == 0 else 1)
        with sp.Fori(1, E_IT + 1) as turn:
            i = turn - 1
            for g in range(2):
                for j in range(8):
                    load(E0, E_N, i, 8 * g + j, row_chunk(w_out, 2 * j, 0, i * 2 + g))
        def load_expert(n, c, used=True):
            if used:
                sp.wait_ge(echunk_used, n * E_CH + (c - RING + 1))
            if c < 16:
                w = w1 if c < 8 else w3
                k = 2 * (c % 8)
                src = w[ds(n, 1), k * P:(k + 2) * P, :].rearrange("e (k p) n -> p (e k) n", p=P)
                dst = eraw[c % RING].rearrange("p (k n) -> p k n", k=2)
            else:
                k = c - 16
                src = w2[ds(n, 1), k * P:(k + 1) * P, :].rearrange("e p n -> p (e n)")
                dst = eraw[c % RING][:]
            sp.dma_start(dst, src).then_inc(eraw_in[c % RING], 16)

        for c in range(E_CH):
            if c == 0:
                sp.wait_ge(merged_ready, 2 * D_IT)
            if c == 4:
                sp.wait_ge(rest_ready, NT)
            load_expert(0, c, used=c >= RING)
        with sp.Fori(2, E + 1) as turn:
            for c in range(E_CH):
                load_expert(turn - 1, c)
        for t in range(NT):
            sp.wait_ge(fin_ready, t + 1)
            sp.dma_start(out[t * P:(t + 1) * P, :], x2[:, t]).then_inc(out_written, 16)
        sp.wait_ge(out_written, 16 * NT)

    @block.scalar
    def _(act):
        copy = ACT.Copy

        def split_hi(n0, per, i, j):
            n = n0 + j
            act.wait_ge(raw_in[n % 4], (i * per // 4 if isinstance(i, int) else i * (per // 4)) * 16
                        + 16 * (n // 4 + 1))
            if n >= DENSE_RING:
                act.wait_ge(chunk_used, i * per + (n - DENSE_RING + 1))
            act.activation(hi[:, n % DENSE_RING], raw[:, n % DENSE_RING], copy).then_inc(hi_ready, 1)

        for t in range(NT):
            act.dma_start(xin[:, t], x[t * P:(t + 1) * P, :]).then_inc(x_in[t], 16)
        act.dma_start(g1_col, norm1_g.rearrange("o (k p) -> p (o k)", p=P)).then_inc(consts_in, 16)
        act.dma_start(g2_col, norm2_g.rearrange("o (k p) -> p (o k)", p=P)).then_inc(consts_in, 16)
        act.dma_start(mh_col, mh_g.rearrange("o (k p) -> p (o k)", p=P)).then_inc(consts_in, 16)
        act.dma_start(bif_col, b_if.rearrange("o a (h c) -> (o a h) c", c=1)).then_inc(consts_in, 16)
        act.dma_start(wif[:], w_in[:, COL_IF:COL_IF + N_GATE].rearrange("(k p) n -> p k n", p=P)).then_inc(consts_in, 16)
        act.dma_start(dft_raw[:], dft_channel.rearrange("(k p) n -> p k n", p=P)).then_inc(dft_in, 16)
        for t in range(NT):
            act.wait_ge(x_in[t], 16)
            if t:
                act.wait_ge(ss1_ready, t)
            act.activation(junk[:], xin[:, t], ACT.Square, accum_out=ss1[:, t:t + 1]).then_inc(ss1_ready, 1)
        for j in range(DENSE_AHEAD):
            split_hi(A0, 0, 0, j)
        act.wait_ge(consts_in, 16 * 6)
        for k in range(KD):
            act.wait_ge(xt_mm, k + 1)
            act.activation(xh[:, k], ps[:, k % 8], copy, scale=g1_col[:, k:k + 1]).then_inc(xh_ready, 1)
        act.wait_ge(dft_in, 16)
        act.wait_ge(ss1_ready, NT)
        act.activation(dft_hi[:], dft_raw[:], copy).then_inc(dft_hi_ready, 1)
        for i in range(A_IT):
            for j in range(A_N):
                split_hi(A0 + i * A_N, 0, 0, j + DENSE_AHEAD)
                if j == 7:
                    act.wait_ge(chunk_used, A0 + i * A_N + 8)
                    for m in range(4):
                        act.activation(uh[:, m], ps[:, m], copy).then_inc(uh_ready, 1)
                    for b in range(8):
                        act.wait_ge(v_mm, 8 * i + b + 1)
                        act.activation(vh[:, b % 4, b // 4], ps[:, (4 + b) % 8], copy).then_inc(vh_ready, 1)
                if j == 11:
                    act.wait_ge(chunk_used, A0 + (i + 1) * A_N)
                    for m in range(2):
                        act.activation(uf[:, 4 * i + m], ps[:, 4 + m], copy).then_inc(uf_act, 1)
        act.wait_ge(gates_mm, 1)
        act.activation(r_g16[:], ps[0:N_GATE, 0], ACT.Identity, bias=bif_col).then_inc(g16_ready, 1)
        act.wait_ge(gsel_mm, 1)
        act.activation(r_1[:], ps[0:64, 2], ACT.Abs).then_inc(rows_act, 1)
        act.wait_ge(rows_act, 1)
        act.activation(r_2[:], r_1[:], ACT.Exp, scale=-1.0).then_inc(rows_act, 1)
        act.wait_ge(rows_act, 2)
        act.activation(r_1[:], r_2[:], ACT.Ln, bias=1.0).then_inc(rows_act, 1)
        act.wait_ge(rows_t, 1)
        act.activation(a_col[:], ps[:, 3, 0:256].rearrange("p (t c) -> p t c", t=NT), copy).then_inc(cols_ready, 1)
        act.activation(em_col[:], ps[:, 3, 256:512].rearrange("p (t c) -> p t c", t=NT), ACT.Exp,
                       scale=-1.0).then_inc(cols_ready, 1)
        with act.Fori(0, C_IT) as i:
            for j in range(C_N):
                split_hi(C0, C_N, i, j + DENSE_AHEAD)
                if j == 7:
                    act.wait_ge(chunk_used, i * C_N + (C0 + 8))
                    for m in range(2):
                        act.activation(k_t[:, m], ps[:, m], copy).then_inc(kq_act, 1)
                if j == 15:
                    act.wait_ge(chunk_used, i * C_N + (C0 + 16))
                    for m in range(2):
                        act.activation(q_t[:, m], ps[:, 4 + m], copy).then_inc(kq_act, 1)
                if j == 23:
                    act.wait_ge(chunk_used, i * C_N + (C0 + 24))
                    for t in range(2):
                        act.activation(v_aug[:, t, :, 0:DH], ps[:, t].rearrange("p (h d) -> p h d", h=2),
                                       copy).then_inc(v_act, 1)
                if j == 31:
                    act.wait_ge(chunk_used, i * C_N + (C0 + 32))
                    for m in range(4):
                        act.activation(o_t[:, m], ps[:, 4 + m], ACT.Exp, scale=-1.0).then_inc(o_exp, 1)
                    for hh in range(2):
                        act.wait_ge(diag_ready, i * 4 + 2 * hh + 2)
                        for s in range(NT):
                            if s >= 2:
                                act.wait_ge(p_ready, i * 16 + 8 * hh + 2 * s - 2)
                            elif hh:
                                act.wait_ge(p_ready, i * 16 + 8)
                            for d in range(2):
                                bias = a_col[:, s, ds(i * 2 + (hh + 32 * d), 1)]
                                act.activation(wgt[:, d, s % 2, s * P:(s + 1) * P], diag[:, d, s * P:(s + 1) * P],
                                               ACT.Exp, bias=bias).then_inc(wgt_ready, 1)
                                rest = slice((s + 1) * P, NB) if d == 0 else slice(0, s * P)
                                if rest.stop > rest.start:
                                    act.activation(wgt[:, d, s % 2, rest], ps[:, d, rest],
                                                   ACT.Exp, bias=bias).then_inc(wgt_ready, 1)
                        for t in range(NT):
                            act.wait_ge(pv_out, i * 8 + 4 * hh + t + 1)
                            if t or hh:
                                act.wait_ge(ssh_ready, i * 8 + 4 * hh + t)
                            act.activation(junk_h[:], hcomb[:, t], ACT.Square, scale=DH ** -0.5,
                                           accum_out=ssh[:, t:t + 1]).then_inc(ssh_ready, 1)
        for half, base in ((0, D0), (1, D2)):
            src = hm if half else uf
            if half:
                act.wait_ge(chunk_used, D2)
            else:
                act.wait_ge(hm_ready, 4 * C_IT)
                act.wait_ge(hn_t, 2 * C_IT)
            for k in range(KM):
                act.activation(bh[:, k], src[:, k], copy, scale=0.5).then_inc(bh_ready, 1)
            if not half:
                act.wait_ge(bl_ready, KM)

            def gated_group(i, merge_from=None):
                for j in range(D_N):
                    split_hi(base, D_N, i, j + DENSE_AHEAD)
                    if j == 7:
                        act.wait_ge(chunk_used, i * D_N + (base + 8))
                        if half or not isinstance(i, int):
                            act.wait_ge(merged_ready, i + D_IT * half)
                        for m in range(4):
                            act.activation(sig[:, m], ps[:, m], ACT.Tanh, scale=0.5).then_inc(sig_tanh, 1)
                    if j >= 8 and merge_from is not None:
                        for k in range(3 * (j - 8), 3 * (j - 7)):
                            act.activation(xh[:, k], merged[:, k], copy).then_inc(mh_ready, 1)

            if half == 0:
                gated_group(0)
                with act.Fori(1, D_IT) as i:
                    gated_group(i)
            else:
                with act.Fori(0, D_IT - 1) as i:
                    gated_group(i)
                gated_group(D_IT - 1, merge_from=0)
        act.wait_ge(merged_ready, 2 * D_IT)
        for k in range(12, KD):
            act.activation(xh[:, k], merged[:, k], copy).then_inc(mh_ready, 1)
        act.wait_ge(chunk_used, E0)
        for t in range(NT):
            act.dma_start(x2[:, t], x[t * P:(t + 1) * P, :]).then_inc(x2_in, 16)
        act.dma_start(wif[:], w_router.rearrange("(k p) n -> p k n", p=P)).then_inc(wr_in, 16)

        def squares(g):
            act.wait_ge(x2_ready, 4 * g + 4)
            for t in range(NT):
                n = 4 * g + t
                if n:
                    act.wait_ge(sq2_ready, n)
                act.activation(junk_f[:], x2[:, t, g * NB:(g + 1) * NB], ACT.Square,
                               accum_out=ss2_parts[:, n:n + 1]).then_inc(sq2_ready, 1)

        def transposed_act(g):
            for c in range(2):
                act.wait_ge(x2t_mm, 4 * g + c + 1)
                act.activation(x2t[:, 4 * g + c], ps[:, 4 * (g % 2) + c], copy).then_inc(x2t_act, 1)

        for g in range(4):
            for j in range(8):
                if 8 * g + j < 4 * 8 - DENSE_AHEAD:
                    split_hi(E0, 0, 0, 8 * g + j + DENSE_AHEAD)
                if g and j == 1:
                    squares(g - 1)
                if g and j == 3:
                    transposed_act(g - 1)
        act.wait_ge(chunk_used, DENSE)
        act.dma_start(gain[:], norm2_g[0:1, :].partition_broadcast(P)).then_inc(gain_in, 16)
        squares(3)
        transposed_act(3)
        for t in range(2):
            act.wait_ge(h2_ready, t + 1)
            if t == 0:
                act.wait_ge(logit_mm, 4)
            act.activation(h2_parts[:, t, 0], h2[:, t], copy).then_inc(part1_ready, 1)
        for t in range(NT):
            act.wait_ge(negmax_ready, 1)
            act.activation(logit[:, t], logit[:, t], ACT.Exp, bias=stat[:, 8 + t:9 + t],
                           accum_out=stat[:, 12 + t:13 + t]).then_inc(expl_ready, 1)
        for t in range(2, NT):
            act.wait_ge(h2_ready, t + 1)
            act.activation(h2_parts[:, t, 0], h2[:, t], copy).then_inc(part1_ready, 1)
        for t in range(NT):
            act.wait_ge(rem1_ready, t + 1)
            act.activation(h2_parts[:, t, 1], h2[:, t], copy).then_inc(part2_ready, 1)

        def split_ehi(n, c, first=False):
            act.wait_ge(eraw_in[c % RING], n * (E_CH // RING * 16) + 16 * (c // RING + 1))
            if not first:
                act.wait_ge(echunk_used, n * E_CH + (c - E_HI + 1))
            act.activation(ehi[:, c % E_HI], eraw[c % RING][:], copy).then_inc(ehi_ready, 1)

        def gathered_hi(n, half):
            act.wait_ge(gather_mm, 2 * n + (half + 1))
            act.activation(xg[:, 8 * half:8 * half + 8, 0:CAP], ps[:, half].rearrange("p (k n) -> p k n", k=8),
                           copy).then_inc(xgh_ready, 1)

        def onehot_bf16(n):
            act.wait_ge(onehot_ready, n + 1)
            act.activation(onehot_b[:], onehot[:, :, 0:CAP], copy).then_inc(onehot_b_ready, 1)

        act.wait_ge(logit_mm, 4)
        for c in range(E_HI):
            split_ehi(0, c, True)
        onehot_bf16(0)
        gathered_hi(0, 0)
        gathered_hi(0, 1)

        def expert(n, last):
            for c in range(E_CH):
                if c and not (last and c > E_CH - E_HI):
                    split_ehi(n, c + E_HI - 1)
                if 2 <= c <= 9:
                    for blk in (2 * c - 4, 2 * c - 3):
                        act.wait_ge(sc_out_mm, n * 16 + (blk + 1))
                        act.wait_ge(acc_ready, n * 16 + (blk - 1 + 2))
                        act.activation(scattered[:, blk % 2], ps[:, 4 + blk % 4], copy).then_inc(scat_out, 1)
                if c == 15:
                    act.wait_ge(echunk_used, n * E_CH + 16)
                    for b in range(2):
                        act.activation(ab[:, b * NB:(b + 1) * NB], ps[:, 2 + b], copy).then_inc(b_out, 1)
                    onehot_bf16(n + 1)
                    act.wait_ge(h_ready, n + 1)
                    act.activation(hx[:, :, 0:CAP], h_f[:].rearrange("p (k n) -> p k n", k=KF),
                                   copy).then_inc(hh_ready, 1)
                if c == 7:
                    act.wait_ge(echunk_used, n * E_CH + 8)
                    for b in range(2):
                        act.activation(ab[:, b * NB:(b + 1) * NB], ps[:, b], copy).then_inc(a_out, 1)
                if c == 9:
                    act.wait_ge(at_mm, n + 1)
                    act.activation(act_s[:], ps[:, 0], ACT.Tanh, scale=0.5).then_inc(a_tanh, 1)
                if c == 13:
                    act.wait_ge(onehot_t_mm, n + 1)
                    act.activation(onehot_t[:], ps[:, 1], copy).then_inc(onehot_t_ready, 1)
                if c == 19:
                    gathered_hi(n + 1, 0)
                if c == 22:
                    gathered_hi(n + 1, 1)
                if c == 23:
                    act.wait_ge(echunk_used, n * E_CH + E_CH)
                    act.wait_ge(gate_ready, n + 1)
                    for b in range(4):
                        act.activation(yh[:, b * NB:(b + 1) * NB], ps[:, 4 + b], copy,
                                       scale=gate[:, 0:1]).then_inc(yh_ready, 1)

        with act.Fori(0, E - 1) as n:
            expert(n, False)
            split_ehi(n + 1, E_HI - 1)
        expert(E - 1, True)
        act.wait_ge(echunk_used, E * E_CH)
        act.dma_start(fgain[:], final_g.rearrange("(o n) -> o n", o=1).partition_broadcast(P)).then_inc(fg_in, 16)
        for t in range(NT):
            act.wait_ge(acc_ready, 16 * E + 2 + 4 * (t + 1))
            if t:
                act.wait_ge(ss3_ready, t)
            act.activation(junk_g[:], x2[:, t], ACT.Square, accum_out=stat[:, t:t + 1]).then_inc(ss3_ready, 1)

    @block.gpsimd
    def _(pool):
        pool.memset(neg_half, -0.5).then_inc(neg_half_set, 1)
        pool.memset(eps4, EPS).then_inc(neg_half_set, 1)
        for t in range(NT):
            pool.wait_ge(ss1_ready, t + 1)
            if t == 0:
                pool.wait_ge(neg_half_set, 2)
            pool.tensor_scalar(rs1[:, t:t + 1], ss1[:, t:t + 1], 1.0 / D, EPS, ALU.mult, ALU.add).then_inc(rs1_mid, 1)
            pool.wait_ge(rs1_mid, t + 1)
            pool.tensor_tensor(rs1[:, t:t + 1], rs1[:, t:t + 1], neg_half[:, 0:1], ALU.pow).then_inc(rs1_ready, 1)
        pool.wait_ge(dft_lo_ready, 1)
        pool.wait_ge(ul_ready, 4 * A_IT)
        pool.wait_ge(chunk_used, C0)
        pool.memset(v_aug[:, :, :, DH:DH + 1], 1.0).then_inc(ones_ready, 1)
        with pool.Fori(0, C_IT) as i:
            for hh in range(2):
                pool.wait_ge(ssh_ready, i * 8 + 4 * hh + 4)
                pool.tensor_tensor(rsh, ssh, eps4, ALU.add).then_inc(rsh_mid, 1)
                pool.wait_ge(rsh_mid, i * 2 + (hh + 1))
                pool.tensor_tensor(rsh, rsh, neg_half, ALU.pow).then_inc(rsh_ready, 1)
        pool.wait_ge(ss2_ready, 1)
        pool.tensor_scalar(stat[:, 4:8], stat[:, 0:4], 1.0 / D, EPS, ALU.mult, ALU.add).then_inc(rs2_mid, 1)
        pool.wait_ge(rs2_mid, 1)
        pool.tensor_tensor(stat[:, 4:8], stat[:, 4:8], neg_half, ALU.pow).then_inc(rs2_ready, 1)
        for t in range(NT):
            pool.wait_ge(part1_ready, t + 1)
            pool.tensor_tensor(h2[:, t], h2[:, t], h2_parts[:, t, 0], ALU.subtract).then_inc(rem1_ready, 1)
        pool.wait_ge(rest_ready, 2)
        pool.memset(yh[:].bitcast(F32), 0.0).then_inc(yh_ready, 4)
        pool.memset(yl[:].bitcast(F32), 0.0).then_inc(yl_ready, 4)
        pool.wait_ge(aff_t_mm, 1)
        pool.memset(onehot_t[:].bitcast(F32), 0.0).then_inc(onehot_t_ready, 1)
        pool.wait_ge(x2_ready, 16)
        pool.sem_inc(acc_ready, 2)
        with pool.Fori(0, E) as n:
            for blk in range(16):
                t, b = blk // 4, blk % 4
                pool.wait_ge(scat_out, n * 16 + (blk + 1))
                dst = x2[:, t, b * NB:(b + 1) * NB]
                pool.tensor_tensor(dst, dst, scattered[:, blk % 2], ALU.add).then_inc(acc_ready, 1)
        for t in range(NT):
            pool.wait_ge(ss3_ready, t + 1)
            pool.tensor_scalar(stat[:, 4 + t:5 + t], stat[:, t:t + 1], 1.0 / D, EPS, ALU.mult,
                               ALU.add).then_inc(rs3_mid, 1)
            pool.wait_ge(rs3_mid, t + 1)
            pool.tensor_tensor(stat[:, 4 + t:5 + t], stat[:, 4 + t:5 + t], neg_half[:, 0:1],
                               ALU.pow).then_inc(rs3_ready, 1)

    @block.vector
    def _(dve):
        def split_lo(n0, per, i, j):
            n = n0 + j
            dve.wait_ge(hi_ready, i * per + (n + 1))
            at = n % DENSE_RING
            dve.tensor_tensor(lo[:, at], raw[:, at], hi[:, at].bitcast(F32),
                              ALU.subtract).then_inc(lo_ready, 1)

        for t in range(NT):
            dve.wait_ge(rs1_ready, t + 1)
            dve.tensor_scalar(xin[:, t], xin[:, t], rs1[:, t:t + 1], None, ALU.mult).then_inc(x_scaled, 1)
        for j in range(DENSE_AHEAD):
            split_lo(A0, 0, 0, j)
        for k in range(KD):
            dve.wait_ge(xh_ready, k + 1)
            dve.scalar_tensor_tensor(xl[:, k], ps[:, k % 8], g1_col[:, k:k + 1], xh[:, k].bitcast(F32),
                                     ALU.mult, ALU.subtract).then_inc(xl_ready, 1)
        dve.wait_ge(dft_hi_ready, 1)
        dve.tensor_tensor(dft_lo[:], dft_raw[:], dft_hi[:].bitcast(F32), ALU.subtract).then_inc(dft_lo_ready, 1)
        for i in range(A_IT):
            for j in range(A_N):
                split_lo(A0 + i * A_N, 0, 0, j + DENSE_AHEAD)
                if j == 7:
                    for m in range(4):
                        dve.wait_ge(uh_ready, 4 * i + m + 1)
                        dve.tensor_tensor(ul[:, m], ps[:, m], uh[:, m].bitcast(F32),
                                          ALU.subtract).then_inc(ul_ready, 1)
                    for b in range(8):
                        dve.wait_ge(vh_ready, 8 * i + b + 1)
                        dve.tensor_tensor(vl[:, b % 4, b // 4], ps[:, (4 + b) % 8],
                                          vh[:, b % 4, b // 4].bitcast(F32), ALU.subtract).then_inc(vl_ready, 1)
                if j == 11:
                    dve.wait_ge(chunk_used, A0 + (i + 1) * A_N)
                    for m in range(2, 4):
                        dve.tensor_copy(uf[:, 4 * i + m], ps[:, 4 + m]).then_inc(uf_dve, 1)
        dve.memset(r_ones[:], 1.0).then_inc(rows_dve, 1)
        dve.memset(r_b[:], 0.0).then_inc(rows_dve, 1)
        dve.wait_ge(gsel_mm, 1)
        dve.wait_ge(rows_act, 3)
        dve.scalar_tensor_tensor(r_2[:], ps[0:64, 2], 0.0, r_1[:], ALU.min, ALU.subtract).then_inc(rows_dve, 1)
        dve.wait_ge(rows_dve, 3)
        dve.tensor_tensor_scan(r_b[0:4], r_ones[0:4], r_2[0:4], 0.0, ALU.mult, ALU.add).then_inc(rows_dve, 1)
        dve.tensor_tensor_scan(r_b[32:36, ::-1], r_ones[32:36, ::-1], r_2[32:36, ::-1], 0.0,
                               ALU.mult, ALU.add).then_inc(rows_dve, 1)
        dve.wait_ge(rows_dve, 5)
        dve.tensor_tensor(r_a[:], ps[0:64, 1], r_b[:], ALU.subtract).then_inc(rows_dve, 1)
        dve.memset(r_m[:], 0.0).then_inc(rows_dve, 1)
        dve.wait_ge(rows_dve, 7)
        dve.tensor_tensor_scan(r_m[0:4], r_ones[0:4], r_a[0:4], 0.0, ALU.mult, ALU.max).then_inc(rows_dve, 1)
        dve.tensor_tensor_scan(r_m[32:36, ::-1], r_ones[32:36, ::-1], r_a[32:36, ::-1], 0.0,
                               ALU.mult, ALU.max).then_inc(rows_dve, 1)
        dve.wait_ge(rows_dve, 9)
        dve.tensor_scalar(neg_m[:], r_m[:], -1.0, None, ALU.mult).then_inc(rows_dve, 1)
        dve.tensor_tensor(r_b[:], r_b[:], r_m[:], ALU.add).then_inc(rows_dve, 1)
        with dve.Fori(0, C_IT) as i:
            for j in range(C_N):
                split_lo(C0, C_N, i, j + DENSE_AHEAD)
                if j == 7:
                    dve.wait_ge(chunk_used, i * C_N + (C0 + 8))
                    for m in range(2, 4):
                        dve.tensor_copy(k_t[:, m], ps[:, m]).then_inc(kq_dve, 1)
                    dve.tensor_copy(sel_pair[:].rearrange("p a b -> p (a b)"),
                                    cst[0:64, ds(i * 4 * P + C_SELROW, 4 * P)]).then_inc(sel_ready, 1)
                if j == 15:
                    dve.wait_ge(chunk_used, i * C_N + (C0 + 16))
                    for m in range(2, 4):
                        dve.tensor_copy(q_t[:, m], ps[:, 4 + m]).then_inc(kq_dve, 1)
                if j == 23:
                    dve.wait_ge(chunk_used, i * C_N + (C0 + 24))
                    for t in range(2, 4):
                        dve.tensor_copy(v_aug[:, t, :, 0:DH],
                                        ps[:, t].rearrange("p (h d) -> p h d", h=2)).then_inc(v_dve, 1)
                if j == 31:
                    for m in range(4):
                        dve.wait_ge(o_exp, i * 4 + (m + 1))
                        dve.tensor_scalar(o_t[:, m], o_t[:, m], 1.0, None, ALU.add).then_inc(o_dve, 1)
                        dve.wait_ge(o_dve, i * 8 + (2 * m + 1))
                        dve.reciprocal(o_t[:, m], o_t[:, m]).then_inc(o_dve, 1)
                    for hh in range(2):
                        for d in range(2):
                            dve.wait_ge(bc_mm, i * 4 + (2 * hh + d + 1))
                            dve.tensor_tensor(diag[:, d], ps[:, d],
                                              cst[:, C_MASK + d * NB:C_MASK + (d + 1) * NB],
                                              ALU.add).then_inc(diag_ready, 1)
                        w_seen = 0
                        for s in range(NT):
                            w_seen += 4 - (s == NT - 1) - (s == 0)
                            dve.wait_ge(sc_mm, i * 8 + (4 * hh + s + 1))
                            dve.wait_ge(wgt_ready, i * 28 + (14 * hh + w_seen))
                            f0 = s * NT - s * (s - 1) // 2
                            dve.scalar_tensor_tensor(
                                prob[:, 0, f0:f0 + NT - s].rearrange("p a b -> p (a b)"),
                                ps[:, 2 + s % 2, s * P:NB], DH ** -0.5, wgt[:, 0, s % 2, s * P:NB],
                                ALU.mult, ALU.mult).then_inc(p_ready, 1)
                            b0 = s * (s + 1) // 2
                            dve.scalar_tensor_tensor(
                                prob[:, 1, b0:b0 + s + 1].rearrange("p a b -> p (a b)"),
                                ps[:, 2 + s % 2, 0:(s + 1) * P], DH ** -0.5, wgt[:, 1, s % 2, 0:(s + 1) * P],
                                ALU.mult, ALU.mult).then_inc(p_ready, 1)
                        for t in range(NT):
                            b = 2 * (t % 2)
                            dd = den[:, 4 * (t % 2):4 * (t % 2) + 2]
                            rr = den[:, 4 * (t % 2) + 2:4 * (t % 2) + 4]
                            dve.wait_ge(pv_mm, i * 8 + (4 * hh + t + 1))
                            em = em_col[:, t].rearrange("p (d c) -> p d c", d=2)[:, :, ds(i * 2 + hh, 1)]
                            row_sum = ps[:, b:b + 2, DH:DH + 1]
                            dd3 = dd.rearrange("p (d c) -> p d c", c=1)
                            base = 32 * hh + 8 * t
                            dve.scalar_tensor_tensor(dd3, row_sum, -1.0, em, ALU.mult, ALU.max).then_inc(c_chain, 1)
                            dve.wait_ge(c_chain, i * 64 + (base + 1))
                            dve.tensor_tensor(dd3, row_sum, dd3, ALU.max).then_inc(c_chain, 1)
                            dve.wait_ge(c_chain, i * 64 + (base + 2))
                            dve.reciprocal(rr, dd).then_inc(c_chain, 1)
                            dve.wait_ge(c_chain, i * 64 + (base + 3))
                            dve.tensor_scalar(hcomb[:, t], ps[:, b, 0:DH], rr[:, 0:1], None,
                                              ALU.mult).then_inc(c_chain, 5)
                            dve.wait_ge(c_chain, i * 64 + (base + 8))
                            dve.scalar_tensor_tensor(hcomb[:, t], ps[:, b + 1, 0:DH], rr[:, 1:2], hcomb[:, t],
                                                     ALU.mult, ALU.add).then_inc(pv_out, 1)
                        dve.wait_ge(rsh_ready, i * 2 + (hh + 1))
                        for t in range(NT):
                            dve.tensor_scalar(hcomb[:, t], hcomb[:, t], rsh[:, t:t + 1], None,
                                              ALU.mult).then_inc(hn_ready, 1)
                        dve.wait_ge(hn_t, i * 2 + (hh + 1))
                        for c in range(2):
                            dve.scalar_tensor_tensor(hm[:, ds(i * 4 + (2 * hh + c), 1)].rearrange("p a b -> p (a b)"),
                                                     ps[:, c], mh_col[:, ds(i * 4 + (2 * hh + c), 1)],
                                                     o_t[:, 2 * hh + c], ALU.mult, ALU.mult).then_inc(hm_ready, 1)
        def merged_lo(ks):
            for k in ks:
                dve.wait_ge(mh_ready, k + 1)
                dve.tensor_tensor(xl[:, k], merged[:, k], xh[:, k].bitcast(F32), ALU.subtract).then_inc(ml_ready, 1)

        for half, base in ((0, D0), (1, D2)):
            src = hm if half else uf
            for k in range(KM):
                dve.wait_ge(bh_ready, KM * half + k + 1)
                dve.scalar_tensor_tensor(bl[:, k], src[:, k], 0.5, bh[:, k].bitcast(F32), ALU.mult,
                                         ALU.subtract).then_inc(bl_ready, 1)

            def merge_group(i, merge_from=None):
                for j in range(D_N):
                    split_lo(base, D_N, i, j + DENSE_AHEAD)
                    if j >= 8 and merge_from is not None:
                        merged_lo(range(3 * (j - 8), 3 * (j - 7)))
                    if j == 11:
                        dve.wait_ge(chunk_used, i * D_N + (base + D_N))
                        for m in range(4):
                            dve.wait_ge(sig_tanh, i * 4 + (4 * D_IT * half + m + 1))
                            dst = merged[:, ds(i * 4 + m, 1)].rearrange("p a b -> p (a b)")
                            if half == 0:
                                ins = dve.scalar_tensor_tensor(dst, sig[:, m], 1.0, ps[:, 4 + m], ALU.add, ALU.mult)
                            else:
                                dve.scalar_tensor_tensor(sig[:, m], sig[:, m], 1.0, ps[:, 4 + m], ALU.add,
                                                         ALU.mult).then_inc(d_chain, 1)
                                dve.wait_ge(d_chain, i * 4 + (m + 1))
                                ins = dve.tensor_tensor(dst, dst, sig[:, m], ALU.add)
                        ins.then_inc(merged_ready, 1)

            if half == 0:
                with dve.Fori(0, D_IT) as i:
                    merge_group(i)
            else:
                with dve.Fori(0, D_IT - 1) as i:
                    merge_group(i)
                merge_group(D_IT - 1, merge_from=0)
        merged_lo(range(12, KD))

        dve.wait_ge(wr_in, 16)
        dve.tensor_tensor(wif[:], wif[:], g2_col.unsqueeze(2).to_broadcast([P, KD, E]), ALU.mult).then_inc(wg_ready, 1)

        def add_out(g):
            dve.wait_ge(chunk_used, E0 + 8 * (g + 1))
            if g == 0:
                dve.wait_ge(x2_in, 16 * NT)
            for t in range(NT):
                dst = x2[:, t, g * NB:(g + 1) * NB]
                dve.tensor_tensor(dst, dst, ps[:, 4 * (g % 2) + t], ALU.add).then_inc(x2_ready, 1)

        def transposed_dve(g):
            for c in range(2, 4):
                dve.wait_ge(x2t_mm, 4 * g + c + 1)
                dve.tensor_copy(x2t[:, 4 * g + c], ps[:, 4 * (g % 2) + c]).then_inc(x2t_dve, 1)

        def add_logits(g):
            dve.wait_ge(logit_mm, g + 1)
            part = ps[:, 4 * (g % 2), 0:NT * E].rearrange("p (t e) -> p t e", t=NT)
            if g == 0:
                dve.tensor_copy(logit[:], part).then_inc(logit_added, 1)
            else:
                dve.wait_ge(logit_added, g)
                dve.tensor_tensor(logit[:], logit[:], part, ALU.add).then_inc(logit_added, 1)

        for g in range(4):
            for j in range(8):
                if 8 * g + j < 4 * 8 - DENSE_AHEAD:
                    split_lo(E0, 0, 0, 8 * g + j + DENSE_AHEAD)
                if g and j == 3:
                    transposed_dve(g - 1)
                if g and j == 6:
                    add_logits(g - 1)
                if j == 7:
                    add_out(g)
        dve.memset(aff[:], 0.0).then_inc(f_chain, 1)
        dve.memset(slot[:], -1.0).then_inc(f_chain, 1)
        dve.wait_ge(sq2_ready, 16)
        dve.memset(e_ones[:], 1.0).then_inc(f_chain, 1)
        dve.tensor_reduce(stat[:, 0:4], ss2_parts.rearrange("p (g t) -> p t g", g=4), AXX,
                          ALU.add).then_inc(ss2_ready, 1)
        transposed_dve(3)

        def normed(t):
            dve.scalar_tensor_tensor(h2[:, t], x2[:, t], stat[:, 4 + t:5 + t], gain[:], ALU.mult,
                                     ALU.mult).then_inc(h2_ready, 1)

        dve.wait_ge(rs2_ready, 1)
        dve.wait_ge(gain_in, 16)
        normed(0)
        normed(1)
        add_logits(3)
        dve.wait_ge(logit_added, 4)
        dve.tensor_tensor(logit[:], logit[:], stat[:, 4:8].unsqueeze(2).to_broadcast([P, NT, E]),
                          ALU.mult).then_inc(logit_scaled, 1)
        dve.wait_ge(logit_scaled, 1)
        dve.tensor_reduce(stat[:, 8:12], logit[:], AXX, ALU.max, negate=True).then_inc(negmax_ready, 1)
        normed(2)
        dve.wait_ge(expl_ready, NT)
        dve.reciprocal(stat[:, 16:20], stat[:, 12:16]).then_inc(f_chain, 1)
        dve.wait_ge(f_chain, 4)
        for t in range(NT):
            dve.tensor_scalar(aff[:, t, 0:E], logit[:, t], stat[:, 16 + t:17 + t], None,
                              ALU.mult).then_inc(aff_ready, 1)
        dve.wait_ge(aff_t_mm, 1)
        dve.tensor_copy(work[:], ps[0:E, 5]).then_inc(f_chain, 1)
        normed(3)
        n = 5
        for r in range(CAP // 8):
            dve.wait_ge(f_chain, n)
            dve.max(top8[:], work[:]).then_inc(f_chain, 1)
            dve.wait_ge(f_chain, n + 1)
            dve.match_replace(work[:], top8[:], work[:], -1.0).then_inc(f_chain, 1)
            n += 2
        dve.wait_ge(f_chain, n)
        dve.tensor_scalar(picked[:], work[:], 0.0, None, ALU.is_lt).then_inc(f_chain, 1)
        dve.wait_ge(f_chain, n + 1)
        dve.tensor_tensor_scan(place[:], e_ones[:], picked[:], 0.0, ALU.mult, ALU.add).then_inc(f_chain, 1)
        dve.wait_ge(f_chain, n + 2)
        dve.tensor_tensor(place[:], place[:], picked[:], ALU.mult).then_inc(f_chain, 1)
        dve.wait_ge(f_chain, n + 3)
        dve.tensor_scalar(place[:], place[:], 1.0, None, ALU.subtract).then_inc(f_chain, 1)
        def rest(t):
            dve.wait_ge(part2_ready, t + 1)
            dve.tensor_tensor(h2_rest[:, t], h2[:, t], h2_parts[:, t, 1], ALU.subtract).then_inc(rest_ready, 1)

        rest(0)
        dve.wait_ge(slot_mm, 1)
        dve.tensor_copy(slot[:, :, 0:E], ps[:, 6, 0:NT * E].rearrange("p (t e) -> p t e", t=NT)).then_inc(slot_ready, 1)

        def split_elo(n, c):
            dve.wait_ge(ehi_ready, n * E_CH + (c + 1))
            dve.tensor_tensor(elo[c % RING][:], eraw[c % RING][:], ehi[:, c % E_HI].bitcast(F32),
                              ALU.subtract).then_inc(elo_ready, 1)

        def gathered_lo(n, half):
            dve.wait_ge(xgh_ready, 2 * n + (half + 1))
            dve.tensor_tensor(xg[:, 8 * half:8 * half + 8, CAP:2 * CAP],
                              ps[:, half].rearrange("p (k n) -> p k n", k=8),
                              xg[:, 8 * half:8 * half + 8, 0:CAP].bitcast(F32),
                              ALU.subtract).then_inc(xgl_ready, 1)

        def build_onehot(n):
            dve.tensor_tensor(onehot[:], cst[:, C_IOTA:C_IOTA + P].unsqueeze(1).to_broadcast([P, NT, P]),
                              slot[:, :, ds(n, 1)].to_broadcast([P, NT, P]), ALU.is_equal).then_inc(onehot_ready, 1)

        def gate_out(n):
            dve.wait_ge(gate_g_mm, n + 1)
            dve.tensor_copy(gate[:], ps[:, 2, 0:1]).then_inc(gate_ready, 1)

        dve.wait_ge(slot_ready, 1)
        build_onehot(0)
        for t in range(1, NT):
            rest(t)
        for c in range(E_HI):
            split_elo(0, c)
        gathered_lo(0, 0)
        gathered_lo(0, 1)
        gate_out(0)

        def expert(n, last):
            for c in range(E_CH):
                if c and not (last and c > E_CH - E_HI):
                    split_elo(n, c + E_HI - 1)
                if c == 10:
                    dve.wait_ge(a_tanh, n + 1)
                    dve.scalar_tensor_tensor(act_s[:], act_s[:], 1.0, ps[:, 0], ALU.add,
                                             ALU.mult).then_inc(silu_ready, 1)
                if c == 14:
                    dve.wait_ge(onehot_t_mm, n + 1)
                    build_onehot(n + 1)
                if c == 15:
                    dve.wait_ge(bt_mm, n + 1)
                    dve.wait_ge(silu_ready, n + 1)
                    dve.scalar_tensor_tensor(h_f[:], ps[:, 2], 0.5, act_s[:], ALU.mult,
                                             ALU.mult).then_inc(h_ready, 1)
                    dve.wait_ge(hh_ready, n + 1)
                    dve.tensor_tensor(hx[:, :, CAP:2 * CAP], h_f[:].rearrange("p (k n) -> p k n", k=KF),
                                      hx[:, :, 0:CAP].bitcast(F32), ALU.subtract).then_inc(hl_ready, 1)
                if c == 19:
                    gathered_lo(n + 1, 0)
                if c == 22:
                    gathered_lo(n + 1, 1)
                if c == 23:
                    for b in range(4):
                        dve.wait_ge(yh_ready, n * 4 + (b + 5))
                        dve.scalar_tensor_tensor(yl[:, b * NB:(b + 1) * NB], ps[:, 4 + b], gate[:, 0:1],
                                                 yh[:, b * NB:(b + 1) * NB].bitcast(F32), ALU.mult,
                                                 ALU.subtract).then_inc(yl_ready, 1)
                    dve.wait_ge(yl_ready, n * 4 + 8)
                    gate_out(n + 1)

        with dve.Fori(0, E - 1) as n:
            expert(n, False)
            split_elo(n + 1, E_HI - 1)
        expert(E - 1, True)
        dve.wait_ge(acc_ready, 16 * E + 2)
        for blk in range(16):
            t, b = blk // 4, blk % 4
            dve.wait_ge(sc_out_mm, 16 * E + blk + 1)
            dst = x2[:, t, b * NB:(b + 1) * NB]
            dve.tensor_tensor(dst, dst, ps[:, 4 + b], ALU.add).then_inc(acc_ready, 1)
        dve.wait_ge(fg_in, 16)
        for t in range(NT):
            dve.wait_ge(rs3_ready, t + 1)
            dve.scalar_tensor_tensor(x2[:, t], x2[:, t], stat[:, 4 + t:5 + t], fgain[:], ALU.mult,
                                     ALU.mult).then_inc(fin_ready, 1)

    @block.tensor
    def _(pe):
        def three(dst, wh, wl, mh, ml, first, last):
            pe.matmul(dst, wh, mh, start=first, stop=False)
            pe.matmul(dst, wh, ml, start=False, stop=False)
            return pe.matmul(dst, wl, mh, start=False, stop=last)

        def weights_stationary(n0, per, i, j, mh, ml, bank0, k0, k_total, done=None):
            n = n0 + j
            pe.wait_ge(lo_ready, i * per + (n + 1))
            for kk in range(2):
                k = k0 + kk
                for m in range(4):
                    cols = slice(m * P, (m + 1) * P)
                    ins = three(ps[:, bank0 + m], hi[:, n % DENSE_RING, kk, cols], lo[:, n % DENSE_RING, kk, cols],
                                mh[:, k], ml[:, k], k == 0, k == k_total - 1)
            ins.then_inc(chunk_used, 1)

        def tokens_stationary(n0, per, i, j, bank0, k0, k_total):
            n = n0 + j
            pe.wait_ge(lo_ready, i * per + (n + 1))
            for kk in range(2):
                k = k0 + kk
                for t in range(NT):
                    tok = slice(t * P, (t + 1) * P)
                    ins = three(ps[:, bank0 + t], xh[:, k, tok], xl[:, k, tok], hi[:, n % DENSE_RING, kk], lo[:, n % DENSE_RING, kk],
                                k == 0, k == k_total - 1)
            ins.then_inc(chunk_used, 1)

        pe.wait_ge(consts_in, 16 * 6)
        pe.wait_ge(x_scaled, NT)
        for k in range(KD):
            if k >= 8:
                pe.wait_ge(xl_ready, k - 7)
            for t in range(NT):
                ins = pe.transpose(ps[:, k % 8, t * P:(t + 1) * P], xin[:, t, k * P:(k + 1) * P], ident)
            ins.then_inc(xt_mm, 1)
        pe.wait_ge(xl_ready, KD)
        for i in range(A_IT):
            base = A0 + i * A_N
            for j in range(8):
                weights_stationary(base, 0, 0, j, xh, xl, 0, 2 * j, KD)
            if i == 0:
                pe.wait_ge(dft_lo_ready, 1)
            else:
                pe.wait_ge(uf_act, 2 * i)
                pe.wait_ge(uf_dve, 2 * i)
            pe.wait_ge(ul_ready, 4 * i + 4)
            for b in range(8):
                g, t = b // 4, b % 4
                tok = slice(t * P, (t + 1) * P)
                for k in range(2):
                    ins = three(ps[:, (4 + b) % 8], uh[:, 2 * g + k, tok], ul[:, 2 * g + k, tok],
                                dft_hi[:, k], dft_lo[:, k], k == 0, k == 1)
                ins.then_inc(v_mm, 1)
            pe.wait_ge(vl_ready, 8 * i + 8)
            for t in range(NT):
                n = base + 8 + t
                pe.wait_ge(lo_ready, n + 1)
                for m in range(4):
                    for cs in range(2):
                        c0 = cs * DH + (m % 2) * P
                        ins = three(ps[:, 4 + m], vh[:, t, m // 2, c0:c0 + P], vl[:, t, m // 2, c0:c0 + P],
                                    hi[:, n % DENSE_RING, cs], lo[:, n % DENSE_RING, cs], t == 0 and cs == 0, t == NT - 1 and cs == 1)
                ins.then_inc(chunk_used, 1)
        for k in range(KD):
            pe.matmul(ps[0:N_GATE, 0], wif[:, k], xh[:, k].bitcast(F32), start=k == 0, stop=False)
            ins = pe.matmul(ps[0:N_GATE, 0], wif[:, k], xl[:, k].bitcast(F32), start=False, stop=k == KD - 1)
        ins.then_inc(gates_mm, 1)
        pe.wait_ge(g16_ready, 1)
        pe.matmul(ps[0:64, 1], cst[0:N_GATE, C_SELI:C_SELI + 64], r_g16[:], start=True, stop=True)
        pe.matmul(ps[0:64, 2], cst[0:N_GATE, C_SELF:C_SELF + 64], r_g16[:], start=True, stop=True).then_inc(gsel_mm, 1)
        pe.wait_ge(rows_dve, 11)
        for t in range(NT):
            pe.transpose(ps[:, 3, t * 64:(t + 1) * 64], r_a[:, t * P:(t + 1) * P], ident[0:64, 0:64])
        for t in range(NT):
            ins = pe.transpose(ps[:, 3, 256 + t * 64:256 + (t + 1) * 64], r_b[:, t * P:(t + 1) * P],
                               ident[0:64, 0:64])
        ins.then_inc(rows_t, 1)
        pe.wait_ge(cols_ready, 2)
        with pe.Fori(0, C_IT) as i:
            for j in range(8):
                weights_stationary(C0, C_N, i, j, xh, xl, 0, 2 * j, KD)
            for j in range(8):
                weights_stationary(C0, C_N, i, 8 + j, xh, xl, 4, 2 * j, KD)
            pe.wait_ge(kq_act, i * 4 + 2)
            pe.wait_ge(kq_dve, i * 4 + 2)
            for j in range(8):
                tokens_stationary(C0, C_N, i, 16 + j, 0, 2 * j, KD)
            pe.wait_ge(kq_act, i * 4 + 4)
            pe.wait_ge(kq_dve, i * 4 + 4)
            for j in range(8):
                weights_stationary(C0, C_N, i, 24 + j, xh, xl, 4, 2 * j, KD)
            pe.wait_ge(v_act, i * 2 + 2)
            pe.wait_ge(v_dve, i * 2 + 2)
            pe.wait_ge(sel_ready, i + 1)
            pe.wait_ge(ones_ready, 1)
            for hh in range(2):
                if hh:
                    pe.wait_ge(hm_ready, i * 4 + 2)
                for d in range(2):
                    pe.matmul(ps[:, d], sel_pair[:, 2 * hh + d], neg_m[:], start=True,
                              stop=True).then_inc(bc_mm, 1)
                for s in range(NT):
                    if s >= 2:
                        pe.wait_ge(p_ready, i * 16 + (8 * hh + 2 * s - 2))
                    elif hh:
                        pe.wait_ge(pv_out, i * 8 + 4)
                    for c in range(2):
                        ins = pe.matmul(ps[:, 2 + s % 2], k_t[:, 2 * hh + c, s * P:(s + 1) * P],
                                        q_t[:, 2 * hh + c], start=c == 0, stop=c == 1)
                    ins.then_inc(sc_mm, 1)
                pe.wait_ge(p_ready, i * 16 + (8 * hh + 8))
                for t in range(NT):
                    if t >= 2:
                        pe.wait_ge(pv_out, i * 8 + (4 * hh + t - 1))
                    b = 2 * (t % 2)
                    for s in range(t + 1):
                        f0 = s * NT - s * (s - 1) // 2 + t - s
                        pe.matmul(ps[:, b, 0:DH + 1], prob[:, 0, f0], v_aug[:, s, hh], start=s == 0, stop=s == t)
                    for s in range(t, NT):
                        ins = pe.matmul(ps[:, b + 1, 0:DH + 1], prob[:, 1, s * (s + 1) // 2 + t], v_aug[:, s, hh],
                                        start=s == t, stop=s == NT - 1)
                    ins.then_inc(pv_mm, 1)
                pe.wait_ge(hn_ready, i * 8 + (4 * hh + 4))
                for t in range(NT):
                    for c in range(2):
                        ins = pe.transpose(ps[:, c, t * P:(t + 1) * P], hcomb[:, t, c * P:(c + 1) * P], ident)
                ins.then_inc(hn_t, 1)
            pe.wait_ge(hm_ready, i * 4 + 4)
            pe.wait_ge(o_exp, i * 4 + 4)
        for half, base in ((0, D0), (1, D2)):

            def gated_group(i, first):
                for j in range(8):
                    weights_stationary(base, D_N, i, j, xh, xl, 0, 2 * j, KD)
                pe.wait_ge(bl_ready, KM * (half + 1))
                if not first:
                    pe.wait_ge(merged_ready, i + D_IT * half)
                for j in range(4):
                    weights_stationary(base, D_N, i, 8 + j, bh, bl, 4, 2 * j, KM)
                pe.wait_ge(sig_tanh, i * 4 + (4 * D_IT * half + 4))

            if half == 0:
                gated_group(0, True)
            with pe.Fori(1 - half, D_IT) as i:
                gated_group(i, False)
        def transpose_x2(g):
            pe.wait_ge(x2_ready, 4 * g + 4)
            for c in range(4):
                for t in range(NT):
                    at = (4 * g + c) * P
                    ins = pe.transpose(ps[:, 4 * (g % 2) + c, t * P:(t + 1) * P], x2[:, t, at:at + P], ident)
                ins.then_inc(x2t_mm, 1)

        def logits(g):
            pe.wait_ge(x2t_act, 2 * g + 2)
            pe.wait_ge(x2t_dve, 2 * g + 2)
            if g == 0:
                pe.wait_ge(wg_ready, 1)
            for t in range(NT):
                for c in range(4):
                    k = 4 * g + c
                    ins = pe.matmul(ps[:, 4 * (g % 2), t * E:(t + 1) * E], x2t[:, k, t * P:(t + 1) * P], wif[:, k],
                                    start=c == 0, stop=c == 3)
            ins.then_inc(logit_mm, 1)

        pe.wait_ge(merged_ready, 2 * D_IT)
        for g in range(4):
            if g >= 2:
                pe.wait_ge(logit_added, g - 1)
            for j in range(8):
                if g == 0:
                    pe.wait_ge(ml_ready, 2 * j + 2)
                tokens_stationary(E0, 0, 0, 8 * g + j, 4 * (g % 2), 2 * j, KD)
                if g and j == 2:
                    transpose_x2(g - 1)
                if g and j == 5:
                    logits(g - 1)
        transpose_x2(3)
        logits(3)
        pe.wait_ge(aff_ready, NT)
        for t in range(NT):
            ins = pe.transpose(ps[0:E, 5, t * P:(t + 1) * P], aff[:, t, 0:E], ident)
        ins.then_inc(aff_t_mm, 1)
        pe.wait_ge(f_chain, 5 + 2 * (CAP // 8) + 4)
        for t in range(NT):
            ins = pe.transpose(ps[:, 6, t * E:(t + 1) * E], place[:, t * P:(t + 1) * P], ident[0:E, 0:E])
        ins.then_inc(slot_mm, 1)

        def gather(ks, done):
            for k in ks:
                dst, cols = ps[:, k // 8, (k % 8) * CAP:(k % 8 + 1) * CAP], slice(k * P, (k + 1) * P)
                for t in range(NT):
                    pe.matmul(dst, h2_parts[:, t, 0, cols], onehot_b[:, t], start=t == 0, stop=False)
                    pe.matmul(dst, h2_parts[:, t, 1, cols], onehot_b[:, t], start=False, stop=False)
                    ins = pe.matmul(dst, h2_rest[:, t, cols], onehot_b[:, t], start=False, stop=t == NT - 1)
            if done:
                ins.then_inc(gather_mm, 1)

        def gather_gate(g):
            for t in range(NT):
                ins = pe.matmul(ps[:, 2, 0:1], onehot[:, t], aff[:, t, ds(g, 1)], start=t == 0, stop=t == NT - 1)
            ins.then_inc(gate_g_mm, 1)

        def scatter(blk):
            t, b = blk // 4, blk % 4
            tok, cols = slice(t * P, (t + 1) * P), slice(b * NB, (b + 1) * NB)
            pe.matmul(ps[:, 4 + b], onehot_t[:, tok], yh[:, cols], start=True, stop=False)
            pe.matmul(ps[:, 4 + b], onehot_t[:, tok], yl[:, cols], start=False, stop=True).then_inc(sc_out_mm, 1)

        pe.wait_ge(onehot_b_ready, 1)
        pe.wait_ge(rest_ready, NT)
        gather(range(0, 8), True)
        gather(range(8, 16), True)
        gather_gate(0)
        with pe.Fori(0, E) as n:
            pe.wait_ge(xgl_ready, n * 2 + 2)
            for c in range(E_CH):
                if c == 8:
                    pe.wait_ge(gate_ready, n + 1)
                if c == 16:
                    pe.wait_ge(hl_ready, n + 1)
                    pe.wait_ge(scat_out, n * 16 + 16)
                pe.wait_ge(elo_ready, n * E_CH + (c + 1))
                if c < 16:
                    for kk in range(2):
                        k = 2 * (c % 8) + kk
                        for half in range(2):
                            dst = ps[:, 2 * (c // 8) + half]
                            cols = slice(kk * FE + half * NB, kk * FE + (half + 1) * NB)
                            pe.matmul(dst, xg[:, k], ehi[:, c % E_HI, cols], start=k == 0, stop=False)
                            ins = pe.matmul(dst, xg[:, k], elo[c % RING][:, cols], start=False, stop=k == KD - 1)
                else:
                    k = c - 16
                    for b in range(4):
                        cols = slice(b * NB, (b + 1) * NB)
                        pe.matmul(ps[:, 4 + b], hx[:, k], ehi[:, c % E_HI, cols], start=k == 0, stop=False)
                        ins = pe.matmul(ps[:, 4 + b], hx[:, k], elo[c % RING][:, cols], start=False,
                                        stop=k == KF - 1)
                ins.then_inc(echunk_used, 1)
                if 1 <= c <= 8:
                    if c == 1:
                        pe.wait_ge(yl_ready, n * 4 + 4)
                        pe.wait_ge(onehot_t_ready, n + 1)
                    for blk in (2 * c - 2, 2 * c - 1):
                        if blk >= 4:
                            pe.wait_ge(scat_out, n * 16 + (blk - 3))
                        scatter(blk)
                if c == 8:
                    for f in range(KF):
                        if f % 4 == 0:
                            pe.wait_ge(a_out, n * 2 + (f // 4 + 1))
                        ins = pe.matmul(ps[:, 0, f * CAP:(f + 1) * CAP], ab[:, f * P:(f + 1) * P], pair_sum,
                                        start=True, stop=True)
                    ins.then_inc(at_mm, 1)
                if c == 12:
                    for t in range(NT):
                        ins = pe.transpose(ps[:, 1, t * P:(t + 1) * P], onehot[:, t], ident)
                    ins.then_inc(onehot_t_mm, 1)
                if c == 15:
                    for f in range(KF):
                        if f % 4 == 0:
                            pe.wait_ge(b_out, n * 2 + (f // 4 + 1))
                        ins = pe.matmul(ps[:, 2, f * CAP:(f + 1) * CAP], ab[:, f * P:(f + 1) * P], pair_sum,
                                        start=True, stop=True)
                    ins.then_inc(bt_mm, 1)
                if 16 <= c < 22:
                    if c == 16:
                        pe.wait_ge(onehot_b_ready, n + 2)
                    k = 8 * ((c - 16) // 3) + 3 * ((c - 16) % 3)
                    gather(range(k, k + (2 if c in (18, 21) else 3)), c in (18, 21))
                if c == 22:
                    gather_gate(n + 1)
        pe.wait_ge(yl_ready, 4 * E + 4)
        pe.wait_ge(onehot_t_ready, E + 1)
        for blk in range(16):
            pe.wait_ge(acc_ready, 16 * E + 2 + max(blk - 3, 0))
            scatter(blk)


_INS = ["x", "norm1_g", "w_in", "b_if", "mh_g", "w_a", "w_b", "w_out", "norm2_g", "w_router", "w1", "w3", "w2",
        "final_g"]


def kernel(**inputs):
    import concourse.bacc as bacc
    from concourse.bass_utils import run_bass_kernel_spmd

    nc = bacc.Bacc("TRN2", target_bir_lowering=False, num_devices=1)
    arrays = {f"in_{n}": np.ascontiguousarray(inputs[n]) for n in _INS}
    arrays["in_consts"], arrays["in_dft_channel"], arrays["in_dft_token"] = shape_constants()
    views = {n: nc.dram_tensor(n, a.shape, mybir.dt.from_np(a.dtype), kind="ExternalInput").ap()
             for n, a in arrays.items()}
    out = nc.dram_tensor("out", (1, SEQ, D), F32, kind="ExternalOutput").ap()
    make(nc, views, out)
    return run_bass_kernel_spmd(nc, [arrays], core_ids=[0]).results[0]["out"]


def make(nc, v, out):
    build(nc, v["in_x"].rearrange("b s d -> (b s) d"), v["in_norm1_g"],
          v["in_w_in"].rearrange("l d n -> (l d) n"), v["in_b_if"], v["in_mh_g"],
          v["in_w_a"].rearrange("l d n -> (l d) n"), v["in_w_b"].rearrange("l d n -> (l d) n"),
          v["in_w_out"].rearrange("l d n -> (l d) n"), v["in_norm2_g"],
          v["in_w_router"].rearrange("l d n -> (l d) n"),
          v["in_w1"].rearrange("l e d n -> (l e) d n"), v["in_w3"].rearrange("l e d n -> (l e) d n"),
          v["in_w2"].rearrange("l e d n -> (l e) d n"), v["in_final_g"], v["in_consts"], v["in_dft_channel"],
          v["in_dft_token"], out.rearrange("b s d -> (b s) d"))
```

```python
from contextlib import ExitStack

import numpy as np
import concourse.bass as bass
from concourse import mybir

ACT = mybir.ActivationFunctionType
ALU = mybir.AluOpType
F32 = mybir.dt.float32
F32R = mybir.dt.float32r
BF16 = mybir.dt.bfloat16
AXX = mybir.AxisListType.X
ds = bass.ds

P = 128
SEQ, D = 512, 2048
NT, KD = SEQ // P, D // P
H, DH = 4, 256
DM = H * DH
KM = DM // P
N_GATE = 4 * H
E, CAP, FE = 16, 64, 1024
KF = FE // P
EPS = 1e-6
NB = 512
COL_Q, COL_K, COL_V, COL_O, COL_U = (DM * i for i in range(5))
COL_IF = 5 * DM
COL_GA = COL_IF + N_GATE
COL_GB = COL_GA + D
MASKED = -1e30
DENSE_RING, DENSE_AHEAD = 4, 3

C_ID, C_IOTA, C_PAIR, C_SELI, C_SELF, C_MASK, C_SELROW = 0, 128, 256, 320, 384, 448, 1472
C_END = C_SELROW + 8 * P


def shape_constants():
    c = np.zeros((P, C_END), np.float32)
    p = np.arange(P)
    c[p, C_ID + p] = 1.0
    c[:, C_IOTA:C_IOTA + P] = np.arange(P) % CAP
    c[p, C_PAIR + p % CAP] = 1.0
    for h in range(H):
        for direction in range(2):
            c[2 * direction * H + h, C_SELI + 32 * direction + h] = 1.0
            c[(2 * direction + 1) * H + h, C_SELF + 32 * direction + h] = 1.0
            at = C_SELROW + (2 * h + direction) * P
            c[32 * direction + h, at:at + P] = 1.0
    later = np.where(p[None, :] >= p[:, None], 0.0, MASKED)
    c[:, C_MASK:C_MASK + NB] = np.tile(later, (1, NT))
    c[:, C_MASK + NB:C_MASK + 2 * NB] = np.tile(later.T, (1, NT))
    a = 2 * np.pi * (np.outer(np.arange(DH), np.arange(DH)) % DH) / DH
    channel = np.concatenate([np.cos(a), -np.sin(a)], 1) / np.sqrt(DH)
    a = 2 * np.pi * (np.outer(np.arange(SEQ), np.arange(SEQ)) % SEQ) / SEQ
    token = np.concatenate([np.cos(a), np.sin(a)], 1) / np.sqrt(SEQ)
    return c, channel.astype(np.float32), token.astype(np.float32)


def build(nc, x, norm1_g, w_in, b_if, mh_g, w_a, w_b, w_out, norm2_g, w_router, w1, w3, w2, final_g,
          consts, dft_channel, dft_token, out):
    ctx = ExitStack()
    ctx.enter_context(nc.allow_non_contiguous_dma(reason="small per-channel vectors"))
    KB = 1024
    BASE = 16512

    def sb(name, kb, shape, dt=F32):
        return nc.alloc_sbuf_tensor_at(name, shape, dt, offset=BASE + int(kb * KB))

    def sem(name):
        return ctx.enter_context(nc.semaphore(name))

    cst = sb("cst", 0, [P, C_END])
    wif = sb("wif", 9.75, [P, KD, N_GATE])
    small = sb("small", 10.75, [P, 320])
    raw = sb("raw", 12, [P, DENSE_RING, 2, NB])
    lo = sb("lo", 12, [P, DENSE_RING, 2, NB], F32R)
    hi = sb("hi", 28, [P, DENSE_RING, 2, NB], F32R)
    xh = sb("xh", 44, [P, KD, NB], F32R)
    xl = sb("xl", 76, [P, KD, NB], F32R)
    uh = sb("uh", 108, [P, 4, NB], F32R)
    ul = sb("ul", 116, [P, 4, NB], F32R)
    dft_raw = sb("dft_raw", 124, [P, 2, NB])
    dft_hi = sb("dft_hi", 128, [P, 2, NB], F32R)
    dft_lo = sb("dft_lo", 132, [P, 2, NB], F32R)
    wif_h = sb("wif_h", 136, [P, KD, N_GATE], F32R)
    wif_l = sb("wif_l", 137, [P, KD, N_GATE], F32R)
    junk = sb("junk", 108, [P, D])
    xin = sb("xin", 140, [P, NT, D])
    vh = sb("vh", 140, [P, NT, 2, NB], F32R)
    vl = sb("vl", 156, [P, NT, 2, NB], F32R)
    uf = sb("uf", 172, [P, KM, NB])
    q_t = sb("q_t", 108, [P, 4, NB])
    k_t = sb("k_t", 116, [P, 4, NB])
    o_t = sb("o_t", 124, [P, 4, NB])
    v_aug = sb("v_aug", 132, [P, NT, 2, DH + 1])
    prob = sb("prob", 140.5, [P, 2, 10, P])
    hcomb = sb("hcomb", 150.5, [P, NT, DH])
    wgt = sb("wgt", 154.5, [P, 2, 2, NB])
    neg_m = sb("neg_m", 204, [64, NB])
    negm_h = sb("negm_h", 168.5, [64, NB], F32R)
    negm_l = sb("negm_l", 204, [64, NB], F32R)
    diag = sb("diag", 164.5, [P, 2, NB])
    a_col = sb("a_col", 9.75, [P, NT, 64])
    em_col = sb("em_col", 206, [P, NT, 64])
    sel_pair = sb("sel_pair", 162.5, [64, 4, P], F32R)
    r_g16 = sb("r_g16", 188, [N_GATE, NB])
    r_ones = sb("r_ones", 142.5, [64, NB])
    r_1 = sb("r_1", 144.5, [64, NB])
    r_2 = sb("r_2", 146.5, [64, NB])
    r_b = sb("r_b", 148.5, [64, NB])
    r_m = sb("r_m", 150.5, [64, NB])
    r_a = sb("r_a", 152.5, [64, NB])
    hm = sb("hm", 188, [P, KM, NB])
    merged = sb("merged", 108, [P, KD, NB])
    bh = sb("bh", 140, [P, KM, NB], F32R)
    bl = sb("bl", 156, [P, KM, NB], F32R)
    sig = sb("sig", 172, [P, 4, NB])
    x2 = sb("x2", 140, [P, NT, D])
    x2t = sb("x2t", 108, [P, KD, NB])
    gain = sb("gain", 76, [P, D])
    h2 = sb("h2", 44, [P, NT, D])
    logit = sb("logit", 5.75, [P, NT, E])
    work = sb("work", 88, [E, NB])
    picked = sb("picked", 90, [E, NB])
    place = sb("place", 86, [E, NB])
    e_ones = sb("e_ones", 3.75, [E, NB])
    top8 = sb("top8", 84, [E, 8])
    h2_parts = sb("h2_parts", 108, [P, NT, 2, D], BF16)
    h2_rest = sb("h2_rest", 92, [P, NT, D], BF16)
    aff = sb("aff", 204, [P, NT, E + 1])
    slot = sb("slot", 204.5, [P, NT, E + 1])
    gate = sb("gate", 205, [P, 1])
    stat = sb("stat", 205.25, [P, 48])
    ring_at = (172, 180, 188, 196, 28, 36)
    eraw = [sb(f"eraw{s}", kb, [P, D]) for s, kb in enumerate(ring_at)]
    elo = [sb(f"elo{s}", kb, [P, D], F32R) for s, kb in enumerate(ring_at)]
    ehi = sb("ehi", 44, [P, 3, D], F32R)
    act_s = sb("act_s", 74, [P, NB])
    onehot = sb("onehot", 84, [P, NT, P])
    onehot_b = sb("onehot_b", 86, [P, NT, CAP], BF16)
    h_f = sb("h_f", 72, [P, NB])
    xg = sb("xg", 76, [P, KD, P], F32R)
    ab = sb("ab", 68, [P, FE])
    hx = sb("hx", 88, [P, KF, P], F32R)
    onehot_t = sb("onehot_t", 1.75, [P, NB], F32R)
    scattered = sb("scattered", 5.75, [P, 2, NB])
    yh = sb("yh", 12, [P, D], F32R)
    yl = sb("yl", 20, [P, D], F32R)
    fgain = sb("fgain", 44, [P, D])
    junk_g = sb("junk_g", 60, [P, D])

    ps = ctx.enter_context(nc.psum_tensor("ps", [P, 8, NB], F32))

    ident = cst[:, C_ID:C_ID + P]
    pair_sum = cst[:, C_PAIR:C_PAIR + CAP]
    g1_col = small[:, 0:16]
    g2_col = small[:, 64:80]
    ss2_parts = small[:, 80:96]
    mh_col = small[:, 16:24]
    bif_col = small[0:N_GATE, 24:25]
    ss1 = small[:, 28:32]
    rs1 = small[:, 32:36]
    neg_half = small[:, 36:40]
    den = small[:, 40:48]
    ssh = small[:, 48:52]
    rsh = small[:, 52:56]
    junk_h = sb("junk_h", 171, [P, DH])
    eps4 = small[:, 56:60]
    junk_f = sb("junk_f", 3.75, [P, NB])

    def row_chunk(w, k, col, g):
        width = (w.shape[1] - col) // NB * NB
        block = w[k * P:(k + 2) * P, col:col + width].rearrange("(k p) (g n) -> p g k n", p=P, n=NB)
        return block[:, ds(g, 1)].rearrange("p g k n -> p (g k) n")

    A_N, C_N, D_N, E_N = 12, 32, 12, 16
    A_IT, C_IT, D_IT, E_IT = 2, 2, 4, 2
    A0 = 0
    C0 = A0 + A_N * A_IT
    D0 = C0 + C_N * C_IT
    D2 = D0 + D_N * D_IT
    E0 = D2 + D_N * D_IT
    DENSE = E0 + E_N * E_IT

    ident_in, tables_in, vectors_in = sem("ident_in"), sem("tables_in"), sem("vectors_in")
    dft_in = sem("dft_in")
    x_in = [sem(f"x_in{t}") for t in range(NT)]
    raw_in = [sem(f"raw_in{s}") for s in range(DENSE_RING)]
    hi_ready, lo_ready, chunk_used = sem("hi_ready"), sem("lo_ready"), sem("chunk_used")
    neg_half_set, ss1_ready, rs1_mid = sem("neg_half_set"), sem("ss1_ready"), sem("rs1_mid")
    rs1_ready, x_scaled, xt_mm, xh_ready = sem("rs1_ready"), sem("x_scaled"), sem("xt_mm"), sem("xh_ready")
    xl_ready, dft_hi_ready, dft_lo_ready = sem("xl_ready"), sem("dft_hi_ready"), sem("dft_lo_ready")
    uh_ready, ul_ready, v_mm, vh_ready = sem("uh_ready"), sem("ul_ready"), sem("v_mm"), sem("vh_ready")
    vl_ready, uf_act, uf_dve = sem("vl_ready"), sem("uf_act"), sem("uf_dve")
    gates_mm, g16_ready, gsel_mm = sem("gates_mm"), sem("g16_ready"), sem("gsel_mm")
    rows_dve, rows_act, rows_t = sem("rows_dve"), sem("rows_act"), sem("rows_t")
    cols_ready, wif_hi_ready, wif_lo_ready = sem("cols_ready"), sem("wif_hi_ready"), sem("wif_lo_ready")
    mh_scaled, negm_hi_ready, negm_lo_ready = sem("mh_scaled"), sem("negm_hi_ready"), sem("negm_lo_ready")
    kq_act, kq_dve, v_act, v_dve = sem("kq_act"), sem("kq_dve"), sem("v_act"), sem("v_dve")
    o_tanh, sel_ready, ones_ready = sem("o_tanh"), sem("sel_ready"), sem("ones_ready")
    decay_mm, diag_ready, wgt_ready = sem("decay_mm"), sem("diag_ready"), sem("wgt_ready")
    scores_mm, prob_ready, head_mm = sem("scores_mm"), sem("prob_ready"), sem("head_mm")
    head_ready, head_chain, head_ss_ready = sem("head_ready"), sem("head_chain"), sem("head_ss_ready")
    head_rs_mid, head_rs_ready, head_normed = sem("head_rs_mid"), sem("head_rs_ready"), sem("head_normed")
    head_t_mm, head_t_out, hm_ready = sem("head_t_mm"), sem("head_t_out"), sem("hm_ready")
    bh_ready, bl_ready, sig_tanh = sem("bh_ready"), sem("bl_ready"), sem("sig_tanh")
    gated_ready, merged_ready = sem("gated_ready"), sem("merged_ready")
    merged_hi_ready, merged_lo_ready = sem("merged_hi_ready"), sem("merged_lo_ready")
    x2_in, x2_ready, gain_in, router_in = sem("x2_in"), sem("x2_ready"), sem("gain_in"), sem("router_in")
    router_scaled, x2t_mm, x2t_act = sem("router_scaled"), sem("x2t_mm"), sem("x2t_act")
    x2t_dve, logit_mm, logit_added = sem("x2t_dve"), sem("logit_mm"), sem("logit_added")
    sq2_ready, ss2_ready, rs2_mid = sem("sq2_ready"), sem("ss2_ready"), sem("rs2_mid")
    rs2_ready, h2_ready, part1_ready = sem("rs2_ready"), sem("h2_ready"), sem("part1_ready")
    rem1_ready, part2_ready, rest_ready = sem("rem1_ready"), sem("part2_ready"), sem("rest_ready")
    rest_pool_ready, logit_scaled = sem("rest_pool_ready"), sem("logit_scaled")
    negmax_ready, expl_ready, aff_ready = sem("negmax_ready"), sem("expl_ready"), sem("aff_ready")
    aff_t_mm, topk_chain, slot_mm = sem("aff_t_mm"), sem("topk_chain"), sem("slot_mm")
    slot_ready = sem("slot_ready")
    eraw_in = [sem(f"eraw_in{s}") for s in range(len(eraw))]
    ehi_ready, elo_ready, echunk_used = sem("ehi_ready"), sem("elo_ready"), sem("echunk_used")
    onehot_b_ready, scatter_out, onehot_ready = sem("onehot_b_ready"), sem("scatter_out"), sem("onehot_ready")
    gather_mm, xgh_ready, xgl_ready = sem("gather_mm"), sem("xgh_ready"), sem("xgl_ready")
    gate_g_mm, gate_ready, onehot_t_mm = sem("gate_g_mm"), sem("gate_ready"), sem("onehot_t_mm")
    onehot_t_ready, a_out, a_t_mm, a_tanh = sem("onehot_t_ready"), sem("a_out"), sem("a_t_mm"), sem("a_tanh")
    silu_ready, b_out, b_t_mm, h_ready = sem("silu_ready"), sem("b_out"), sem("b_t_mm"), sem("h_ready")
    hh_ready, hl_ready, yh_ready = sem("hh_ready"), sem("hl_ready"), sem("yh_ready")
    yl_ready, scatter_mm, acc_ready = sem("yl_ready"), sem("scatter_mm"), sem("acc_ready")
    final_gain_in, ss3_ready, rs3_mid = sem("final_gain_in"), sem("ss3_ready"), sem("rs3_mid")
    rs3_ready, fin_ready, out_written = sem("rs3_ready"), sem("fin_ready"), sem("out_written")
    block = ctx.enter_context(nc.Block())

    E_CH = 24
    RING, E_HI = len(eraw), 3

    @block.sync
    def _(sp):
        def load(n0, per, i, j, src, slots=1):
            n = n0 + j
            if n >= 4 and slots:
                sp.wait_ge(chunk_used, i * per + (n - 4 + slots))
            sp.dma_start(raw[:, n % 4], src).then_inc(raw_in[n % 4], 16)

        sp.dma_start(cst[:, 0:C_MASK], consts[:, 0:C_MASK]).then_inc(ident_in, 16)
        sp.wait_ge(x_in[1], 16)
        for j in range(4):
            load(A0, 0, 0, j, row_chunk(w_in, 2 * j, COL_U, 0))
        sp.dma_start(cst[:, C_MASK:C_END], consts[:, C_MASK:C_END]).then_inc(tables_in, 16)
        for i in range(A_IT):
            for j in range(4 if i == 0 else 0, 8):
                load(A0 + i * A_N, 0, 0, j, row_chunk(w_in, 2 * j, COL_U, i))
            for t in range(NT):
                load(A0 + i * A_N, 0, 0, 8 + t,
                     dft_token[t * P:(t + 1) * P, :].rearrange("p (k n) -> p k n", k=2))
        with sp.Fori(1, C_IT + 1) as turn:
            i = turn - 1
            for g, col in enumerate((COL_K, COL_Q, COL_V, COL_O)):
                for j in range(8):
                    load(C0, C_N, i, 8 * g + j, row_chunk(w_in, 2 * j, col, i),
                         slots=2 if (g, j) == (0, 7) else 0 if (g, j) == (1, 0) else 1)
        for base, col, w in ((D0, COL_GB, w_b), (D2, COL_GA, w_a)):
            with sp.Fori(1, D_IT + 1) as turn:
                i = turn - 1
                for j in range(8):
                    load(base, D_N, i, j, row_chunk(w_in, 2 * j, col, i), slots=2 if j == 7 else 1)
                for j in range(4):
                    load(base, D_N, i, 8 + j, row_chunk(w, 2 * j, 0, i), slots=0 if j == 0 else 1)
        with sp.Fori(1, E_IT + 1) as turn:
            i = turn - 1
            for g in range(2):
                for j in range(8):
                    load(E0, E_N, i, 8 * g + j, row_chunk(w_out, 2 * j, 0, i * 2 + g))
        def load_expert(n, c, used=True):
            if used:
                sp.wait_ge(echunk_used, n * E_CH + (c - RING + 1))
            if c < 16:
                w = w1 if c < 8 else w3
                k = 2 * (c % 8)
                src = w[ds(n, 1), k * P:(k + 2) * P, :].rearrange("e (k p) n -> p (e k) n", p=P)
                dst = eraw[c % RING].rearrange("p (k n) -> p k n", k=2)
            else:
                k = c - 16
                src = w2[ds(n, 1), k * P:(k + 1) * P, :].rearrange("e p n -> p (e n)")
                dst = eraw[c % RING][:]
            sp.dma_start(dst, src).then_inc(eraw_in[c % RING], 16)

        for c in range(E_CH):
            if c == 0:
                sp.wait_ge(merged_ready, 2 * D_IT)
            if c == 4:
                sp.wait_ge(chunk_used, DENSE)
            load_expert(0, c, used=c >= RING)
        with sp.Fori(2, E + 1) as turn:
            for c in range(E_CH):
                load_expert(turn - 1, c)
        for t in range(NT):
            for half in range(2):
                sp.wait_ge(fin_ready, 2 * t + half + 1)
                cols = slice(half * (D // 2), (half + 1) * (D // 2))
                sp.dma_start(out[t * P:(t + 1) * P, cols], x2[:, t, cols]).then_inc(out_written, 16)
        sp.wait_ge(out_written, 16 * NT * 2)

    @block.scalar
    def _(act):
        copy = ACT.Copy

        def split_hi(n0, per, i, j):
            n = n0 + j
            act.wait_ge(raw_in[n % DENSE_RING], i * (per // DENSE_RING * 16) + 16 * (n // DENSE_RING + 1))
            if n >= DENSE_RING:
                act.wait_ge(chunk_used, i * per + (n - DENSE_RING + 1))
            act.activation(hi[:, n % DENSE_RING], raw[:, n % DENSE_RING], copy).then_inc(hi_ready, 1)

        for t in range(NT):
            act.dma_start(xin[:, t], x[t * P:(t + 1) * P, :]).then_inc(x_in[t], 16)
        act.dma_start(g1_col, norm1_g.rearrange("o (k p) -> p (o k)", p=P)).then_inc(vectors_in, 16)
        act.dma_start(g2_col, norm2_g.rearrange("o (k p) -> p (o k)", p=P)).then_inc(vectors_in, 16)
        act.dma_start(mh_col, mh_g.rearrange("o (k p) -> p (o k)", p=P)).then_inc(vectors_in, 16)
        act.dma_start(bif_col, b_if.rearrange("o a (h c) -> (o a h) c", c=1)).then_inc(vectors_in, 16)
        act.dma_start(wif[:], w_in[:, COL_IF:COL_IF + N_GATE].rearrange("(k p) n -> p k n",
                                                                        p=P)).then_inc(vectors_in, 16)
        act.dma_start(dft_raw[:], dft_channel.rearrange("(k p) n -> p k n", p=P)).then_inc(dft_in, 16)
        for t in range(NT):
            act.wait_ge(x_in[t], 16)
            if t:
                act.wait_ge(ss1_ready, t)
            act.activation(junk[:], xin[:, t], ACT.Square, accum_out=ss1[:, t:t + 1]).then_inc(ss1_ready, 1)
        act.wait_ge(vectors_in, 16 * 5)
        for k in range(KD):
            act.wait_ge(xt_mm, k + 1)
            act.activation(xh[:, k], ps[:, k % 8], copy, scale=g1_col[:, k:k + 1]).then_inc(xh_ready, 1)
            if k >= KD - DENSE_AHEAD - 1 and k < KD - 1:
                split_hi(A0, 0, 0, k - (KD - DENSE_AHEAD - 1))
        act.wait_ge(dft_in, 16)
        act.wait_ge(ss1_ready, NT)
        act.activation(dft_hi[:], dft_raw[:], copy).then_inc(dft_hi_ready, 1)
        act.activation(wif_h[:], wif[:], copy).then_inc(wif_hi_ready, 1)
        for i in range(A_IT):
            for j in range(A_N):
                split_hi(A0 + i * A_N, 0, 0, j + DENSE_AHEAD)
                if i == 1 and j == 3:
                    act.wait_ge(gsel_mm, 1)
                    act.activation(r_1[:], ps[0:64, 6], ACT.Abs).then_inc(rows_act, 1)
                    act.wait_ge(rows_act, 1)
                    act.activation(r_2[:], r_1[:], ACT.Exp, scale=-1.0).then_inc(rows_act, 1)
                    act.wait_ge(rows_act, 2)
                    act.activation(r_1[:], r_2[:], ACT.Ln, bias=1.0).then_inc(rows_act, 1)
                if j == 7:
                    act.wait_ge(chunk_used, A0 + i * A_N + 8)
                    for m in range(4):
                        act.activation(uh[:, m], ps[:, m], copy).then_inc(uh_ready, 1)
                    if i == 0:
                        act.wait_ge(gates_mm, 1)
                        act.activation(r_g16[:], ps[0:N_GATE, 7], ACT.Identity, bias=bif_col).then_inc(g16_ready, 1)
                    else:
                        act.wait_ge(rows_t, 1)
                        act.activation(a_col[:], ps[:, 7, 0:256].rearrange("p (t c) -> p t c", t=NT),
                                       copy).then_inc(cols_ready, 1)
                        act.activation(em_col[:], ps[:, 7, 256:512].rearrange("p (t c) -> p t c", t=NT), ACT.Exp,
                                       scale=-1.0).then_inc(cols_ready, 1)
                    for b in range(8):
                        act.wait_ge(v_mm, 8 * i + b + 1)
                        act.activation(vh[:, b % 4, b // 4], ps[:, (4 * (1 - i) + b) % 8], copy).then_inc(vh_ready, 1)
                if j == 11:
                    act.wait_ge(chunk_used, A0 + (i + 1) * A_N)
                    for m in range(2):
                        act.activation(uf[:, 4 * i + m], ps[:, 4 * (1 - i) + m], copy).then_inc(uf_act, 1)
        act.wait_ge(chunk_used, C0)
        act.activation(negm_h[:], neg_m[:], copy).then_inc(negm_hi_ready, 1)

        def decay_weights(i, hh, ss):
            act.wait_ge(diag_ready, i * 4 + (2 * hh + 2))
            for s in ss:
                if s >= 2:
                    act.wait_ge(prob_ready, i * 16 + (8 * hh + 2 * s - 2))
                elif hh:
                    act.wait_ge(prob_ready, i * 16 + 8)
                for d in range(2):
                    bias = a_col[:, s, ds(i * 2 + (hh + 32 * d), 1)]
                    act.activation(wgt[:, d, s % 2, s * P:(s + 1) * P], diag[:, d, s * P:(s + 1) * P],
                                   ACT.Exp, bias=bias).then_inc(wgt_ready, 1)
                    rest = slice((s + 1) * P, NB) if d == 0 else slice(0, s * P)
                    if rest.stop > rest.start:
                        act.activation(wgt[:, d, s % 2, rest], ps[:, d, rest],
                                       ACT.Exp, bias=bias).then_inc(wgt_ready, 1)

        def head_squares(i, hh, ts):
            for t in ts:
                act.wait_ge(head_ready, i * 8 + (4 * hh + t + 1))
                if t or hh:
                    act.wait_ge(head_ss_ready, i * 8 + (4 * hh + t))
                act.activation(junk_h[:], hcomb[:, t], ACT.Square, scale=DH ** -0.5,
                               accum_out=ssh[:, t:t + 1]).then_inc(head_ss_ready, 1)

        with act.Fori(0, C_IT) as i:
            for j in range(C_N):
                split_hi(C0, C_N, i, j + DENSE_AHEAD)
                if j == 7:
                    act.wait_ge(chunk_used, i * C_N + (C0 + 8))
                    for m in range(2):
                        act.activation(k_t[:, m], ps[:, 4 + m], copy).then_inc(kq_act, 1)
                if j == 15:
                    act.wait_ge(chunk_used, i * C_N + (C0 + 16))
                    for m in range(2):
                        act.activation(q_t[:, m], ps[:, m], copy).then_inc(kq_act, 1)
                if j in (17, 18):
                    decay_weights(i, 0, (0, 1) if j == 17 else (2, 3))
                if j == 23:
                    act.wait_ge(chunk_used, i * C_N + (C0 + 24))
                    for t in range(2):
                        act.activation(v_aug[:, t, :, 0:DH], ps[:, 4 + t].rearrange("p (h d) -> p h d", h=2),
                                       copy).then_inc(v_act, 1)
                if j in (24, 25):
                    head_squares(i, 0, (0, 1) if j == 24 else (2, 3))
                if j in (27, 28):
                    decay_weights(i, 1, (0, 1) if j == 27 else (2, 3))
                if j in (29, 30):
                    head_squares(i, 1, (0, 1) if j == 29 else (2, 3))
                if j == 31:
                    act.wait_ge(chunk_used, i * C_N + (C0 + 32))
                    for m in range(4):
                        act.activation(o_t[:, m], ps[:, 4 + m], ACT.Tanh, scale=0.5).then_inc(o_tanh, 1)
        for half, base in ((0, D0), (1, D2)):
            src = hm if half else uf
            if half:
                act.wait_ge(chunk_used, D2)
            else:
                act.wait_ge(mh_scaled, 1)
                act.wait_ge(hm_ready, 4 * C_IT)
                act.wait_ge(head_t_mm, 2 * C_IT)
            for k in range(KM):
                act.activation(bh[:, k], src[:, k], copy,
                               scale=mh_col[:, k:k + 1] if half else 0.5).then_inc(bh_ready, 1)
            if not half:
                act.wait_ge(bl_ready, KM)

            def gated_group(i, first=False, last=False):
                for j in range(D_N):
                    split_hi(base, D_N, i, j + DENSE_AHEAD)
                    if j == 7:
                        act.wait_ge(chunk_used, i * D_N + (base + 8))
                        if not first:
                            act.wait_ge(merged_ready, i + D_IT * half)
                        for m in range(4):
                            act.activation(sig[:, m], ps[:, m], ACT.Tanh, scale=0.5).then_inc(sig_tanh, 1)
                    if j >= 8 and last:
                        for k in range(3 * (j - 8), 3 * (j - 7)):
                            act.activation(xh[:, k], merged[:, k], copy).then_inc(merged_hi_ready, 1)

            if half == 0:
                gated_group(0, first=True)
                with act.Fori(1, D_IT) as i:
                    gated_group(i)
            else:
                with act.Fori(0, D_IT - 1) as i:
                    gated_group(i)
                gated_group(D_IT - 1, last=True)
        act.wait_ge(merged_ready, 2 * D_IT)
        for k in range(12, KD):
            act.activation(xh[:, k], merged[:, k], copy).then_inc(merged_hi_ready, 1)
        act.wait_ge(chunk_used, E0)
        for t in range(NT):
            act.dma_start(x2[:, t], x[t * P:(t + 1) * P, :]).then_inc(x2_in, 16)
        act.dma_start(wif[:], w_router.rearrange("(k p) n -> p k n", p=P)).then_inc(router_in, 16)

        def squares(g):
            act.wait_ge(x2_ready, 4 * g + 4)
            for t in range(NT):
                n = 4 * g + t
                if n:
                    act.wait_ge(sq2_ready, n)
                act.activation(junk_f[:], x2[:, t, g * NB:(g + 1) * NB], ACT.Square,
                               accum_out=ss2_parts[:, n:n + 1]).then_inc(sq2_ready, 1)

        def transposed_act(g):
            for c in range(2):
                act.wait_ge(x2t_mm, 4 * g + c + 1)
                act.activation(x2t[:, 4 * g + c], ps[:, 4 * (g % 2) + c], copy).then_inc(x2t_act, 1)

        for g in range(4):
            for j in range(8):
                if 8 * g + j < 4 * 8 - DENSE_AHEAD:
                    split_hi(E0, 0, 0, 8 * g + j + DENSE_AHEAD)
                if g and j == 1:
                    squares(g - 1)
                if g and j == 3:
                    transposed_act(g - 1)
        act.wait_ge(chunk_used, DENSE)
        act.dma_start(gain[:], norm2_g[0:1, :].partition_broadcast(P)).then_inc(gain_in, 16)
        squares(3)
        transposed_act(3)
        for t in range(NT):
            act.wait_ge(negmax_ready, 1)
            act.activation(logit[:, t], logit[:, t], ACT.Exp, bias=stat[:, 8 + t:9 + t],
                           accum_out=stat[:, 12 + t:13 + t]).then_inc(expl_ready, 1)
        act.wait_ge(logit_mm, 4)
        for t in range(NT):
            act.wait_ge(h2_ready, t + 1)
            act.activation(h2_parts[:, t, 0], h2[:, t], copy).then_inc(part1_ready, 1)
        for t in range(NT):
            act.wait_ge(rem1_ready, t + 1)
            act.activation(h2_parts[:, t, 1], h2[:, t], copy).then_inc(part2_ready, 1)

        def split_ehi(n, c, first=False):
            act.wait_ge(eraw_in[c % RING], n * (E_CH // RING * 16) + 16 * (c // RING + 1))
            if not first:
                act.wait_ge(echunk_used, n * E_CH + (c - E_HI + 1))
            act.activation(ehi[:, c % E_HI], eraw[c % RING][:], copy).then_inc(ehi_ready, 1)

        def gathered_hi(n, half):
            act.wait_ge(gather_mm, 2 * n + (half + 1))
            act.activation(xg[:, 8 * half:8 * half + 8, 0:CAP], ps[:, half].rearrange("p (k n) -> p k n", k=8),
                           copy).then_inc(xgh_ready, 1)

        def onehot_bf16(n):
            act.wait_ge(onehot_ready, n + 1)
            act.activation(onehot_b[:], onehot[:, :, 0:CAP], copy).then_inc(onehot_b_ready, 1)

        onehot_bf16(0)
        act.wait_ge(rest_ready, 2)
        act.wait_ge(rest_pool_ready, 2)
        for c in range(E_HI):
            split_ehi(0, c, True)
        gathered_hi(0, 0)
        gathered_hi(0, 1)

        def expert(n, last):
            for c in range(E_CH):
                if c and not (last and c > E_CH - E_HI):
                    split_ehi(n, c + E_HI - 1)
                if 2 <= c <= 9:
                    for blk in (2 * c - 4, 2 * c - 3):
                        act.wait_ge(scatter_mm, n * 16 + (blk + 1))
                        act.wait_ge(acc_ready, n * 16 + (blk - 1 + 2))
                        act.activation(scattered[:, blk % 2], ps[:, 4 + blk % 4], copy).then_inc(scatter_out, 1)
                if c == 7:
                    act.wait_ge(echunk_used, n * E_CH + 8)
                    for b in range(2):
                        act.activation(ab[:, b * NB:(b + 1) * NB], ps[:, b], copy).then_inc(a_out, 1)
                if c == 9:
                    act.wait_ge(a_t_mm, n + 1)
                    act.activation(act_s[:], ps[:, 0], ACT.Tanh, scale=0.5).then_inc(a_tanh, 1)
                if c == 10:
                    act.wait_ge(onehot_t_mm, n + 1)
                    act.activation(onehot_t[:], ps[:, 1], copy).then_inc(onehot_t_ready, 1)
                if c == 12:
                    onehot_bf16(n + 1)
                if c == 15:
                    act.wait_ge(echunk_used, n * E_CH + 16)
                    for b in range(2):
                        act.activation(ab[:, b * NB:(b + 1) * NB], ps[:, 2 + b], copy).then_inc(b_out, 1)
                    act.wait_ge(h_ready, n + 1)
                    act.activation(hx[:, :, 0:CAP], h_f[:].rearrange("p (k n) -> p k n", k=KF),
                                   copy).then_inc(hh_ready, 1)
                if c == 19:
                    gathered_hi(n + 1, 0)
                if c == 22:
                    gathered_hi(n + 1, 1)
                if c == 23:
                    act.wait_ge(echunk_used, n * E_CH + E_CH)
                    act.wait_ge(gate_ready, n + 1)
                    for b in range(4):
                        act.activation(yh[:, b * NB:(b + 1) * NB], ps[:, 4 + b], copy,
                                       scale=gate[:, 0:1]).then_inc(yh_ready, 1)

        with act.Fori(0, E - 1) as n:
            expert(n, False)
            split_ehi(n + 1, E_HI - 1)
        expert(E - 1, True)
        act.wait_ge(echunk_used, E * E_CH)
        act.dma_start(fgain[:],
                      final_g.rearrange("(o n) -> o n", o=1).partition_broadcast(P)).then_inc(final_gain_in, 16)
        for t in range(NT):
            act.wait_ge(acc_ready, 16 * E + 2 + 4 * (t + 1))
            if t:
                act.wait_ge(ss3_ready, t)
            act.activation(junk_g[:], x2[:, t], ACT.Square, accum_out=stat[:, t:t + 1]).then_inc(ss3_ready, 1)

    @block.gpsimd
    def _(pool):
        pool.memset(neg_half, -0.5).then_inc(neg_half_set, 1)
        pool.memset(eps4, EPS).then_inc(neg_half_set, 1)
        for t in range(NT):
            pool.wait_ge(ss1_ready, t + 1)
            if t == 0:
                pool.wait_ge(neg_half_set, 2)
            pool.tensor_scalar(rs1[:, t:t + 1], ss1[:, t:t + 1], 1.0 / D, EPS, ALU.mult, ALU.add).then_inc(rs1_mid, 1)
            pool.wait_ge(rs1_mid, t + 1)
            pool.tensor_tensor(rs1[:, t:t + 1], rs1[:, t:t + 1], neg_half[:, 0:1], ALU.pow).then_inc(rs1_ready, 1)
        pool.wait_ge(dft_lo_ready, 1)
        pool.wait_ge(ul_ready, 4 * A_IT)
        pool.wait_ge(chunk_used, C0)
        pool.memset(v_aug[:, :, :, DH:DH + 1], 1.0).then_inc(ones_ready, 1)
        with pool.Fori(0, C_IT) as i:
            for hh in range(2):
                pool.wait_ge(head_ss_ready, i * 8 + 4 * hh + 4)
                pool.tensor_tensor(rsh, ssh, eps4, ALU.add).then_inc(head_rs_mid, 1)
                pool.wait_ge(head_rs_mid, i * 2 + (hh + 1))
                pool.tensor_tensor(rsh, rsh, neg_half, ALU.pow).then_inc(head_rs_ready, 1)
        pool.wait_ge(ss2_ready, 1)
        pool.tensor_scalar(stat[:, 4:8], stat[:, 0:4], 1.0 / D, EPS, ALU.mult, ALU.add).then_inc(rs2_mid, 1)
        pool.wait_ge(rs2_mid, 1)
        pool.tensor_tensor(stat[:, 4:8], stat[:, 4:8], neg_half, ALU.pow).then_inc(rs2_ready, 1)
        pool.wait_ge(chunk_used, DENSE)
        pool.memset(yh[:].bitcast(F32), 0.0).then_inc(yh_ready, 4)
        pool.memset(yl[:].bitcast(F32), 0.0).then_inc(yl_ready, 4)
        pool.memset(onehot_t[:].bitcast(F32), 0.0).then_inc(onehot_t_ready, 1)
        for t in range(NT):
            pool.wait_ge(part1_ready, t + 1)
            pool.tensor_tensor(h2[:, t], h2[:, t], h2_parts[:, t, 0], ALU.subtract).then_inc(rem1_ready, 1)
        for t in range(2, NT):
            pool.wait_ge(part2_ready, t + 1)
            pool.tensor_tensor(h2_rest[:, t], h2[:, t], h2_parts[:, t, 1], ALU.subtract).then_inc(rest_pool_ready, 1)
        pool.wait_ge(x2_ready, 16)
        pool.wait_ge(aff_ready, NT)
        pool.memset(scattered[:], 0.0).then_inc(acc_ready, 2)
        with pool.Fori(0, E) as n:
            for blk in range(16):
                t, b = blk // 4, blk % 4
                pool.wait_ge(scatter_out, n * 16 + (blk + 1))
                dst = x2[:, t, b * NB:(b + 1) * NB]
                pool.tensor_tensor(dst, dst, scattered[:, blk % 2], ALU.add).then_inc(acc_ready, 1)
        for t in range(NT):
            pool.wait_ge(ss3_ready, t + 1)
            pool.tensor_scalar(stat[:, 4 + t:5 + t], stat[:, t:t + 1], 1.0 / D, EPS, ALU.mult,
                               ALU.add).then_inc(rs3_mid, 1)
            pool.wait_ge(rs3_mid, t + 1)
            pool.tensor_tensor(stat[:, 4 + t:5 + t], stat[:, 4 + t:5 + t], neg_half[:, 0:1],
                               ALU.pow).then_inc(rs3_ready, 1)

    @block.vector
    def _(dve):
        def split_lo(n0, per, i, j):
            n = n0 + j
            dve.wait_ge(hi_ready, i * per + (n + 1))
            at = n % DENSE_RING
            dve.tensor_tensor(lo[:, at], raw[:, at], hi[:, at].bitcast(F32),
                              ALU.subtract).then_inc(lo_ready, 1)

        for t in range(NT):
            dve.wait_ge(rs1_ready, t + 1)
            dve.tensor_scalar(xin[:, t], xin[:, t], rs1[:, t:t + 1], None, ALU.mult).then_inc(x_scaled, 1)
        for k in range(KD):
            dve.wait_ge(xh_ready, k + 1)
            dve.scalar_tensor_tensor(xl[:, k], ps[:, k % 8], g1_col[:, k:k + 1], xh[:, k].bitcast(F32),
                                     ALU.mult, ALU.subtract).then_inc(xl_ready, 1)
            if k >= KD - DENSE_AHEAD - 1 and k < KD - 1:
                split_lo(A0, 0, 0, k - (KD - DENSE_AHEAD - 1))
        dve.wait_ge(dft_hi_ready, 1)
        dve.tensor_tensor(dft_lo[:], dft_raw[:], dft_hi[:].bitcast(F32), ALU.subtract).then_inc(dft_lo_ready, 1)
        dve.wait_ge(wif_hi_ready, 1)
        dve.tensor_tensor(wif_l[:], wif[:], wif_h[:].bitcast(F32), ALU.subtract).then_inc(wif_lo_ready, 1)
        dve.tensor_scalar(mh_col, mh_col, 0.25, None, ALU.mult).then_inc(mh_scaled, 1)
        def log_gates():
            dve.wait_ge(gates_mm, 1)
            dve.memset(r_ones[:], 1.0).then_inc(rows_dve, 1)
            dve.memset(r_b[:], 0.0).then_inc(rows_dve, 1)
            dve.wait_ge(gsel_mm, 1)
            dve.wait_ge(rows_act, 3)
            dve.scalar_tensor_tensor(r_2[:], ps[0:64, 6], 0.0, r_1[:], ALU.min, ALU.subtract).then_inc(rows_dve, 1)
            dve.wait_ge(rows_dve, 3)
            dve.tensor_tensor_scan(r_b[0:4], r_ones[0:4], r_2[0:4], 0.0, ALU.mult, ALU.add).then_inc(rows_dve, 1)
            dve.tensor_tensor_scan(r_b[32:36, ::-1], r_ones[32:36, ::-1], r_2[32:36, ::-1], 0.0,
                                   ALU.mult, ALU.add).then_inc(rows_dve, 1)
            dve.wait_ge(rows_dve, 5)
            dve.tensor_tensor(r_a[:], ps[0:64, 5], r_b[:], ALU.subtract).then_inc(rows_dve, 1)
            dve.memset(r_m[:], 0.0).then_inc(rows_dve, 1)
            dve.wait_ge(rows_dve, 7)
            dve.tensor_tensor_scan(r_m[0:4], r_ones[0:4], r_a[0:4], 0.0, ALU.mult, ALU.max).then_inc(rows_dve, 1)
            dve.tensor_tensor_scan(r_m[32:36, ::-1], r_ones[32:36, ::-1], r_a[32:36, ::-1], 0.0,
                                   ALU.mult, ALU.max).then_inc(rows_dve, 1)
            dve.wait_ge(rows_dve, 9)
            dve.tensor_scalar(neg_m[:], r_m[:], -1.0, None, ALU.mult).then_inc(rows_dve, 1)
            dve.tensor_tensor(r_b[:], r_b[:], r_m[:], ALU.add).then_inc(rows_dve, 1)

        for i in range(A_IT):
            for j in range(A_N):
                split_lo(A0 + i * A_N, 0, 0, j + DENSE_AHEAD)
                if i == 1 and j == 3:
                    log_gates()
                if j == 7:
                    for m in range(4):
                        dve.wait_ge(uh_ready, 4 * i + m + 1)
                        dve.tensor_tensor(ul[:, m], ps[:, m], uh[:, m].bitcast(F32),
                                          ALU.subtract).then_inc(ul_ready, 1)
                    for b in range(8):
                        dve.wait_ge(vh_ready, 8 * i + b + 1)
                        dve.tensor_tensor(vl[:, b % 4, b // 4], ps[:, (4 * (1 - i) + b) % 8],
                                          vh[:, b % 4, b // 4].bitcast(F32), ALU.subtract).then_inc(vl_ready, 1)
                if j == 11:
                    dve.wait_ge(chunk_used, A0 + (i + 1) * A_N)
                    for m in range(2, 4):
                        dve.tensor_copy(uf[:, 4 * i + m], ps[:, 4 * (1 - i) + m]).then_inc(uf_dve, 1)
        dve.wait_ge(negm_hi_ready, 1)
        dve.tensor_tensor(negm_l[:], neg_m[:], negm_h[:].bitcast(F32), ALU.subtract).then_inc(negm_lo_ready, 1)
        dve.wait_ge(tables_in, 16)

        def mask_diagonal(i, hh):
            for d in range(2):
                dve.wait_ge(decay_mm, i * 4 + (2 * hh + d + 1))
                dve.tensor_tensor(diag[:, d], ps[:, d], cst[:, C_MASK + d * NB:C_MASK + (d + 1) * NB],
                                  ALU.add).then_inc(diag_ready, 1)

        def probabilities(i, hh, ss):
            for s in ss:
                w_seen = (3, 7, 11, 14)[s]
                dve.wait_ge(scores_mm, i * 8 + (4 * hh + s + 1))
                dve.wait_ge(wgt_ready, i * 28 + (14 * hh + w_seen))
                f0 = s * NT - s * (s - 1) // 2
                dve.scalar_tensor_tensor(
                    prob[:, 0, f0:f0 + NT - s].rearrange("p a b -> p (a b)"),
                    ps[:, 2 + s % 2, s * P:NB], DH ** -0.5, wgt[:, 0, s % 2, s * P:NB],
                    ALU.mult, ALU.mult).then_inc(prob_ready, 1)
                b0 = s * (s + 1) // 2
                dve.scalar_tensor_tensor(
                    prob[:, 1, b0:b0 + s + 1].rearrange("p a b -> p (a b)"),
                    ps[:, 2 + s % 2, 0:(s + 1) * P], DH ** -0.5, wgt[:, 1, s % 2, 0:(s + 1) * P],
                    ALU.mult, ALU.mult).then_inc(prob_ready, 1)

        def head_out(i, hh, ts):
            for t in ts:
                b = 2 * (t % 2)
                dd = den[:, 4 * (t % 2):4 * (t % 2) + 2]
                rr = den[:, 4 * (t % 2) + 2:4 * (t % 2) + 4]
                dve.wait_ge(head_mm, i * 8 + (4 * hh + t + 1))
                em = em_col[:, t].rearrange("p (d c) -> p d c", d=2)[:, :, ds(i * 2 + hh, 1)]
                row_sum = ps[:, b:b + 2, DH:DH + 1]
                dd3 = dd.rearrange("p (d c) -> p d c", c=1)
                base = 16 * hh + 4 * t
                dve.scalar_tensor_tensor(dd3, row_sum, -1.0, em, ALU.mult, ALU.max).then_inc(head_chain, 1)
                dve.wait_ge(head_chain, i * 32 + (base + 1))
                dve.tensor_tensor(dd3, row_sum, dd3, ALU.max).then_inc(head_chain, 1)
                dve.wait_ge(head_chain, i * 32 + (base + 2))
                dve.reciprocal(rr, dd).then_inc(head_chain, 1)
                dve.wait_ge(head_chain, i * 32 + (base + 3))
                dve.tensor_scalar(hcomb[:, t], ps[:, b, 0:DH], rr[:, 0:1], None, ALU.mult).then_inc(head_chain, 1)
                dve.wait_ge(head_chain, i * 32 + (base + 4))
                dve.scalar_tensor_tensor(hcomb[:, t], ps[:, b + 1, 0:DH], rr[:, 1:2], hcomb[:, t],
                                         ALU.mult, ALU.add).then_inc(head_ready, 1)

        def head_norm(i, hh):
            dve.wait_ge(head_rs_ready, i * 2 + (hh + 1))
            for t in range(NT):
                dve.tensor_scalar(hcomb[:, t], hcomb[:, t], rsh[:, t:t + 1], None, ALU.mult).then_inc(head_normed, 1)
            dve.wait_ge(head_t_mm, i * 2 + (hh + 1))
            for c in range(2):
                dve.tensor_copy(hm[:, ds(i * 4 + (2 * hh + c), 1)].rearrange("p a b -> p (a b)"),
                                ps[:, c]).then_inc(head_t_out, 1)

        with dve.Fori(0, C_IT) as i:
            for j in range(C_N):
                split_lo(C0, C_N, i, j + DENSE_AHEAD)
                if j == 7:
                    dve.wait_ge(chunk_used, i * C_N + (C0 + 8))
                    for m in range(2, 4):
                        dve.tensor_copy(k_t[:, m], ps[:, 4 + m]).then_inc(kq_dve, 1)
                    dve.tensor_copy(sel_pair[:].rearrange("p a b -> p (a b)"),
                                    cst[0:64, ds(i * 4 * P + C_SELROW, 4 * P)]).then_inc(sel_ready, 1)
                if j == 15:
                    dve.wait_ge(chunk_used, i * C_N + (C0 + 16))
                    for m in range(2, 4):
                        dve.tensor_copy(q_t[:, m], ps[:, m]).then_inc(kq_dve, 1)
                if j == 17:
                    mask_diagonal(i, 0)
                    probabilities(i, 0, (0, 1))
                if j == 23:
                    dve.wait_ge(chunk_used, i * C_N + (C0 + 24))
                    for t in range(2, 4):
                        dve.tensor_copy(v_aug[:, t, :, 0:DH],
                                        ps[:, 4 + t].rearrange("p (h d) -> p h d", h=2)).then_inc(v_dve, 1)
                    probabilities(i, 0, (2, 3))
                if j in (24, 25):
                    head_out(i, 0, (0, 1) if j == 24 else (2, 3))
                if j == 26:
                    head_norm(i, 0)
                if j == 27:
                    mask_diagonal(i, 1)
                    probabilities(i, 1, (0, 1))
                if j == 28:
                    probabilities(i, 1, (2, 3))
                if j in (29, 30):
                    head_out(i, 1, (0, 1) if j == 29 else (2, 3))
                if j == 31:
                    head_norm(i, 1)
                    for m in range(4):
                        dve.wait_ge(o_tanh, i * 4 + (m + 1))
                        dve.wait_ge(head_t_out, i * 4 + (m + 1))
                        tile = hm[:, ds(i * 4 + m, 1)].rearrange("p a b -> p (a b)")
                        dve.scalar_tensor_tensor(tile, o_t[:, m], 1.0, tile, ALU.add, ALU.mult).then_inc(hm_ready, 1)
        def merged_lo(ks):
            for k in ks:
                dve.wait_ge(merged_hi_ready, k + 1)
                dve.tensor_tensor(xl[:, k], merged[:, k], xh[:, k].bitcast(F32),
                                  ALU.subtract).then_inc(merged_lo_ready, 1)

        for half, base in ((0, D0), (1, D2)):
            src = hm if half else uf
            dve.wait_ge(mh_scaled, 1)
            for k in range(KM):
                dve.wait_ge(bh_ready, KM * half + k + 1)
                dve.scalar_tensor_tensor(bl[:, k], src[:, k], mh_col[:, k:k + 1] if half else 0.5,
                                         bh[:, k].bitcast(F32), ALU.mult, ALU.subtract).then_inc(bl_ready, 1)

            def merge_group(i, last=False):
                for j in range(D_N):
                    split_lo(base, D_N, i, j + DENSE_AHEAD)
                    if j >= 8 and last:
                        merged_lo(range(3 * (j - 8), 3 * (j - 7)))
                    if j == 11:
                        dve.wait_ge(chunk_used, i * D_N + (base + D_N))
                        for m in range(4):
                            dve.wait_ge(sig_tanh, i * 4 + (4 * D_IT * half + m + 1))
                            dst = merged[:, ds(i * 4 + m, 1)].rearrange("p a b -> p (a b)")
                            if half == 0:
                                ins = dve.scalar_tensor_tensor(dst, sig[:, m], 1.0, ps[:, 4 + m], ALU.add, ALU.mult)
                            else:
                                dve.scalar_tensor_tensor(sig[:, m], sig[:, m], 1.0, ps[:, 4 + m], ALU.add,
                                                         ALU.mult).then_inc(gated_ready, 1)
                                dve.wait_ge(gated_ready, i * 4 + (m + 1))
                                ins = dve.tensor_tensor(dst, dst, sig[:, m], ALU.add)
                        ins.then_inc(merged_ready, 1)

            if half == 0:
                with dve.Fori(0, D_IT) as i:
                    merge_group(i)
            else:
                with dve.Fori(0, D_IT - 1) as i:
                    merge_group(i)
                merge_group(D_IT - 1, last=True)
        merged_lo(range(12, KD))

        def add_out(g):
            dve.wait_ge(chunk_used, E0 + 8 * (g + 1))
            if g == 0:
                dve.wait_ge(x2_in, 16 * NT)
            for t in range(NT):
                dst = x2[:, t, g * NB:(g + 1) * NB]
                dve.tensor_tensor(dst, dst, ps[:, 4 * (g % 2) + t], ALU.add).then_inc(x2_ready, 1)

        def transposed_dve(g):
            for c in range(2, 4):
                dve.wait_ge(x2t_mm, 4 * g + c + 1)
                dve.tensor_copy(x2t[:, 4 * g + c], ps[:, 4 * (g % 2) + c]).then_inc(x2t_dve, 1)

        def add_logits(g):
            dve.wait_ge(logit_mm, g + 1)
            part = ps[:, 4 * (g % 2), 0:NT * E].rearrange("p (t e) -> p t e", t=NT)
            if g == 0:
                dve.tensor_copy(logit[:], part).then_inc(logit_added, 1)
            else:
                dve.wait_ge(logit_added, g)
                dve.tensor_tensor(logit[:], logit[:], part, ALU.add).then_inc(logit_added, 1)

        for g in range(4):
            for j in range(8):
                if 8 * g + j < 4 * 8 - DENSE_AHEAD:
                    split_lo(E0, 0, 0, 8 * g + j + DENSE_AHEAD)
                if g and j == 3:
                    transposed_dve(g - 1)
                if g and j == 6:
                    add_logits(g - 1)
                if g == 0 and j == 7:
                    dve.wait_ge(router_in, 16)
                    dve.tensor_tensor(wif[:], wif[:], g2_col.unsqueeze(2).to_broadcast([P, KD, E]),
                                      ALU.mult).then_inc(router_scaled, 1)
                if j == 7:
                    add_out(g)
        dve.memset(aff[:], 0.0).then_inc(topk_chain, 1)
        dve.memset(slot[:], -1.0).then_inc(topk_chain, 1)
        dve.wait_ge(sq2_ready, 16)
        dve.memset(e_ones[:], 1.0).then_inc(topk_chain, 1)
        dve.tensor_reduce(stat[:, 0:4], ss2_parts.rearrange("p (g t) -> p t g", g=4), AXX,
                          ALU.add).then_inc(ss2_ready, 1)
        transposed_dve(3)

        def normed(t):
            dve.scalar_tensor_tensor(h2[:, t], x2[:, t], stat[:, 4 + t:5 + t], gain[:], ALU.mult,
                                     ALU.mult).then_inc(h2_ready, 1)

        dve.wait_ge(rs2_ready, 1)
        dve.wait_ge(gain_in, 16)
        normed(0)
        normed(1)
        add_logits(3)
        dve.wait_ge(logit_added, 4)
        dve.tensor_tensor(logit[:], logit[:], stat[:, 4:8].unsqueeze(2).to_broadcast([P, NT, E]),
                          ALU.mult).then_inc(logit_scaled, 1)
        dve.wait_ge(logit_scaled, 1)
        dve.tensor_reduce(stat[:, 8:12], logit[:], AXX, ALU.max, negate=True).then_inc(negmax_ready, 1)
        dve.wait_ge(expl_ready, NT)
        dve.reciprocal(stat[:, 16:20], stat[:, 12:16]).then_inc(topk_chain, 1)
        dve.wait_ge(topk_chain, 4)
        for t in range(NT):
            dve.tensor_scalar(aff[:, t, 0:E], logit[:, t], stat[:, 16 + t:17 + t], None,
                              ALU.mult).then_inc(aff_ready, 1)
        normed(2)
        dve.wait_ge(aff_t_mm, 1)
        dve.tensor_copy(work[:], ps[0:E, 5]).then_inc(topk_chain, 1)
        normed(3)
        n = 5
        for r in range(CAP // 8):
            dve.wait_ge(topk_chain, n)
            dve.max(top8[:], work[:]).then_inc(topk_chain, 1)
            dve.wait_ge(topk_chain, n + 1)
            dve.match_replace(work[:], top8[:], work[:], -1.0).then_inc(topk_chain, 1)
            n += 2
        dve.wait_ge(topk_chain, n)
        dve.tensor_scalar(picked[:], work[:], 0.0, None, ALU.is_lt).then_inc(topk_chain, 1)
        dve.wait_ge(topk_chain, n + 1)
        dve.tensor_tensor_scan(place[:], e_ones[:], picked[:], 0.0, ALU.mult, ALU.add).then_inc(topk_chain, 1)
        dve.wait_ge(topk_chain, n + 2)
        dve.tensor_tensor(place[:], place[:], picked[:], ALU.mult).then_inc(topk_chain, 1)
        dve.wait_ge(topk_chain, n + 3)
        dve.tensor_scalar(place[:], place[:], 1.0, None, ALU.subtract).then_inc(topk_chain, 1)
        def rest(t):
            dve.wait_ge(part2_ready, t + 1)
            dve.tensor_tensor(h2_rest[:, t], h2[:, t], h2_parts[:, t, 1], ALU.subtract).then_inc(rest_ready, 1)

        dve.wait_ge(slot_mm, 1)
        dve.tensor_copy(slot[:, :, 0:E], ps[:, 6, 0:NT * E].rearrange("p (t e) -> p t e", t=NT)).then_inc(slot_ready, 1)

        def split_elo(n, c):
            dve.wait_ge(ehi_ready, n * E_CH + (c + 1))
            dve.tensor_tensor(elo[c % RING][:], eraw[c % RING][:], ehi[:, c % E_HI].bitcast(F32),
                              ALU.subtract).then_inc(elo_ready, 1)

        def gathered_lo(n, half):
            dve.wait_ge(xgh_ready, 2 * n + (half + 1))
            dve.tensor_tensor(xg[:, 8 * half:8 * half + 8, CAP:2 * CAP],
                              ps[:, half].rearrange("p (k n) -> p k n", k=8),
                              xg[:, 8 * half:8 * half + 8, 0:CAP].bitcast(F32),
                              ALU.subtract).then_inc(xgl_ready, 1)

        def build_onehot(n):
            dve.tensor_tensor(onehot[:], cst[:, C_IOTA:C_IOTA + P].unsqueeze(1).to_broadcast([P, NT, P]),
                              slot[:, :, ds(n, 1)].to_broadcast([P, NT, P]), ALU.is_equal).then_inc(onehot_ready, 1)

        def gate_out(n):
            dve.wait_ge(gate_g_mm, n + 1)
            dve.tensor_copy(gate[:], ps[:, 2, 0:1]).then_inc(gate_ready, 1)

        dve.wait_ge(slot_ready, 1)
        build_onehot(0)
        rest(0)
        rest(1)
        for c in range(E_HI):
            split_elo(0, c)
        gathered_lo(0, 0)
        gathered_lo(0, 1)
        gate_out(0)

        def expert(n, last):
            for c in range(E_CH):
                if c and not (last and c > E_CH - E_HI):
                    split_elo(n, c + E_HI - 1)
                if c == 10:
                    dve.wait_ge(a_tanh, n + 1)
                    dve.scalar_tensor_tensor(act_s[:], act_s[:], 1.0, ps[:, 0], ALU.add,
                                             ALU.mult).then_inc(silu_ready, 1)
                if c == 11:
                    dve.wait_ge(onehot_t_mm, n + 1)
                    build_onehot(n + 1)
                if c == 15:
                    dve.wait_ge(b_t_mm, n + 1)
                    dve.wait_ge(silu_ready, n + 1)
                    dve.scalar_tensor_tensor(h_f[:], ps[:, 2], 0.5, act_s[:], ALU.mult,
                                             ALU.mult).then_inc(h_ready, 1)
                    dve.wait_ge(hh_ready, n + 1)
                    dve.tensor_tensor(hx[:, :, CAP:2 * CAP], h_f[:].rearrange("p (k n) -> p k n", k=KF),
                                      hx[:, :, 0:CAP].bitcast(F32), ALU.subtract).then_inc(hl_ready, 1)
                if c == 19:
                    gathered_lo(n + 1, 0)
                if c == 22:
                    gathered_lo(n + 1, 1)
                if c == 23:
                    for b in range(4):
                        dve.wait_ge(yh_ready, n * 4 + (b + 5))
                        dve.scalar_tensor_tensor(yl[:, b * NB:(b + 1) * NB], ps[:, 4 + b], gate[:, 0:1],
                                                 yh[:, b * NB:(b + 1) * NB].bitcast(F32), ALU.mult,
                                                 ALU.subtract).then_inc(yl_ready, 1)
                    dve.wait_ge(yl_ready, n * 4 + 8)
                    gate_out(n + 1)

        with dve.Fori(0, E - 1) as n:
            expert(n, False)
            split_elo(n + 1, E_HI - 1)
        expert(E - 1, True)
        def final_norm(t):
            dve.wait_ge(final_gain_in, 16)
            dve.wait_ge(rs3_ready, t + 1)
            for half in range(2):
                cols = slice(half * (D // 2), (half + 1) * (D // 2))
                dve.scalar_tensor_tensor(x2[:, t, cols], x2[:, t, cols], stat[:, 4 + t:5 + t], fgain[:, cols],
                                         ALU.mult, ALU.mult).then_inc(fin_ready, 1)

        dve.wait_ge(acc_ready, 16 * E + 2)
        for blk in range(16):
            t, b = blk // 4, blk % 4
            dve.wait_ge(scatter_mm, 16 * E + blk + 1)
            dst = x2[:, t, b * NB:(b + 1) * NB]
            dve.tensor_tensor(dst, dst, ps[:, 4 + b], ALU.add).then_inc(acc_ready, 1)
            if t >= 2 and b == 3:
                final_norm(t - 2)
        for t in range(NT - 2, NT):
            final_norm(t)

    @block.tensor
    def _(pe):
        def three(dst, wh, wl, mh, ml, first, last):
            pe.matmul(dst, wh, mh, start=first, stop=False)
            pe.matmul(dst, wh, ml, start=False, stop=False)
            return pe.matmul(dst, wl, mh, start=False, stop=last)

        def weights_stationary(n0, per, i, j, mh, ml, bank0, k0, k_total):
            n = n0 + j
            pe.wait_ge(lo_ready, i * per + (n + 1))
            for kk in range(2):
                k = k0 + kk
                for m in range(4):
                    cols = slice(m * P, (m + 1) * P)
                    ins = three(ps[:, bank0 + m], hi[:, n % DENSE_RING, kk, cols], lo[:, n % DENSE_RING, kk, cols],
                                mh[:, k], ml[:, k], k == 0, k == k_total - 1)
            ins.then_inc(chunk_used, 1)

        def tokens_stationary(n0, per, i, j, bank0, k0, k_total):
            n = n0 + j
            pe.wait_ge(lo_ready, i * per + (n + 1))
            for kk in range(2):
                k = k0 + kk
                for t in range(NT):
                    tok = slice(t * P, (t + 1) * P)
                    ins = three(ps[:, bank0 + t], xh[:, k, tok], xl[:, k, tok], hi[:, n % DENSE_RING, kk],
                                lo[:, n % DENSE_RING, kk], k == 0, k == k_total - 1)
            ins.then_inc(chunk_used, 1)

        pe.wait_ge(ident_in, 16)
        for t in range(NT):
            pe.wait_ge(x_scaled, t + 1)
            for k in range(8):
                ins = pe.transpose(ps[:, k, t * P:(t + 1) * P], xin[:, t, k * P:(k + 1) * P], ident)
                if t == NT - 1:
                    ins.then_inc(xt_mm, 1)
        for k in range(8, KD):
            pe.wait_ge(xl_ready, k - 7)
            for t in range(NT):
                ins = pe.transpose(ps[:, k % 8, t * P:(t + 1) * P], xin[:, t, k * P:(k + 1) * P], ident)
            ins.then_inc(xt_mm, 1)
        pe.wait_ge(xl_ready, 12)
        for i in range(A_IT):
            base = A0 + i * A_N
            for j in range(8):
                if i == 0:
                    pe.wait_ge(xl_ready, min(2 * j + 2, KD))
                weights_stationary(base, 0, 0, j, xh, xl, 0, 2 * j, KD)
                if i == 0 and j == 7:
                    pe.wait_ge(wif_lo_ready, 1)
                    for k in range(KD):
                        ins = three(ps[0:N_GATE, 7], wif_h[:, k], wif_l[:, k], xh[:, k], xl[:, k], k == 0, k == KD - 1)
                    ins.then_inc(gates_mm, 1)
                if i == 1 and j == 2:
                    pe.wait_ge(g16_ready, 1)
                    pe.wait_ge(uf_act, 2)
                    pe.wait_ge(uf_dve, 2)
                    pe.matmul(ps[0:64, 5], cst[0:N_GATE, C_SELI:C_SELI + 64], r_g16[:], start=True, stop=True)
                    pe.matmul(ps[0:64, 6], cst[0:N_GATE, C_SELF:C_SELF + 64], r_g16[:], start=True,
                              stop=True).then_inc(gsel_mm, 1)
                if i == 1 and j == 7:
                    pe.wait_ge(rows_dve, 11)
                    for r, row in enumerate((r_a, r_b)):
                        for t in range(NT):
                            at = r * 256 + t * 64
                            ins = pe.transpose(ps[:, 7, at:at + 64], row[:, t * P:(t + 1) * P], ident[0:64, 0:64])
                    ins.then_inc(rows_t, 1)
            if i == 0:
                pe.wait_ge(dft_lo_ready, 1)
            else:
                pe.wait_ge(uf_act, 2 * i)
                pe.wait_ge(uf_dve, 2 * i)
            for b in range(8):
                g, t = b // 4, b % 4
                tok = slice(t * P, (t + 1) * P)
                if t == 0:
                    pe.wait_ge(ul_ready, 4 * i + 2 * g + 2)
                if i == 1 and b == 2:
                    pe.wait_ge(ul_ready, 4 * i + 4)
                if i == 0 and b == 3:
                    pe.wait_ge(g16_ready, 1)
                if i == 1 and b == 7:
                    pe.wait_ge(cols_ready, 2)
                for k in range(2):
                    ins = three(ps[:, (4 * (1 - i) + b) % 8], uh[:, 2 * g + k, tok], ul[:, 2 * g + k, tok],
                                dft_hi[:, k], dft_lo[:, k], k == 0, k == 1)
                ins.then_inc(v_mm, 1)
            for t in range(NT):
                n = base + 8 + t
                pe.wait_ge(vl_ready, 8 * i + 5 + t)
                pe.wait_ge(lo_ready, n + 1)
                for m in range(4):
                    for cs in range(2):
                        c0 = cs * DH + (m % 2) * P
                        ins = three(ps[:, 4 * (1 - i) + m], vh[:, t, m // 2, c0:c0 + P], vl[:, t, m // 2, c0:c0 + P],
                                    hi[:, n % DENSE_RING, cs], lo[:, n % DENSE_RING, cs],
                                    t == 0 and cs == 0, t == NT - 1 and cs == 1)
                ins.then_inc(chunk_used, 1)
        def decay_rows(i, hh):
            for d in range(2):
                pe.matmul(ps[:, d], sel_pair[:, 2 * hh + d], negm_h[:], start=True, stop=False)
                pe.matmul(ps[:, d], sel_pair[:, 2 * hh + d], negm_l[:], start=False, stop=True).then_inc(decay_mm, 1)

        def scores(i, hh, ss):
            for s in ss:
                if s >= 2:
                    pe.wait_ge(prob_ready, i * 16 + (8 * hh + 2 * s - 2))
                elif hh:
                    pe.wait_ge(head_ready, i * 8 + 4)
                for c in range(2):
                    ins = pe.matmul(ps[:, 2 + s % 2], k_t[:, 2 * hh + c, s * P:(s + 1) * P],
                                    q_t[:, 2 * hh + c], start=c == 0, stop=c == 1)
                ins.then_inc(scores_mm, 1)

        def head_product(i, hh, ts):
            pe.wait_ge(prob_ready, i * 16 + (8 * hh + 8))
            for t in ts:
                if t >= 2:
                    pe.wait_ge(head_ready, i * 8 + (4 * hh + t - 1))
                b = 2 * (t % 2)
                for s in range(t + 1):
                    f0 = s * NT - s * (s - 1) // 2 + t - s
                    pe.matmul(ps[:, b, 0:DH + 1], prob[:, 0, f0], v_aug[:, s, hh], start=s == 0, stop=s == t)
                for s in range(t, NT):
                    ins = pe.matmul(ps[:, b + 1, 0:DH + 1], prob[:, 1, s * (s + 1) // 2 + t], v_aug[:, s, hh],
                                    start=s == t, stop=s == NT - 1)
                ins.then_inc(head_mm, 1)

        def head_transpose(i, hh):
            pe.wait_ge(head_normed, i * 8 + (4 * hh + 4))
            for t in range(NT):
                for c in range(2):
                    ins = pe.transpose(ps[:, c, t * P:(t + 1) * P], hcomb[:, t, c * P:(c + 1) * P], ident)
            ins.then_inc(head_t_mm, 1)

        with pe.Fori(0, C_IT) as i:
            for j in range(8):
                weights_stationary(C0, C_N, i, j, xh, xl, 4, 2 * j, KD)
            pe.wait_ge(uf_act, 2 * A_IT)
            pe.wait_ge(uf_dve, 2 * A_IT)
            for j in range(8):
                weights_stationary(C0, C_N, i, 8 + j, xh, xl, 0, 2 * j, KD)
            pe.wait_ge(kq_act, i * 4 + 2)
            pe.wait_ge(kq_dve, i * 4 + 2)
            for j in range(8):
                tokens_stationary(C0, C_N, i, 16 + j, 4, 2 * j, KD)
                if j == 1:
                    pe.wait_ge(kq_act, i * 4 + 4)
                    pe.wait_ge(kq_dve, i * 4 + 4)
                    pe.wait_ge(sel_ready, i + 1)
                    pe.wait_ge(negm_lo_ready, 1)
                    decay_rows(i, 0)
                    scores(i, 0, (0, 1))
            scores(i, 0, (2, 3))
            pe.wait_ge(ones_ready, 1)
            pe.wait_ge(v_act, i * 2 + 2)
            pe.wait_ge(v_dve, i * 2 + 2)
            for j in range(8):
                weights_stationary(C0, C_N, i, 24 + j, xh, xl, 4, 2 * j, KD)
                if j in (0, 1):
                    head_product(i, 0, (0, 1) if j == 0 else (2, 3))
                if j == 2:
                    head_transpose(i, 0)
                    scores(i, 1, (0, 1))
                if j == 3:
                    pe.wait_ge(head_t_out, i * 4 + 2)
                    decay_rows(i, 1)
                if j == 4:
                    scores(i, 1, (2, 3))
                if j in (5, 6):
                    head_product(i, 1, (0, 1) if j == 5 else (2, 3))
                if j == 7:
                    head_transpose(i, 1)
            pe.wait_ge(head_t_out, i * 4 + 4)
            pe.wait_ge(o_tanh, i * 4 + 4)
        for half, base in ((0, D0), (1, D2)):

            def gated_group(i, first):
                for j in range(8):
                    weights_stationary(base, D_N, i, j, xh, xl, 0, 2 * j, KD)
                pe.wait_ge(bl_ready, KM * (half + 1))
                if not first:
                    pe.wait_ge(merged_ready, i + D_IT * half)
                for j in range(4):
                    weights_stationary(base, D_N, i, 8 + j, bh, bl, 4, 2 * j, KM)
                pe.wait_ge(sig_tanh, i * 4 + (4 * D_IT * half + 4))

            if half == 0:
                gated_group(0, True)
            with pe.Fori(1 - half, D_IT) as i:
                gated_group(i, False)
        def transpose_x2(g):
            pe.wait_ge(x2_ready, 4 * g + 4)
            for c in range(4):
                for t in range(NT):
                    at = (4 * g + c) * P
                    ins = pe.transpose(ps[:, 4 * (g % 2) + c, t * P:(t + 1) * P], x2[:, t, at:at + P], ident)
                ins.then_inc(x2t_mm, 1)

        def logits(g):
            pe.wait_ge(x2t_act, 2 * g + 2)
            pe.wait_ge(x2t_dve, 2 * g + 2)
            if g == 0:
                pe.wait_ge(router_scaled, 1)
            for t in range(NT):
                for c in range(4):
                    k = 4 * g + c
                    ins = pe.matmul(ps[:, 4 * (g % 2), t * E:(t + 1) * E], x2t[:, k, t * P:(t + 1) * P], wif[:, k],
                                    start=c == 0, stop=c == 3)
            ins.then_inc(logit_mm, 1)

        for g in range(4):
            if g == 1:
                pe.wait_ge(merged_ready, 2 * D_IT)
            if g >= 2:
                pe.wait_ge(logit_added, g - 1)
            for j in range(8):
                if g == 0:
                    pe.wait_ge(merged_lo_ready, 2 * j + 2)
                tokens_stationary(E0, 0, 0, 8 * g + j, 4 * (g % 2), 2 * j, KD)
                if g and j == 2:
                    transpose_x2(g - 1)
                if g and j == 5:
                    logits(g - 1)
        transpose_x2(3)
        logits(3)
        pe.wait_ge(aff_ready, NT)
        for t in range(NT):
            ins = pe.transpose(ps[0:E, 5, t * P:(t + 1) * P], aff[:, t, 0:E], ident)
        ins.then_inc(aff_t_mm, 1)
        pe.wait_ge(topk_chain, 5 + 2 * (CAP // 8) + 4)
        for t in range(NT):
            ins = pe.transpose(ps[:, 6, t * E:(t + 1) * E], place[:, t * P:(t + 1) * P], ident[0:E, 0:E])
        ins.then_inc(slot_mm, 1)

        def gather(ks, done):
            for k in ks:
                dst, cols = ps[:, k // 8, (k % 8) * CAP:(k % 8 + 1) * CAP], slice(k * P, (k + 1) * P)
                for t in range(NT):
                    pe.matmul(dst, h2_parts[:, t, 0, cols], onehot_b[:, t], start=t == 0, stop=False)
                    pe.matmul(dst, h2_parts[:, t, 1, cols], onehot_b[:, t], start=False, stop=False)
                    ins = pe.matmul(dst, h2_rest[:, t, cols], onehot_b[:, t], start=False, stop=t == NT - 1)
            if done:
                ins.then_inc(gather_mm, 1)

        def gather_gate(g):
            for t in range(NT):
                ins = pe.matmul(ps[:, 2, 0:1], onehot[:, t], aff[:, t, ds(g, 1)], start=t == 0, stop=t == NT - 1)
            ins.then_inc(gate_g_mm, 1)

        def scatter(blk):
            t, b = blk // 4, blk % 4
            tok, cols = slice(t * P, (t + 1) * P), slice(b * NB, (b + 1) * NB)
            pe.matmul(ps[:, 4 + b], onehot_t[:, tok], yh[:, cols], start=True, stop=False)
            pe.matmul(ps[:, 4 + b], onehot_t[:, tok], yl[:, cols], start=False, stop=True).then_inc(scatter_mm, 1)

        pe.wait_ge(onehot_b_ready, 1)
        pe.wait_ge(rest_ready, 2)
        pe.wait_ge(rest_pool_ready, 2)
        gather(range(0, 8), True)
        gather(range(8, 16), True)
        gather_gate(0)
        with pe.Fori(0, E) as n:
            pe.wait_ge(xgl_ready, n * 2 + 2)
            for c in range(E_CH):
                if c == 8:
                    pe.wait_ge(gate_ready, n + 1)
                if c == 16:
                    pe.wait_ge(hl_ready, n + 1)
                    pe.wait_ge(scatter_out, n * 16 + 16)
                pe.wait_ge(elo_ready, n * E_CH + (c + 1))
                if c < 16:
                    for kk in range(2):
                        k = 2 * (c % 8) + kk
                        for half in range(2):
                            dst = ps[:, 2 * (c // 8) + half]
                            cols = slice(kk * FE + half * NB, kk * FE + (half + 1) * NB)
                            pe.matmul(dst, xg[:, k], ehi[:, c % E_HI, cols], start=k == 0, stop=False)
                            ins = pe.matmul(dst, xg[:, k], elo[c % RING][:, cols], start=False, stop=k == KD - 1)
                else:
                    k = c - 16
                    for b in range(4):
                        cols = slice(b * NB, (b + 1) * NB)
                        pe.matmul(ps[:, 4 + b], hx[:, k], ehi[:, c % E_HI, cols], start=k == 0, stop=False)
                        ins = pe.matmul(ps[:, 4 + b], hx[:, k], elo[c % RING][:, cols], start=False,
                                        stop=k == KF - 1)
                ins.then_inc(echunk_used, 1)
                if 1 <= c <= 7:
                    if c == 1:
                        pe.wait_ge(yl_ready, n * 4 + 4)
                        pe.wait_ge(onehot_t_ready, n + 1)
                    for blk in range(4) if c == 1 else (2 * c, 2 * c + 1):
                        if blk >= 4:
                            pe.wait_ge(scatter_out, n * 16 + (blk - 3))
                        scatter(blk)
                if c == 8:
                    for f in range(KF):
                        if f % 4 == 0:
                            pe.wait_ge(a_out, n * 2 + (f // 4 + 1))
                        ins = pe.matmul(ps[:, 0, f * CAP:(f + 1) * CAP], ab[:, f * P:(f + 1) * P], pair_sum,
                                        start=True, stop=True)
                    ins.then_inc(a_t_mm, 1)
                if c == 9:
                    for t in range(NT):
                        ins = pe.transpose(ps[:, 1, t * P:(t + 1) * P], onehot[:, t], ident)
                    ins.then_inc(onehot_t_mm, 1)
                if c == 13:
                    pe.wait_ge(onehot_b_ready, n + 2)
                    pe.wait_ge(silu_ready, n + 1)
                    gather(range(0, 2), False)
                if c == 14:
                    gather(range(2, 4), False)
                if c == 15:
                    gather(range(4, 6), False)
                    for f in range(KF):
                        if f % 4 == 0:
                            pe.wait_ge(b_out, n * 2 + (f // 4 + 1))
                        ins = pe.matmul(ps[:, 2, f * CAP:(f + 1) * CAP], ab[:, f * P:(f + 1) * P], pair_sum,
                                        start=True, stop=True)
                    ins.then_inc(b_t_mm, 1)
                    pe.wait_ge(onehot_t_ready, n + 2)
                    gather(range(6, 8), True)
                    gather(range(8, 10), False)
                if 16 <= c < 22:
                    gather(range(c - 6, c - 5), c == 21)
                if c == 22:
                    gather_gate(n + 1)
        pe.wait_ge(yl_ready, 4 * E + 4)
        pe.wait_ge(onehot_t_ready, E + 1)
        for blk in range(16):
            pe.wait_ge(acc_ready, 16 * E + 2 + max(blk - 3, 0))
            scatter(blk)


_INS = ["x", "norm1_g", "w_in", "b_if", "mh_g", "w_a", "w_b", "w_out", "norm2_g", "w_router", "w1", "w3", "w2",
        "final_g"]


def kernel(**inputs):
    import concourse.bacc as bacc
    from concourse.bass_utils import run_bass_kernel_spmd

    nc = bacc.Bacc("TRN2", target_bir_lowering=False, num_devices=1)
    arrays = {f"in_{n}": np.ascontiguousarray(inputs[n]) for n in _INS}
    arrays["in_consts"], arrays["in_dft_channel"], arrays["in_dft_token"] = shape_constants()
    views = {n: nc.dram_tensor(n, a.shape, mybir.dt.from_np(a.dtype), kind="ExternalInput").ap()
             for n, a in arrays.items()}
    out = nc.dram_tensor("out", (1, SEQ, D), F32, kind="ExternalOutput").ap()
    make(nc, views, out)
    return run_bass_kernel_spmd(nc, [arrays], core_ids=[0]).results[0]["out"]


def make(nc, v, out):
    build(nc, v["in_x"].rearrange("b s d -> (b s) d"), v["in_norm1_g"],
          v["in_w_in"].rearrange("l d n -> (l d) n"), v["in_b_if"], v["in_mh_g"],
          v["in_w_a"].rearrange("l d n -> (l d) n"), v["in_w_b"].rearrange("l d n -> (l d) n"),
          v["in_w_out"].rearrange("l d n -> (l d) n"), v["in_norm2_g"],
          v["in_w_router"].rearrange("l d n -> (l d) n"),
          v["in_w1"].rearrange("l e d n -> (l e) d n"), v["in_w3"].rearrange("l e d n -> (l e) d n"),
          v["in_w2"].rearrange("l e d n -> (l e) d n"), v["in_final_g"], v["in_consts"], v["in_dft_channel"],
          v["in_dft_token"], out.rearrange("b s d -> (b s) d"))
```
